# Optimizing a Trainium2 kernel written in Bass

```python
import math
import jax, jax.numpy as jnp
from jax import lax
import numpy as np

D_MODEL = 1024
BATCH = 1
SEQ = 512
DEPTH = 1

HEAD_DIM = 64
DSA_HEADS = 8
DIFF_HEADS = 4
DIFF_DIM = 64
IDX_HEADS = 8
IDX_DIM = 64
TOPK_MAX = 256
D_FF = 4 * D_MODEL
ROPE_THETA = 10000.0
EPS = 1e-6
Q_BLOCK = 128
NEG = -1e30

DSA_W = DSA_HEADS * HEAD_DIM
DIFF_W = DIFF_HEADS * 2 * DIFF_DIM
MIX_W = DSA_W + DIFF_W
IN_SIZES = (DSA_W, DSA_W, DSA_W,
            IDX_HEADS * IDX_DIM, IDX_DIM, IDX_HEADS,
            DIFF_W, DIFF_W, DIFF_W)
IN_COLS = int(sum(IN_SIZES))
SPLIT_POINTS = tuple(int(v) for v in np.cumsum(IN_SIZES)[:-1])


f32 = jnp.float32

def rmsnorm(x, g):
    xf = x.astype(f32)
    y = xf * lax.rsqrt(jnp.mean(xf * xf, axis=-1, keepdims=True) + EPS)
    return (y * g.astype(f32)).astype(x.dtype)

def rope_tables(seq, dim):
    inv = 1.0 / (ROPE_THETA ** (jnp.arange(0, dim, 2, dtype=f32) / dim))
    ang = jnp.arange(seq, dtype=f32)[:, None] * inv[None, :]
    return jnp.cos(ang), jnp.sin(ang)

def apply_rope(x, cos, sin):
    xf = x.astype(f32)
    x1, x2 = jnp.split(xf, 2, axis=-1)
    c = cos[None, :, None, :]
    s = sin[None, :, None, :]
    return jnp.concatenate([x1 * c - x2 * s, x2 * c + x1 * s], axis=-1).astype(x.dtype)

def dsa_attention(q, k, v, q_idx, k_idx, w_idx):
    B, S, H, Dh = q.shape
    topk = min(TOPK_MAX, S // 4)
    n_blocks = S // Q_BLOCK
    key_pos = jnp.arange(S)
    k_idx_f = k_idx.astype(f32)
    idx_scale = (IDX_HEADS ** -0.5) * (IDX_DIM ** -0.5)

    def block(i):
        start = i * Q_BLOCK
        qpos = start + jnp.arange(Q_BLOCK)
        qi = lax.dynamic_slice_in_dim(q_idx, start, Q_BLOCK, axis=1).astype(f32)
        wi = lax.dynamic_slice_in_dim(w_idx, start, Q_BLOCK, axis=1).astype(f32)
        logits = jnp.einsum('bqhd,bsd->bqhs', qi, k_idx_f)
        score = jnp.einsum('bqhs,bqh->bqs', jax.nn.relu(logits), wi) * idx_scale
        causal = key_pos[None, :] <= qpos[:, None]
        score = jnp.where(causal[None], score, -jnp.inf)
        _, sel = lax.top_k(score, topk)
        valid = sel <= qpos[None, :, None]
        k_sel = jax.vmap(lambda a, ib: a[ib])(k, sel).astype(f32)
        v_sel = jax.vmap(lambda a, ib: a[ib])(v, sel).astype(f32)
        qb = lax.dynamic_slice_in_dim(q, start, Q_BLOCK, axis=1).astype(f32)
        s = jnp.einsum('bqhd,bqkhd->bhqk', qb, k_sel) * (Dh ** -0.5)
        s = jnp.where(valid[:, None], s, NEG)
        p = jax.nn.softmax(s, axis=-1)
        o = jnp.einsum('bhqk,bqkhd->bqhd', p, v_sel)
        return o.astype(q.dtype)

    out = lax.map(block, jnp.arange(n_blocks))
    return out.transpose(1, 0, 2, 3, 4).reshape(B, S, H, Dh)

def diff_attention(q1, q2, k1, k2, v, lam):
    B, S, H, Dd = q1.shape
    n_blocks = S // Q_BLOCK
    key_pos = jnp.arange(S)
    k1f, k2f, vf = k1.astype(f32), k2.astype(f32), v.astype(f32)

    def block(i):
        start = i * Q_BLOCK
        qpos = start + jnp.arange(Q_BLOCK)
        causal = (key_pos[None, :] <= qpos[:, None])[None, None]

        def probs(qh, kf):
            qb = lax.dynamic_slice_in_dim(qh, start, Q_BLOCK, axis=1).astype(f32)
            s = jnp.einsum('bqhd,bshd->bhqs', qb, kf) * (Dd ** -0.5)
            return jax.nn.softmax(jnp.where(causal, s, NEG), axis=-1)

        p = probs(q1, k1f) - lam * probs(q2, k2f)
        o = jnp.einsum('bhqs,bshe->bqhe', p, vf)
        return o.astype(v.dtype)

    out = lax.map(block, jnp.arange(n_blocks))
    return out.transpose(1, 0, 2, 3, 4).reshape(B, S, H, 2 * Dd)

def first_inputs(seed: int = 0) -> dict:
    key = jax.random.key(seed)
    ks = jax.random.split(key, 16)
    nrm = jax.random.normal
    x = nrm(ks[0], (BATCH, SEQ, D_MODEL), f32)
    w_in = nrm(ks[1], (DEPTH, D_MODEL, IN_COLS), f32) * D_MODEL ** -0.5
    w_out = nrm(ks[2], (DEPTH, MIX_W, D_MODEL), f32) * MIX_W ** -0.5
    w_up = nrm(ks[3], (DEPTH, D_MODEL, D_FF), f32) * D_MODEL ** -0.5
    w_down = nrm(ks[4], (DEPTH, D_FF, D_MODEL), f32) * D_FF ** -0.5
    g_pre_mix = 1.0 + 0.02 * nrm(ks[5], (DEPTH, D_MODEL), f32)
    g_post_mix = 1.0 + 0.02 * nrm(ks[6], (DEPTH, D_MODEL), f32)
    g_pre_mlp = 1.0 + 0.02 * nrm(ks[7], (DEPTH, D_MODEL), f32)
    g_post_mlp = 1.0 + 0.02 * nrm(ks[8], (DEPTH, D_MODEL), f32)
    g_diff_sub = 1.0 + 0.02 * nrm(ks[9], (DEPTH, 2 * DIFF_DIM), f32)
    lambda_q1 = 0.1 * nrm(ks[10], (DEPTH, DIFF_DIM), f32)
    lambda_k1 = 0.1 * nrm(ks[11], (DEPTH, DIFF_DIM), f32)
    lambda_q2 = 0.1 * nrm(ks[12], (DEPTH, DIFF_DIM), f32)
    lambda_k2 = 0.1 * nrm(ks[13], (DEPTH, DIFF_DIM), f32)
    return {"x": x, "w_in": w_in, "w_out": w_out, "w_up": w_up, "w_down": w_down,
            "g_pre_mix": g_pre_mix, "g_post_mix": g_post_mix,
            "g_pre_mlp": g_pre_mlp, "g_post_mlp": g_post_mlp,
            "g_diff_sub": g_diff_sub,
            "lambda_q1": lambda_q1, "lambda_k1": lambda_k1,
            "lambda_q2": lambda_q2, "lambda_k2": lambda_k2}

def first_block(x, w_in, w_out, w_up, w_down, g_pre_mix, g_post_mix, g_pre_mlp,
              g_post_mlp, g_diff_sub, lambda_q1, lambda_k1, lambda_q2, lambda_k2):
    B, S, _ = x.shape
    cos, sin = rope_tables(S, HEAD_DIM)
    for layer in range(DEPTH):
        h = rmsnorm(x, g_pre_mix[layer])
        proj = jnp.einsum('bsd,dc->bsc', h, w_in[layer])
        (q_a, k_a, v_a, q_i, k_i, w_i, q_d, k_d, v_d) = jnp.split(proj, SPLIT_POINTS, axis=-1)

        q_a = apply_rope(q_a.reshape(B, S, DSA_HEADS, HEAD_DIM), cos, sin)
        k_a = apply_rope(k_a.reshape(B, S, DSA_HEADS, HEAD_DIM), cos, sin)
        v_a = v_a.reshape(B, S, DSA_HEADS, HEAD_DIM)
        q_i = apply_rope(q_i.reshape(B, S, IDX_HEADS, IDX_DIM), cos, sin)
        k_i = apply_rope(k_i.reshape(B, S, 1, IDX_DIM), cos, sin)[:, :, 0]
        o_a = dsa_attention(q_a, k_a, v_a, q_i, k_i, w_i)

        q_d = q_d.reshape(B, S, DIFF_HEADS, 2, DIFF_DIM)
        k_d = k_d.reshape(B, S, DIFF_HEADS, 2, DIFF_DIM)
        v_d = v_d.reshape(B, S, DIFF_HEADS, 2 * DIFF_DIM)
        q1 = apply_rope(q_d[:, :, :, 0], cos, sin)
        q2 = apply_rope(q_d[:, :, :, 1], cos, sin)
        k1 = apply_rope(k_d[:, :, :, 0], cos, sin)
        k2 = apply_rope(k_d[:, :, :, 1], cos, sin)
        lam_init = 0.8 - 0.6 * math.exp(-0.3 * layer)
        lam = (jnp.exp(jnp.sum(lambda_q1[layer].astype(f32) * lambda_k1[layer].astype(f32)))
               - jnp.exp(jnp.sum(lambda_q2[layer].astype(f32) * lambda_k2[layer].astype(f32)))
               + lam_init)
        o_d = diff_attention(q1, q2, k1, k2, v_d, lam)
        o_d = (rmsnorm(o_d, g_diff_sub[layer]).astype(f32) * (1.0 - lam_init)).astype(x.dtype)

        mix = jnp.concatenate([o_a.reshape(B, S, DSA_W), o_d.reshape(B, S, DIFF_W)], axis=-1)
        y = jnp.einsum('bsc,cd->bsd', mix, w_out[layer])
        x = x + rmsnorm(y, g_post_mix[layer])

        h = rmsnorm(x, g_pre_mlp[layer])
        u = jax.nn.relu(jnp.einsum('bsd,df->bsf', h, w_up[layer]))
        y = jnp.einsum('bsf,fd->bsd', u * u, w_down[layer])
        x = x + rmsnorm(y, g_post_mlp[layer])
    return x


N_HEADS_ATTN = 8
N_KV_HEADS = 2
HEAD_DIM_ATTN = 64
ATTN_GROUP = N_HEADS_ATTN // N_KV_HEADS
WINDOW = 128
ATTN_BLOCK = WINDOW
N_REL_BUCKETS = 32
REL_MAX_DISTANCE = 128
N_HEADS_MLSTM = 4
HEAD_DIM_MLSTM = 128
MLSTM_CHUNK = 64
CONV_WIDTH = 5
ATTN_Q_W = N_HEADS_ATTN * HEAD_DIM_ATTN
ATTN_KV_W = N_KV_HEADS * HEAD_DIM_ATTN
MLSTM_W = N_HEADS_MLSTM * HEAD_DIM_MLSTM
MLSTM_GATE_W = 2 * 2 * N_HEADS_MLSTM
MERGE_W = 2 * D_MODEL
IN_SPLITS = (ATTN_Q_W, ATTN_KV_W, ATTN_KV_W, MLSTM_W, MLSTM_W, MLSTM_W, MLSTM_W, MLSTM_GATE_W, MERGE_W)
D_IN_PROJ = sum(IN_SPLITS)
N_GROUPS = 4
EXPERTS_PER_GROUP = 8
N_EXPERTS = N_GROUPS * EXPERTS_PER_GROUP
TOP_K_EXPERT = 2
D_EXPERT = 512
MOE_BLOCK = 128
RMS_EPS = 1e-6
NEG_INF = -1e30


def rmsnorm_2(x, g):
    xf = x.astype(jnp.float32)
    y = xf * lax.rsqrt(jnp.mean(xf * xf, axis=-1, keepdims=True) + RMS_EPS)
    return (y * g.astype(jnp.float32)).astype(x.dtype)

def split_cols(t, sizes):
    outs, start = [], 0
    for s in sizes:
        outs.append(t[..., start:start + s])
        start += s
    return outs

def t5_bucket(rel):
    half = N_REL_BUCKETS // 2
    max_exact = half // 2
    sign = jnp.where(rel > 0, half, 0)
    n = jnp.abs(rel)
    nf = jnp.maximum(n, 1).astype(jnp.float32)
    large = max_exact + (jnp.log(nf / max_exact) / math.log(REL_MAX_DISTANCE / max_exact)
                         * (half - max_exact)).astype(jnp.int32)
    large = jnp.minimum(large, half - 1)
    return sign + jnp.where(n < max_exact, n, large)

def band_windows(t, nb):
    B = t.shape[0]
    tp = jnp.pad(t, ((0, 0), (ATTN_BLOCK, ATTN_BLOCK), (0, 0), (0, 0)))
    tp = tp.reshape(B, nb + 2, ATTN_BLOCK, t.shape[2], t.shape[3])
    return jnp.concatenate([tp[:, :-2], tp[:, 1:-1], tp[:, 2:]], axis=2)

def windowed_gqa(q, k, v, q_gain, k_gain, rel_table, sink):
    B, S = q.shape[0], q.shape[1]
    nb = S // ATTN_BLOCK
    q = q.reshape(B, S, N_HEADS_ATTN, HEAD_DIM_ATTN)
    k = k.reshape(B, S, N_KV_HEADS, HEAD_DIM_ATTN)
    v = v.reshape(B, S, N_KV_HEADS, HEAD_DIM_ATTN)
    q = rmsnorm_2(q, q_gain) * (HEAD_DIM_ATTN ** -0.5)
    k = rmsnorm_2(k, k_gain)
    qb = q.reshape(B, nb, ATTN_BLOCK, N_KV_HEADS, ATTN_GROUP, HEAD_DIM_ATTN)
    kw = band_windows(k, nb)
    vw = band_windows(v, nb)
    scores = jnp.einsum('bnqkgd,bnskd->bkgnqs', qb, kw).astype(jnp.float32)
    qi = jnp.arange(ATTN_BLOCK)
    ks = jnp.arange(3 * ATTN_BLOCK) - ATTN_BLOCK
    rel = ks[None, :] - qi[:, None]
    bias = jnp.transpose(rel_table[t5_bucket(rel)].astype(jnp.float32), (2, 0, 1))
    bias = bias.reshape(N_KV_HEADS, ATTN_GROUP, 1, ATTN_BLOCK, 3 * ATTN_BLOCK)
    kpos = jnp.arange(nb)[:, None, None] * ATTN_BLOCK + ks[None, None, :]
    valid = (jnp.abs(rel) <= WINDOW)[None] & (kpos >= 0) & (kpos < S)
    scores = jnp.where(valid, scores + bias, NEG_INF)
    sink_col = jnp.broadcast_to(sink.astype(jnp.float32).reshape(N_KV_HEADS, ATTN_GROUP, 1, 1, 1),
                                scores.shape[:-1] + (1,))
    probs = jax.nn.softmax(jnp.concatenate([scores, sink_col], axis=-1), axis=-1)[..., :-1]
    out = jnp.einsum('bkgnqs,bnskd->bnqkgd', probs.astype(v.dtype), vw)
    return out.reshape(B, S, ATTN_Q_W)

def mlstm_scan(q, k, v, ig, lf):
    B, H, S, d = q.shape
    L = MLSTM_CHUNK
    nc = S // L

    def chunks(t):
        return jnp.moveaxis(t.reshape((B, H, nc, L) + t.shape[3:]), 2, 0)

    tril = jnp.tril(jnp.ones((L, L), dtype=bool))

    def step(carry, inp):
        C, n, m = carry
        qc, kc, vc, igc, lfc = inp
        b = jnp.cumsum(lfc, axis=-1)
        dlog = jnp.where(tril, b[..., :, None] - b[..., None, :] + igc[..., None, :], -jnp.inf)
        g_inter = b + m[..., None]
        m_row = jnp.maximum(g_inter, jnp.max(dlog, axis=-1))
        w = jnp.exp(dlog - m_row[..., None])
        s = jnp.einsum('bhtd,bhsd->bhts', qc, kc) * w
        inter = jnp.exp(g_inter - m_row)
        num = jnp.einsum('bhts,bhsd->bhtd', s, vc) + inter[..., None] * jnp.einsum('bhtd,bhde->bhte', qc, C)
        den = jnp.sum(s, axis=-1) + inter * jnp.einsum('bhtd,bhd->bht', qc, n)
        h = num / jnp.maximum(jnp.abs(den), jnp.exp(-m_row))[..., None]
        b_last = b[..., -1]
        wlog = b_last[..., None] - b + igc
        m_new = jnp.maximum(b_last + m, jnp.max(wlog, axis=-1))
        decay = jnp.exp(b_last + m - m_new)
        ws = jnp.exp(wlog - m_new[..., None])
        C_new = decay[..., None, None] * C + jnp.einsum('bhs,bhsd,bhse->bhde', ws, kc, vc)
        n_new = decay[..., None] * n + jnp.einsum('bhs,bhsd->bhd', ws, kc)
        return (C_new, n_new, m_new), h

    init = (jnp.zeros((B, H, d, d), jnp.float32), jnp.zeros((B, H, d), jnp.float32),
            jnp.zeros((B, H), jnp.float32))
    _, h = lax.scan(step, init, (chunks(q), chunks(k), chunks(v), chunks(ig), chunks(lf)))
    return jnp.moveaxis(h, 0, 2).reshape(B, H, S, d)

def mlstm_branch(qm, km, vm, om, gates, conv_w, conv_b, gate_b, out_gain):
    B, S = qm.shape[0], qm.shape[1]
    qk = jnp.concatenate([qm, km], axis=-1)
    qk = lax.conv_general_dilated(qk, conv_w[:, None, :].astype(qk.dtype), (1,),
                                  [(CONV_WIDTH // 2, CONV_WIDTH // 2)],
                                  dimension_numbers=('NWC', 'WIO', 'NWC'),
                                  feature_group_count=qk.shape[-1]) + conv_b
    qk = jax.nn.silu(qk)
    qm, km = qk[..., :MLSTM_W], qk[..., MLSTM_W:]

    def heads(t):
        return t.reshape(B, S, N_HEADS_MLSTM, HEAD_DIM_MLSTM).transpose(0, 2, 1, 3).astype(jnp.float32)

    q = heads(qm)
    k = heads(km) * (HEAD_DIM_MLSTM ** -0.5)
    v = heads(vm)
    g = gates.astype(jnp.float32).reshape(B, S, 2, 2, N_HEADS_MLSTM) + gate_b.astype(jnp.float32)
    g = jnp.transpose(g, (2, 3, 0, 4, 1))
    h_f = mlstm_scan(q, k, v, g[0, 0], jax.nn.log_sigmoid(g[0, 1]))

    def flip(t):
        return jnp.flip(t, axis=2)

    h_b = flip(mlstm_scan(flip(q), flip(k), flip(v), flip(g[1, 0]), flip(jax.nn.log_sigmoid(g[1, 1]))))
    h = (h_f + h_b).transpose(0, 2, 1, 3)
    h = rmsnorm_2(h, out_gain)
    return h.reshape(B, S, MLSTM_W).astype(om.dtype) * jax.nn.sigmoid(om)

def hier_moe(h, w_rg, b_rg, w_re, b_re, w_gate, w_up, w_down):
    B, S, D = h.shape
    T = B * S
    xt = h.reshape(T, D)
    xf = xt.astype(jnp.float32)
    g_logits = xf @ w_rg.astype(jnp.float32) + b_rg.astype(jnp.float32)
    g_idx = jnp.argmax(g_logits, axis=-1).astype(jnp.int32)
    p_group = jnp.take_along_axis(jax.nn.softmax(g_logits, axis=-1), g_idx[:, None], axis=1)[:, 0]
    e_logits = (xf @ w_re.astype(jnp.float32) + b_re.astype(jnp.float32)).reshape(T, N_GROUPS, EXPERTS_PER_GROUP)
    e_in = jnp.take_along_axis(e_logits, g_idx[:, None, None], axis=1)[:, 0]
    top_v, top_i = lax.top_k(e_in, TOP_K_EXPERT)
    top_w = jax.nn.softmax(top_v, axis=-1) * p_group[:, None]
    expert_ids = (g_idx[:, None] * EXPERTS_PER_GROUP + top_i).reshape(-1).astype(jnp.int32)
    weights = top_w.reshape(-1)
    token_ids = jnp.repeat(jnp.arange(T, dtype=jnp.int32), TOP_K_EXPERT)
    A = T * TOP_K_EXPERT
    order = jnp.argsort(expert_ids)
    se, stok, sw = expert_ids[order], token_ids[order], weights[order]
    counts = jnp.bincount(expert_ids, length=N_EXPERTS)
    starts = jnp.cumsum(counts) - counts
    pcounts = ((counts + MOE_BLOCK - 1) // MOE_BLOCK) * MOE_BLOCK
    pends = jnp.cumsum(pcounts)
    pstarts = pends - pcounts
    dest = pstarts[se] + (jnp.arange(A, dtype=jnp.int32) - starts[se])
    P = A + N_EXPERTS * MOE_BLOCK
    nblk = P // MOE_BLOCK
    row_tok = jnp.zeros((P,), jnp.int32).at[dest].set(stok)
    row_w = jnp.zeros((P,), jnp.float32).at[dest].set(sw)
    blk_e = jnp.minimum(jnp.searchsorted(pends, jnp.arange(nblk) * MOE_BLOCK, side='right'),
                        N_EXPERTS - 1).astype(jnp.int32)
    xs = xt[row_tok].reshape(nblk, MOE_BLOCK, D)

    def expert_block(args):
        xb, e = args
        return (jax.nn.silu(xb @ w_gate[e]) * (xb @ w_up[e])) @ w_down[e]

    ys = lax.map(expert_block, (xs, blk_e)).reshape(P, D)
    y = jnp.zeros((T, D), ys.dtype).at[row_tok].add(ys * row_w[:, None].astype(ys.dtype))
    return y.reshape(B, S, D).astype(h.dtype)

def second_inputs(seed: int = 0) -> dict:
    key = jax.random.key(seed)
    ks = jax.random.split(key, 24)

    def nrm(k, shape, scale):
        return jax.random.normal(k, shape, jnp.float32) * scale

    ib = nrm(ks[9], (DEPTH, 2, 1, N_HEADS_MLSTM), 0.1)
    fb = jnp.linspace(3.0, 6.0, N_HEADS_MLSTM, dtype=jnp.float32)[None, None, None, :] + nrm(ks[10], (DEPTH, 2, 1, N_HEADS_MLSTM), 0.01)
    return {
        'x': nrm(ks[0], (BATCH, SEQ, D_MODEL), 1.0),
        'norm1_g': 1.0 + nrm(ks[1], (DEPTH, D_MODEL), 0.01),
        'w_in': nrm(ks[2], (DEPTH, D_MODEL, D_IN_PROJ), D_MODEL ** -0.5),
        'attn_q_gain': 1.0 + nrm(ks[3], (DEPTH, HEAD_DIM_ATTN), 0.01),
        'attn_k_gain': 1.0 + nrm(ks[4], (DEPTH, HEAD_DIM_ATTN), 0.01),
        'attn_sink': nrm(ks[5], (DEPTH, N_HEADS_ATTN), 0.5),
        'rel_bias_table': nrm(ks[6], (N_REL_BUCKETS, N_HEADS_ATTN), 0.5),
        'mlstm_conv_w': nrm(ks[7], (DEPTH, CONV_WIDTH, 2 * MLSTM_W), CONV_WIDTH ** -0.5),
        'mlstm_conv_b': nrm(ks[8], (DEPTH, 2 * MLSTM_W), 0.01),
        'mlstm_gate_b': jnp.concatenate([ib, fb], axis=2),
        'mlstm_out_gain': 1.0 + nrm(ks[11], (DEPTH, N_HEADS_MLSTM, HEAD_DIM_MLSTM), 0.01),
        'w_branch_attn': nrm(ks[12], (DEPTH, ATTN_Q_W, D_MODEL), ATTN_Q_W ** -0.5),
        'w_branch_mlstm': nrm(ks[13], (DEPTH, MLSTM_W, D_MODEL), MLSTM_W ** -0.5),
        'merge_b': nrm(ks[14], (DEPTH, MERGE_W), 0.01),
        'w_out': nrm(ks[15], (DEPTH, D_MODEL, D_MODEL), D_MODEL ** -0.5),
        'norm2_g': 1.0 + nrm(ks[16], (DEPTH, D_MODEL), 0.01),
        'w_router_group': nrm(ks[17], (DEPTH, D_MODEL, N_GROUPS), D_MODEL ** -0.5),
        'b_router_group': nrm(ks[18], (DEPTH, N_GROUPS), 0.01),
        'w_router_expert': nrm(ks[19], (DEPTH, D_MODEL, N_EXPERTS), D_MODEL ** -0.5),
        'b_router_expert': nrm(ks[20], (DEPTH, N_EXPERTS), 0.01),
        'w_expert_gate': nrm(ks[21], (DEPTH, N_EXPERTS, D_MODEL, D_EXPERT), D_MODEL ** -0.5),
        'w_expert_up': nrm(ks[22], (DEPTH, N_EXPERTS, D_MODEL, D_EXPERT), D_MODEL ** -0.5),
        'w_expert_down': nrm(ks[23], (DEPTH, N_EXPERTS, D_EXPERT, D_MODEL), D_EXPERT ** -0.5),
    }

def second_block(x, norm1_g, w_in, attn_q_gain, attn_k_gain, attn_sink, rel_bias_table,
              mlstm_conv_w, mlstm_conv_b, mlstm_gate_b, mlstm_out_gain,
              w_branch_attn, w_branch_mlstm, merge_b, w_out, norm2_g,
              w_router_group, b_router_group, w_router_expert, b_router_expert,
              w_expert_gate, w_expert_up, w_expert_down):
    for l in range(DEPTH):
        h = rmsnorm_2(x, norm1_g[l])
        proj = h @ w_in[l]
        qa, ka, va, qm, km, vm, om, gm, mg = split_cols(proj, IN_SPLITS)
        ya = windowed_gqa(qa, ka, va, attn_q_gain[l], attn_k_gain[l], rel_bias_table, attn_sink[l])
        ym = mlstm_branch(qm, km, vm, om, gm, mlstm_conv_w[l], mlstm_conv_b[l],
                          mlstm_gate_b[l], mlstm_out_gain[l])
        gates = jax.nn.sigmoid(mg + merge_b[l])
        u = gates[..., :D_MODEL] * (ya @ w_branch_attn[l]) + gates[..., D_MODEL:] * (ym @ w_branch_mlstm[l])
        x = x + u @ w_out[l]
        x = x + hier_moe(rmsnorm_2(x, norm2_g[l]), w_router_group[l], b_router_group[l],
                         w_router_expert[l], b_router_expert[l],
                         w_expert_gate[l], w_expert_up[l], w_expert_down[l])
    return x


def setup_inputs(seed=0):
    out = dict(first_inputs(seed))
    for name, value in second_inputs(seed + 1).items():
        if name != "x":
            out[name + "_2"] = value
    return out


def reference(
    x, w_in, w_out, w_up, w_down, g_pre_mix, g_post_mix, g_pre_mlp, g_post_mlp, g_diff_sub,
    lambda_q1, lambda_k1, lambda_q2, lambda_k2, norm1_g_2, w_in_2, attn_q_gain_2, attn_k_gain_2,
    attn_sink_2, rel_bias_table_2, mlstm_conv_w_2, mlstm_conv_b_2, mlstm_gate_b_2,
    mlstm_out_gain_2, w_branch_attn_2, w_branch_mlstm_2, merge_b_2, w_out_2, norm2_g_2,
    w_router_group_2, b_router_group_2, w_router_expert_2, b_router_expert_2, w_expert_gate_2,
    w_expert_up_2, w_expert_down_2,
):
    x = first_block(
        x, w_in, w_out, w_up, w_down, g_pre_mix, g_post_mix, g_pre_mlp, g_post_mlp, g_diff_sub,
        lambda_q1, lambda_k1, lambda_q2, lambda_k2,
    )
    return second_block(
        x, norm1_g_2, w_in_2, attn_q_gain_2, attn_k_gain_2, attn_sink_2, rel_bias_table_2,
        mlstm_conv_w_2, mlstm_conv_b_2, mlstm_gate_b_2, mlstm_out_gain_2, w_branch_attn_2,
        w_branch_mlstm_2, merge_b_2, w_out_2, norm2_g_2, w_router_group_2, b_router_group_2,
        w_router_expert_2, b_router_expert_2, w_expert_gate_2, w_expert_up_2, w_expert_down_2,
    )


_drawn_inputs = setup_inputs


def setup_inputs(seed=0):
    import zlib

    import numpy as np

    out = dict(_drawn_inputs(seed))
    spreads = {}
    factors = {'g_post_mix': 2.721,
     'g_pre_mlp': 2.857,
     'g_post_mlp': 2.903,
     'lambda_q1': 8.0,
     'norm1_g_2': 8.0,
     'attn_q_gain_2': 8.0,
     'attn_k_gain_2': 8.0,
     'attn_sink_2': 8.0,
     'rel_bias_table_2': 2.926,
     'mlstm_conv_b_2': 64.0,
     'mlstm_out_gain_2': 8.0,
     'merge_b_2': 8.0,
     'norm2_g_2': 4.714,
     'b_router_group_2': 5.27,
     'b_router_expert_2': 7.163}
    for name, (base, spread) in spreads.items():
        noise = np.random.default_rng([zlib.crc32(name.encode()), seed]).standard_normal(out[name].shape)
        drawn = base * np.exp(spread * noise) if base else spread * noise
        out[name] = __import__('jax').numpy.asarray(drawn.astype(out[name].dtype))
    for name, factor in factors.items():
        out[name] = (out[name] * factor).astype(out[name].dtype)
    return out
```

```python
import math
from contextlib import ExitStack

import numpy as np

import concourse.bass as bass
from concourse import mybir

F32 = mybir.dt.float32
I32 = mybir.dt.int32
ALU = mybir.AluOpType
ACT = mybir.ActivationFunctionType
AX = mybir.AxisListType

P = 128
D = 1024
SEQ = 512
NT = SEQ // P
KT = D // P
HD = 64
D_FF = 4 * D
FT = D_FF // P
EPS = 1e-6
NEG = -1e30
LOWEST = -3.0e38
TAKEN = -3.4e38
TOPK = 128
IDX_SCALE = (8 ** -0.5) * (64 ** -0.5)
LAM_INIT = 0.8 - 0.6 * math.exp(-0.3 * 0)
CONV = 5
DM = 128
MROWS = 36
NE, NG, EPG = 32, 4, 8
DE = 512
BLK = 96
NBLK = -(-SEQ // BLK)
N_SMALL = 27
MAXJOBS = 2 * SEQ // BLK
BLOCKS = NE + MAXJOBS
ROWS = BLOCKS * BLK

QA, KA, VA, QI, KI, WI, QD, KD, VD = 0, 512, 1024, 1536, 2048, 2112, 2120, 2632, 3144
QA2, KVA2, QM, KM, VM, OM, GM, MG = 0, 512, 768, 1280, 1792, 2304, 2816, 2832


def build(nc, io, out):
    ctx = ExitStack()
    with ctx:
        def sb(name, shape, dt=F32):
            return ctx.enter_context(nc.sbuf_tensor(name, shape, dt))

        def sem(name):
            return ctx.enter_context(nc.semaphore(name))

        ps = ctx.enter_context(nc.psum_tensor("ps", [P, 8, 512], F32))
        W = sb("W", [P, 6 * 4096])
        ring = [W[:, s * 4096:(s + 1) * 4096] for s in range(2)]
        R = W[:, 2 * 4096:]
        expert_w = [[W[:, (3 * s + j) * 4096:(3 * s + j + 1) * 4096] for j in range(3)] for s in (1, 0)]
        x = sb("x", [P, NT, D])
        hT = sb("hT", [P, KT, SEQ])
        mix = sb("mix", [P, NT, D])
        yT = sb("yT", [P, KT, SEQ])
        cbuf = sb("cbuf", [P, 8 * 516])
        stage = sb("stage", [P, 2, D])
        smb = sb("smb", [P, 4, 512])
        ptb = sb("ptb", [P, 2, 512])
        gb = sb("gb", [P, D])
        ident = sb("ident", [P, P])
        cmask = sb("cmask", [P, 512])
        fmask = sb("fmask", [P, P])
        rope = yT[:, 0:2, :]
        ones = sb("ones", [P, P])
        gcol = sb("gcol", [P, 6, 8])
        small = sb("small", [P, 640])
        cur = [0]

        def col(n):
            a = cur[0]
            cur[0] += n
            assert cur[0] <= 640
            return small[:, a:a + n]

        ss, std, rstd = col(16), col(16), col(16)
        ssy, stdy, rsty = col(8), col(8), col(8)
        mx, nm, den, es = col(96), col(96), col(96), col(32)
        hss, hstd, hrs = col(32), col(32), col(32)
        lamv = col(8)
        epsc = col(1)
        m8 = col(8)
        wi = sb("wi", [P, NT, 8])
        lam_in = cbuf[:, 0:4 * HD].rearrange("p (n d) -> p n d", n=4)

        qiT = R[:, 0:2048].rearrange("p (c t) -> p c t", c=4)
        kiT = R[:, 2048:2560]
        qdT = R[:, 2560:4608].rearrange("p (c t) -> p c t", c=4)
        kdT = R[:, 4608:6656].rearrange("p (c t) -> p c t", c=4)
        qaT = R[:, 6656:8704].rearrange("p (c t) -> p c t", c=4)
        kaT = R[:, 8704:10752].rearrange("p (c t) -> p c t", c=4)
        vd = R[:, 10752:12800].rearrange("p (i c) -> p i c", i=NT)
        va = R[:, 12800:14848].rearrange("p (i c) -> p i c", i=NT)
        uT = R[:, 0:FT * 512].rearrange("p (f t) -> p f t", f=FT)
        idx_s = cbuf[:, 0:1536].rearrange("p (i t) -> p i t", i=3)
        dmask = cbuf[:, 1536:3072].rearrange("p (i t) -> p i t", i=3)
        rbuf = cbuf[:, 3072:4096].rearrange("p (s t) -> p s t", s=2)
        qkT = R[:, 0:4096].rearrange("p (c t) -> p c t", c=8)
        vext = R[:, 4096:6160].rearrange("p (i h e) -> p i h e", i=NT, h=4)
        sigT = R[:, 6160:8208].rearrange("p (c t) -> p c t", c=4)
        bias = R[:, 8208:11280].rearrange("p (h t) -> p h t", h=8)
        qT = R[:, 11280:13328].rearrange("p (c t) -> p c t", c=4)
        kdup = R[:, 13328:14352].rearrange("p (g t) -> p g t", g=2)
        va2 = R[:, 14352:14864].rearrange("p (i c) -> p i c", i=NT)
        E = R[:, 8208:12304].rearrange("p (s j t) -> p s j t", s=2, j=NT)
        nmd = R[:, 12304:13328].rearrange("p (s j t) -> p s j t", s=2, j=NT)
        convin = cbuf[:, :].rearrange("p (c t) -> p c t", c=8)
        merged = cbuf[:, 0:4096].rearrange("p (c t) -> p c t", c=8)
        gates = R[:, 0:4096].rearrange("p (b c t) -> p b c t", b=2, c=4)
        gw = [gb[:, a:b] for a, b in ((0, 64), (64, 352), (352, 448), (448, 736))]
        G = gw[0].rearrange("p (i c) -> p i c", i=NT)
        GL = gw[1].rearrange("p (q i r) -> p q i r", q=2, i=NT)
        lfw = gw[2].rearrange("p (q i c) -> p q i c", q=3, i=NT)
        rows = yT[0:MROWS, 0:4, :]
        one_row = yT[0:MROWS, 4, :]
        zero_row = yT[0:MROWS, 5, :]
        selr = yT[0:MROWS, 6:8, :].rearrange("p a (r m) -> p (a r) m", m=P)
        onehot = smb[0:NE, 0, :]
        wmask = smb[0:8, 1, :]
        bline = smb[0:8, 2, :]
        colsb = gw[3].rearrange("p (q i r) -> p q i r", q=2, i=NT)
        mden = sb("mden", [P, 4, 4])
        convw = sb("convw", [P, 8, CONV])
        convb = sb("convb", [P, 8])
        gateb = sb("gateb", [P, 16])
        sink = sb("sink", [P, 8])
        gqk = sb("gqk", [P, 2])
        mergeb = sb("mergeb", [P, 16])
        btab = sb("btab", [NE, 8])
        yTw = yT[:, :, :].rearrange("p a b -> p (a b)")
        late = 32 * BLK
        wr = yTw[:, late:late + KT * (NG + NE)].rearrange("p (k e) -> p k e", k=KT)
        late += KT * (NG + NE)
        ltri = yTw[:, late:late + P]
        allone = yTw[:, late + P:late + 2 * P]
        br = sb("br", [P, NG + NE])
        lg = cbuf[:, 0:NT * (NG + NE)].rearrange("p (i c) -> p i c", i=NT)
        msel = cbuf[:, 256:256 + 3 * NT * NE].rearrange("p (q i e) -> p q i e", q=3, i=NT)
        wpos = sb("wpos", [P, 2, NT])
        ipos = sb("ipos", [P, 2, NT], I32)
        tokid = sb("tokid", [P, NT])
        iot = sb("iot", [P, 64])
        idsT = cbuf[0:BLK, 1024:1024 + BLOCKS].bitcast(I32)
        idcol = sb("idcol", [BLK, 3], I32)
        jobs = sb("jobs", [1, MAXJOBS], I32)
        njobs = sb("njobs", [1, 1], I32)
        iti = sb("iti", [P, 64], I32)
        vzero = mix[0:BLOCKS, 0, 0:BLK]
        rtw = ptb[:, :, :].rearrange("p a b -> p (a b)")
        rcur = [0]

        def work(*shape):
            n = int(np.prod(shape))
            a = rcur[0]
            rcur[0] += n
            assert rcur[0] <= 1024
            v = rtw[:, a:a + n]
            names = "abc"[:len(shape)]
            if len(shape) == 1:
                return v
            return v.rearrange(f"p ({' '.join(names)}) -> p {' '.join(names)}", **dict(zip(names, shape)))

        r_place = work(8)
        r_gm, r_low, r_v1, r_v2, r_dv, r_x2 = (work(NT) for _ in range(6))
        r_gd, r_ge, r_eq4, r_hg = (work(NT, NG) for _ in range(4))
        r_e, r_e2, r_eq8, r_h1, r_h2 = (work(NT, EPG) for _ in range(5))
        r_sel = work(NT, EPG, NG)
        r_off, r_rank, r_row = work(NE), work(NT, NE), work(NT, NE)
        r_ov, r_t, r_cum = work(NE), work(NE), work(NE)
        jw = smb[0:1, 3, :]
        j_ex = jw[:, 0:MAXJOBS]
        j_le = smb[0:1, 2, 0:MAXJOBS * NE].rearrange("p (j e) -> p j e", e=NE)
        xs = mix[:, 0:2, :]
        ys = mix[:, 2:4, :]
        xsT = yTw[:, 0:16 * BLK].rearrange("p (s k t) -> p s k t", s=2, k=KT)
        hTe = yTw[:, 16 * BLK:24 * BLK].rearrange("p (s k t) -> p s k t", s=2, k=4)
        sg = yTw[:, 24 * BLK:32 * BLK].rearrange("p (s k t) -> p s k t", s=2, k=4)
        yg = hT[:, :, :].rearrange("p (a c) t -> p a (c t)", a=4)

        h_dram = nc.dram_tensor("h_scratch", (SEQ, D), F32, kind="Internal").ap()
        y_dram = nc.dram_tensor("y_scratch", (ROWS, D), F32, kind="Internal").ap()
        id_dram = nc.dram_tensor("id_scratch", (ROWS, 1), F32, kind="Internal").ap()
        l_dram = nc.dram_tensor("bias_scratch", (8, P, 512), F32, kind="Internal").ap()

        w1, w2 = io["w_in"][0], io["w_in_2"][0]

        def cols_of(w, a, n):
            return w[:, a:a + n].rearrange("(k p) c -> p k c", p=P)

        chunks = [cols_of(w1, a, n) for a, n in
                  ((QI, 512), (KI, 72), (QD, 512), (KD, 512), (VD, 512), (QA, 512), (KA, 512), (VA, 512))]
        C_WO = len(chunks)
        chunks += [cols_of(io["w_out"][0], 512 * h, 512) for h in range(2)]
        C_UP = len(chunks)
        C_DOWN = C_UP + 8
        C_P2 = C_DOWN + 8
        chunks2 = [cols_of(w2, a, n) for a, n in
                   ((GM, 16), (QM, 512), (KM, 512), (VM, 512), (QA2, 512), (KVA2, 256), (OM, 512))]
        C_MERGE = C_P2 + len(chunks2)
        C_WO2 = C_MERGE + 6
        C_END = C_WO2 + 2

        def ring_view(c, k, n):
            return ring[c % 2][:, 0:k * n].rearrange("p (k n) -> p k n", k=k)

        const_ready = sem("const_ready")
        zero_ready = sem("zero_ready")
        x_load = [sem(f"x_load{i}") for i in range(NT)]
        small_load = sem("small_load")
        gb_load = sem("gb_load")
        ring_load = [sem(f"ring_load{s}") for s in range(2)]
        branch_load = sem("branch_load")
        down_used = sem("down_used")
        dv = sem("dv")
        ac = sem("ac")
        sumsq_done, std_done = sem("sumsq_done"), sem("std_done")
        turn_src, turn_done, turn_evac = sem("turn_src"), sem("turn_done"), sem("turn_evac")
        proj_done = sem("proj_done")
        swap_done, rope_done = sem("swap_done"), sem("rope_done")
        val_done, wi_done, ki_dup = sem("val_done"), sem("wi_done"), sem("ki_dup")
        idx_done, relu_done, comb_done = sem("idx_done"), sem("relu_done"), sem("comb_done")
        lam_dot, lam_exp = sem("lam_dot"), sem("lam_exp")
        score_done, masked, negmax = sem("score_done"), sem("masked"), sem("negmax")
        exp_done, diff_done = sem("exp_done"), sem("diff_done")
        probT_done, pt_ready, pv_done = sem("probT_done"), sem("pt_ready"), sem("pv_done")
        o_sq, o_ss, o_std, o_evac = sem("o_sq"), sem("o_ss"), sem("o_std"), sem("o_evac")
        y_done, x_ready = sem("y_done"), sem("x_ready")
        ysumsq, ystd = sem("ysumsq"), sem("ystd")
        up_done, up_relu, up_free = sem("up_done"), sem("up_relu"), sem("up_free")
        gates_raw, gate_abs, gate_rows = sem("gates_raw"), sem("gate_abs"), sem("gate_rows")
        conv_in, conv_done, qk_ready = sem("conv_in"), sem("conv_done"), sem("qk_ready")
        vone_done = sem("vone_done")
        vext_done, va2_done, sig_done = sem("vext_done"), sem("va2_done"), sem("sig_done")
        sq_done, ssb_done, hstd_done, qkn_done, kdup_done = (
            sem("sq_done"), sem("ssb_done"), sem("hstd_done"), sem("qkn_done"), sem("kdup_done"))
        btab_done, bline_ready, bline_store, bias_load = (
            sem("btab_done"), sem("bline_ready"), sem("bline_store"), sem("bias_load"))
        onehot_load = sem("onehot_load")
        grow_done, grow_evac, scan_done, gcol_done, acol_ready, em_ready = (
            sem("grow_done"), sem("grow_evac"), sem("scan_done"), sem("gcol_done"), sem("acol_ready"),
            sem("em_ready"))
        mb_done, nmd_done, wexp_done, qk_done, sw_done, num_done, hsum_done = (
            sem("mb_done"), sem("nmd_done"), sem("wexp_done"), sem("qk_done"), sem("sw_done"),
            sem("num_done"), sem("hsum_done"))
        msq_done, mss_done, mstd_done, mnorm_done = sem("msq_done"), sem("mss_done"), sem("mstd_done"), sem("mnorm_done")
        gate_sig, u_done = sem("gate_sig"), sem("u_done")
        logits_done, lg_ready, r_exp, r_exp_done = (
            sem("logits_done"), sem("lg_ready"), sem("r_exp"), sem("r_exp_done"))
        h_store = [sem(f"h_store{s}") for s in range(2)]
        sel_ready, rank_done, pos_ready, id_zero, id_scatter, y_zero = (
            sem("sel_ready"), sem("rank_done"), sem("pos_ready"), sem("id_zero"), sem("id_scatter"), sem("y_zero"))
        wr_load = sem("wr_load")
        fetches = sem("fetches")
        id_load, idT_done, ids_ready, job_ready = (
            sem("id_load"), sem("idT_done"), sem("ids_ready"), sem("job_ready"))
        wg_load = [sem(f"wg_load{s}") for s in range(2)]
        wu_load = [sem(f"wu_load{s}") for s in range(2)]
        wd_load = [sem(f"wd_load{s}") for s in range(2)]
        gather = [sem(f"gather{s}") for s in range(2)]
        y_store = [sem(f"y_store{s}") for s in range(2)]
        idcol_ready, xt_done, xT_ready, gu_done, silu_done, hte_ready, down_done, ys_ready = (
            sem("idcol_ready"), sem("xt_done"), sem("xT_ready"), sem("gu_done"), sem("silu_done"),
            sem("hte_ready"), sem("down_done"), sem("ys_ready"))
        ov = {n: sem(f"over_{n}") for n in
              ("wg", "wu", "wd", "id", "gather", "xt", "xT", "gu", "silu", "hte", "down", "ys", "store", "free")}
        y_gather = [sem(f"y_gather{s}") for s in range(4)]
        add_done, out_store = sem("add_done"), sem("out_store")

        G1 = [("rope", 0, c, qiT[:, c, :]) for c in range(4)]
        G1 += [("ki", 1, 0, kiT), ("wi", 1, 0, None)]
        N_IDX_FROM = len(G1)
        for chunk, dst in ((2, qdT), (3, kdT)):
            G1 += [("rope", chunk, c, dst[:, c, :]) for c in range(4)]
        G1 += [("val", 4, i, vd[:, i, :]) for i in range(NT)]
        for chunk, dst in ((5, qaT), (6, kaT)):
            G1 += [("rope", chunk, c, dst[:, c, :]) for c in range(4)]
        G1 += [("val", 7, i, va[:, i, :]) for i in range(NT)]
        b = C_P2
        G2 = [("gates", b, 0)]
        G2 += [("conv", b + 1, c) for c in range(4)] + [("conv", b + 2, c) for c in range(4)]
        G2 += [("vm", b + 3, i) for i in range(NT)]
        G2 += [("qnorm", b + 4, c) for c in range(4)] + [("knorm", b + 5, 0), ("va2", b + 5, 0)]
        G2 += [("om", b + 6, c) for c in range(4)]
        IDX = [(i, h) for i in range(1, NT) for h in range(8)]

        units = []
        for i in range(NT):
            w = (i + 1) * P
            cm = cmask[:, 512 - w:512]
            for h in range(4):
                maps = [(qdT[64 * c:64 * c + 64, h, i * P:(i + 1) * P], kdT[64 * c:64 * c + 64, h, 0:w], cm)
                        for c in range(2)]
                units.append(dict(maps=maps, w=w, k0=0, v=vd, vc=(h * P, (h + 1) * P), oc=(h * P, (h + 1) * P),
                                  kind="diff", tile=i, h=h, last=h == 3, scale=HD ** -0.5))
            for h in range(8):
                r = 64 * (h % 2)
                m = cm if i == 0 else dmask[:, i - 1, 0:w]
                units.append(dict(maps=[(qaT[r:r + 64, h // 2, i * P:(i + 1) * P], kaT[r:r + 64, h // 2, 0:w], m)],
                                  w=w, k0=0, v=va, vc=(h * HD, (h + 1) * HD), oc=(h * HD, (h + 1) * HD),
                                  kind="topk", tile=i, h=h, last=h == 7, scale=HD ** -0.5))
        N_UNITS1 = len(units)
        for n in range(NT):
            lo, hi = max(0, n - 1), min(NT, n + 2)
            for h in range(8):
                r, off = 64 * (h % 2), (lo - n + 1) * P
                w = (hi - lo) * P
                kv = h // 4
                units.append(dict(maps=[(qT[r:r + 64, h // 2, n * P:(n + 1) * P], kdup[r:r + 64, kv, lo * P:hi * P],
                                         bias[:, h, off:off + w])],
                                  w=w, k0=lo, v=va2, vc=(kv * HD, (kv + 1) * HD), oc=(h * HD, (h + 1) * HD),
                                  kind="window", tile=n, h=h, last=h == 7, scale=1.0))
        m = d = g = 0
        map_unit = []
        for u, un in enumerate(units):
            un["u"], un["m"], un["g"] = u, m, g
            m += len(un["maps"])
            map_unit += [u] * len(un["maps"])
            d += un["kind"] == "diff"
            un["d"] = d
            g += un["last"]
        ALL1 = range(0, N_UNITS1)
        ALL2 = range(N_UNITS1, len(units))
        M1 = units[N_UNITS1]["m"]
        MAPS = m
        groups = [un for un in units if un["last"]]

        chunk_done = {}
        for g, it_ in enumerate(G1 + G2):
            chunk_done[it_[1]] = (proj_done, g + 1)
        for half in range(2):
            chunk_done[C_WO + half] = (y_done, 4 * (half + 1))
            for q in range(4):
                chunk_done[C_DOWN + 4 * half + q] = ((down_used, 3 * half + q + 1) if q < 3 else
                                                     (y_done, 8 + 4 * (half + 1)))
            for br_ in range(2):
                chunk_done[C_MERGE + 3 * half + br_] = (proj_done, len(G1) + len(G2) + 8 * half + 4 * (br_ + 1))
            chunk_done[C_MERGE + 3 * half + 2] = (y_done, 16 + 4 * (half + 1))
            chunk_done[C_WO2 + half] = (y_done, 24 + 4 * (half + 1))
        for q in range(8):
            chunk_done[C_UP + q] = (up_done, 4 * (q + 1))

        T_PRE, T_MIX, T_MLP, T_N1, T_BR, T_N2 = range(6)
        NORM = {T_PRE: 0, T_MLP: 1, T_N1: 2, T_N2: 3}

        block = ctx.enter_context(nc.Block())

        @block.sync
        def _(sp):
            for i in range(NT):
                sp.dma_start(x[:, i, :], io["x"][0, i * P:(i + 1) * P, :]).then_inc(x_load[i], 16)

            def load(c, src):
                if c >= 2:
                    sp.wait_ge(*chunk_done[c - 2])
                k, n = src.shape[1], src.shape[2]
                sp.dma_start(ring_view(c, k, n), src).then_inc(ring_load[c % 2], 16)

            def up_cols(at):
                return io["w_up"][0][:, at].rearrange("(k p) c -> p k c", p=P)

            for c in range(C_UP):
                load(c, chunks[c])
            for n in range(2):
                load(C_UP + n, up_cols(slice(n * 512, (n + 1) * 512)))
            with sp.Fori(0, 3) as it:
                for s in range(2):
                    sp.wait_ge(up_done, it * 8 + 4 * (s + 1))
                    sp.dma_start(ring_view(s, KT, 512), up_cols(bass.ds(it * 1024 + (2 + s) * 512, 512))
                                 ).then_inc(ring_load[s], 16)
            for n in range(8):
                half, q = n // 4, n % 4
                load(C_DOWN + n, io["w_down"][0][q * 1024:(q + 1) * 1024, half * 512:(half + 1) * 512]
                     .rearrange("(k p) c -> p k c", p=P))
            for n, src in enumerate(chunks2):
                load(C_P2 + n, src)
            for half in range(2):
                c = C_MERGE + 3 * half
                load(c, cols_of(w2, MG + 512 * half, 512))
                load(c + 1, cols_of(w2, MG + D + 512 * half, 512))
                c += 2
                sp.wait_ge(*chunk_done[c - 2])
                for j, (name, sm) in enumerate((("w_branch_attn_2", ring_load[c % 2]), ("w_branch_mlstm_2", branch_load))):
                    sp.dma_start(ring[c % 2][:, j * 2048:(j + 1) * 2048].rearrange("p (k n) -> p k n", k=4),
                                 io[name][0][:, half * 512:(half + 1) * 512].rearrange("(k p) c -> p k c", p=P)
                                 ).then_inc(sm, 16)
            for half in range(2):
                load(C_WO2 + half, cols_of(io["w_out_2"][0], 512 * half, 512))
            names = ("w_expert_gate_2", "w_expert_up_2", "w_expert_down_2")
            views = [[expert_w[s][j].rearrange("p (k n) -> p k n", k=k) for j, k in enumerate((8, 8, 4))] for s in range(2)]
            source = [io[nm_].rearrange("l e (k p) n -> (l e) p k n", p=P) for nm_ in names]
            loads = (wg_load, wu_load, wd_load)
            sp.wait_ge(turn_evac, 40)
            for j in range(3):
                sp.dma_start(views[0][j], source[j][0]).then_inc(loads[j][0], 16)
            slot_free = {c % 2: chunk_done[c] for c in (C_WO2, C_WO2 + 1)}
            first = C_WO2 % 2
            for j in (first, 1 - first, 2):
                sp.wait_ge(*(slot_free[j] if j < 2 else (u_done, 8)))
                sp.dma_start(views[1][j], source[j][1]).then_inc(loads[j][1], 16)
            for i in range(NT):
                sp.wait_ge(turn_src, 4 * NORM[T_N2] + i + 1)
                sp.dma_start(h_dram[i * P:(i + 1) * P, :], stage[:, i % 2, :]).then_inc(h_store[i % 2], 16)
            with sp.Fori(0, NE // 2 - 1) as it:
                for s in range(2):
                    e = it * 2 + (2 + s)
                    sp.wait_ge(gu_done, it * 2 + (s + 1))
                    for j in range(2):
                        sp.dma_start(views[s][j], source[j][e]).then_inc(loads[j][s], 16)
                    sp.wait_ge(down_done, it * 2 + (s + 1))
                    sp.dma_start(views[s][2], source[2][e]).then_inc(loads[2][s], 16)
            sp.wait_ge(job_ready, 1)
            sp.wait_ge(down_done, NE)
            n = sp.value_load(njobs[0:1, 0:1], min_val=0, max_val=MAXJOBS)
            with sp.If(n > 0):
                with sp.Fori(0, n) as j:
                    ex = sp.value_load(jobs[0:1, bass.ds(j, 1)], min_val=0, max_val=NE - 1)
                    sp.wait_ge(ov["free"], j + 1)
                    for q, nm_ in enumerate(("wg", "wu", "wd")):
                        sp.dma_start(views[0][q], source[q][ex]).then_inc(ov[nm_], 16)
            for i in range(NT):
                sp.wait_ge(add_done, NT + i + 1)
                sp.dma_start(out[0, i * P:(i + 1) * P, :], x[:, i, :]).then_inc(out_store, 16)
            sp.wait_ge(out_store, 16 * NT)

        @block.gpsimd
        def _(pool):
            step = [0]

            def then(ins):
                step[0] += 1
                ins.then_inc(zero_ready, 1)
                pool.wait_ge(zero_ready, step[0])

            for t, v in ((ident, 0.0), (cmask, 0.0), (fmask, 0.0), (ones, 0.0)):
                then(pool.memset(t[:, :], v))
            then(pool.affine_select(out=ident[:, :], in_=ident[:, :], compare_op=ALU.not_equal, fill=1.0,
                                    base=0, pattern=[[-1, P]], channel_multiplier=1))
            then(pool.affine_select(out=cmask[:, 384:512], in_=cmask[:, 384:512], compare_op=ALU.is_ge, fill=NEG,
                                    base=0, pattern=[[-1, P]], channel_multiplier=1))
            then(pool.affine_select(out=fmask[:, :], in_=fmask[:, :], compare_op=ALU.is_ge, fill=NEG,
                                    base=0, pattern=[[1, P]], channel_multiplier=-1))
            for r in range(2):
                then(pool.memset(ones[64 * r:64 * r + 64, 64 * r:64 * r + 64], 1.0))
            then(pool.iota(iti[:, :], pattern=[[1, 64]], base=0, channel_multiplier=0))
            then(pool.tensor_copy(iot[:, :], iti[:, :]))
            then(pool.iota(iti[:, 0:NT], pattern=[[P, NT]], base=0, channel_multiplier=1))
            then(pool.tensor_copy(tokid[:, :], iti[:, 0:NT]))
            then(pool.memset(vzero[:, :], 0.0))
            pool.dma_start(id_dram.rearrange("(p n) o -> p (n o)", p=BLOCKS), vzero[:, :]).then_inc(id_zero, 16)
            pool.wait_ge(id_zero, 16)
            pool.memset(gcol[:, 1, 0:4], 1.0).then_inc(const_ready, 1)
            pool.dma_start(gb[:, :], io["g_post_mix"].partition_broadcast(P).rearrange("p o d -> p (o d)")).then_inc(gb_load, 16)
            pool.dma_start(y_dram[NE * BLK:ROWS, :].rearrange("(s j) (q c) -> s (j q) c", s=BLK, c=256),
                           cmask[0:BLK, 0:256].unsqueeze(1).broadcast_to([BLK, 4 * MAXJOBS, 256])).then_inc(y_zero, 16)
            pool.wait_ge(x_ready, 4)
            pool.dma_start(gb[:, :], io["g_post_mlp"].partition_broadcast(P).rearrange("p o d -> p (o d)")).then_inc(gb_load, 16)
            pool.wait_ge(x_ready, 8)
            then(pool.memset(yT[0:MROWS, :, :], 0.0))
            then(pool.memset(one_row, 1.0))
            for dr in range(2):
                then(pool.affine_select(out=selr[:, 4 * dr:4 * dr + 4, :], in_=selr[:, 4 * dr:4 * dr + 4, :],
                                        compare_op=ALU.not_equal, fill=1.0, base=-32 * dr,
                                        pattern=[[-1, 4], [0, P]], channel_multiplier=1))
            pool.memset(GL[:, :, :, :], 0.0).then_inc(const_ready, 1)
            pool.wait_ge(bline_ready, 1)
            pool.dma_start(l_dram, bline.unsqueeze(1).broadcast_to([8, P, 512])).then_inc(bline_store, 16)
            pool.wait_ge(bline_store, 16)
            skew = bass.AP(tensor=l_dram.tensor, offset=P - 1, ap=[[511, P], [P * 512, 8], [1, 3 * P]])
            pool.dma_start(bias, skew).then_inc(bias_load, 16)
            pool.wait_ge(hsum_done, 8)
            pool.dma_start(gb[:, :], io["norm2_g_2"].partition_broadcast(P).rearrange("p o d -> p (o d)")).then_inc(gb_load, 16)
            pool.wait_ge(u_done, 8)
            then(pool.memset(allone, 1.0))
            then(pool.memset(ltri, 0.0))
            then(pool.affine_select(out=ltri, in_=ltri, compare_op=ALU.is_ge, fill=1.0,
                                    base=0, pattern=[[-1, P]], channel_multiplier=1))
            for dst, name in ((wr[:, :, 0:NG], "w_router_group_2"), (wr[:, :, NG:NG + NE], "w_router_expert_2")):
                pool.dma_start(dst, io[name][0].rearrange("(k p) e -> p k e", p=P), allow_slow_non_contiguous=True
                               ).then_inc(wr_load, 16)
            pool.wait_ge(id_zero, 16)
            pool.wait_ge(pos_ready, 1)
            for c in range(2):
                for i in range(NT):
                    pool.indirect_dma_start(out=id_dram, out_offset=bass.IndirectOffsetOnAxis(ap=ipos[:, c, i:i + 1], axis=0),
                                            in_=tokid[:, i:i + 1], in_offset=None,
                                            bounds_check=ROWS - 1).then_inc(id_scatter, 16)
            pool.wait_ge(id_scatter, 16 * 2 * NT)
            pool.dma_start(smb[0:BLOCKS, 0, 0:BLK], id_dram.rearrange("(r s) o -> r (s o)", r=BLOCKS)).then_inc(id_load, 16)
            pool.wait_ge(y_zero, 16)
            pool.wait_ge(ids_ready, 1)
            for s in range(2):
                pool.wait_ge(h_store[s], 16 * (NT // 2))

            def fetch(e, s):
                pool.tensor_copy(idcol[:, s:s + 1], idsT[:, bass.ds(e, 1)]).then_inc(idcol_ready, 1)
                pool.wait_ge(idcol_ready, e + 1)
                pool.sem_inc(fetches, 1)
                pool.indirect_dma_start(out=xs[0:BLK, s, :], out_offset=None, in_=h_dram,
                                        in_offset=bass.IndirectOffsetOnAxis(ap=idcol[:, s:s + 1], axis=0)).then_inc(gather[s], 16)

            for e in range(2):
                fetch(e, e)
            with pool.Fori(0, NE // 2 - 1) as it:
                for s in range(2):
                    pool.wait_ge(xt_done, it * 2 + (s + 1))
                    fetch(it * 2 + (2 + s), s)
            pool.wait_ge(xt_done, NE)
            n = pool.value_load(njobs[0:1, 0:1], min_val=0, max_val=MAXJOBS)
            with pool.If(n > 0):
                with pool.Fori(0, n) as j:
                    pool.tensor_copy(idcol[:, 2:3], idsT[:, bass.ds(j + NE, 1)]).then_inc(ov["id"], 1)
                    pool.wait_ge(ov["id"], j + 1)
                    pool.sem_inc(fetches, 1)
                    pool.indirect_dma_start(out=xs[0:BLK, 0, :], out_offset=None, in_=h_dram,
                                            in_offset=bass.IndirectOffsetOnAxis(ap=idcol[:, 2:3], axis=0)).then_inc(ov["gather"], 16)
                    pool.wait_ge(ov["store"], j * 16 + 16)
            for s in range(2):
                pool.wait_ge(y_store[s], 16 * (NE // 2))
            for c in range(2):
                for i in range(NT):
                    if c:
                        pool.wait_ge(add_done, i + 1)
                    pool.indirect_dma_start(out=yg[:, i, :], out_offset=None, in_=y_dram,
                                            in_offset=bass.IndirectOffsetOnAxis(ap=ipos[:, c, i:i + 1], axis=0),
                                            bounds_check=ROWS - 1).then_inc(y_gather[i], 16)

        @block.tensor
        def _(pe):
            free_when = {}

            def take(*banks):
                for b in banks:
                    if b in free_when:
                        pe.wait_ge(*free_when.pop(b))

            pe.wait_ge(const_ready, 1)
            turns = [0]

            def turn(n):
                for i in range(NT):
                    src = (mix if n in (T_MIX, T_BR) else None)
                    if n in NORM:
                        pe.wait_ge(turn_src, 4 * NORM[n] + i + 1)
                    elif n == T_MIX:
                        pe.wait_ge(o_evac, 2 * i + 2)
                    else:
                        pe.wait_ge(o_evac, 2 * NT + i + 1)
                        pe.wait_ge(mnorm_done, i + 1)
                    for half in range(2):
                        b = (2 * i + half) % 4
                        take(b)
                        for k in range(4):
                            f = (4 * half + k) * P
                            t = src[:, i, f:f + P] if src is not None else stage[:, i % 2, f:f + P]
                            ins = pe.transpose(ps[:, b, k * P:(k + 1) * P], t, ident[:, :])
                        ins.then_inc(turn_done, 1)
                        turns[0] += 1
                        free_when[b] = (turn_evac, turns[0])

            proj = [0]
            chunk_seen = [-1]

            def use_chunk(c):
                if c != chunk_seen[0]:
                    pe.wait_ge(ring_load[c % 2], 16 * (c // 2 + 1))
                    chunk_seen[0] = c

            def group(bank, wait, value):
                take(bank)
                free_when[bank] = (wait, value)

            turn(T_PRE)
            pe.wait_ge(turn_evac, 8)
            ropes = vals = 0
            for g, (kind, c, j, _) in enumerate(G1):
                bank = 4 + g % 4
                use_chunk(c)
                if kind in ("rope", "ki"):
                    ropes += 1
                    n = P if kind == "rope" else HD
                    group(bank, rope_done, ropes)
                    wv = ring_view(c, KT, 512 if kind == "rope" else 72)
                    for k in range(KT):
                        ins = pe.matmul(ps[0:n, bank, :], wv[:, k, j * P:j * P + n], hT[:, k, :],
                                        start=(k == 0), stop=(k == KT - 1))
                elif kind == "val":
                    vals += 1
                    group(bank, val_done, vals)
                    wv = ring_view(c, KT, 512)
                    for k in range(KT):
                        ins = pe.matmul(ps[:, bank, :], hT[:, k, j * P:(j + 1) * P], wv[:, k, :],
                                        start=(k == 0), stop=(k == KT - 1))
                else:
                    group(bank, wi_done, 1)
                    wv = ring_view(c, KT, 72)
                    for i in range(NT):
                        for k in range(KT):
                            ins = pe.matmul(ps[:, bank, 8 * i:8 * i + 8], hT[:, k, i * P:(i + 1) * P],
                                            wv[:, k, HD:72], start=(k == 0), stop=(k == KT - 1))
                ins.then_inc(proj_done, 1)
                if g + 1 == N_IDX_FROM:
                    pe.wait_ge(rope_done, 5)
                    pe.wait_ge(ki_dup, 1)
                    for q, (i, h) in enumerate(IDX):
                        group(q % 4, relu_done, q + 1)
                        r = 64 * (h % 2)
                        pe.matmul(ps[:, q % 4, 0:(i + 1) * P], qiT[r:r + 64, h // 2, i * P:(i + 1) * P],
                                  kiT[r:r + 64, 0:(i + 1) * P], start=True, stop=True).then_inc(idx_done, 1)
            def attention(us):
                us = list(us)

                def scores(un):
                    for c, (q, k, _) in enumerate(un["maps"]):
                        m = un["m"] + c
                        group(m % 4, masked, m + 1)
                        pe.matmul(ps[:, m % 4, 0:un["w"]], q, k, start=True, stop=True).then_inc(score_done, 1)

                def turn_probs(un):
                    u = un["u"]
                    m = un["m"]
                    if un["kind"] == "diff":
                        pe.wait_ge(diff_done, un["d"])
                    else:
                        pe.wait_ge(exp_done, m + 1)
                    group(4 + u % 2, pt_ready, u + 1)
                    for k in range(un["w"] // P):
                        ins = pe.transpose(ps[:, 4 + u % 2, k * P:(k + 1) * P], smb[:, m % 4, k * P:(k + 1) * P],
                                           ident[:, :])
                    ins.then_inc(probT_done, 1)

                def values(un):
                    u = un["u"]
                    pe.wait_ge(pt_ready, u + 1)
                    bank = 6 + un["g"] % 2
                    if un["h"] == 0:
                        group(bank, o_evac, un["g"] + 1)
                    n = un["w"] // P
                    for k in range(n):
                        ins = pe.matmul(ps[:, bank, un["oc"][0]:un["oc"][1]], ptb[:, u % 2, k * P:(k + 1) * P],
                                        un["v"][:, un["k0"] + k, un["vc"][0]:un["vc"][1]],
                                        start=(k == 0), stop=(k == n - 1))
                    ins.then_inc(pv_done, 1)

                for a in range(len(us) + 2):
                    if a < len(us):
                        scores(units[us[a]])
                    if 0 <= a - 1 < len(us):
                        turn_probs(units[us[a - 1]])
                    if 0 <= a - 2:
                        values(units[us[a - 2]])

            pe.wait_ge(rope_done, 21)
            pe.wait_ge(val_done, 8)
            attention(ALL1)
            turn(T_MIX)
            ydone = [0]

            def token_out(c0, nchunk, lhs, when):
                for half in range(2):
                    for q in range(nchunk):
                        c = c0 + half * nchunk + q
                        use_chunk(c)
                        for k in range(8):
                            for i in range(NT):
                                bank = 2 * i + half
                                if q == 0 and k == 0:
                                    take(bank)
                                first, last = q == 0 and k == 0, q == nchunk - 1 and k == 7
                                ins = pe.matmul(ps[:, bank, :], lhs(8 * q + k, i), ring_view(c, KT, 512)[:, k, :],
                                                start=first, stop=last)
                                if last:
                                    ydone[0] += 1
                                    ins.then_inc(y_done, 1)
                                    free_when[bank] = when(i, half)
                                elif k == 7 and i == NT - 1:
                                    ins.then_inc(down_used, 1)

            pe.wait_ge(turn_evac, 16)
            token_out(C_WO, 1, lambda k, i: hT[:, k, i * P:(i + 1) * P], lambda i, half: (x_ready, i + 1))
            turn(T_MLP)
            pe.wait_ge(turn_evac, 24)
            take(4, 5, 6, 7)
            with pe.Fori(0, 4) as it:
                for s in range(2):
                    pe.wait_ge(ring_load[s], it * 16 + 16 * ((C_UP + s) // 2 + 1))
                    for j in range(4):
                        f = 4 * s + j
                        pe.wait_ge(up_free, it * 8 + (f + 1))
                        for k in range(KT):
                            ins = pe.matmul(ps[:, 4 + f % 4, :], ring_view(s, KT, 512)[:, k, j * P:(j + 1) * P],
                                            hT[:, k, :], start=(k == 0), stop=(k == KT - 1))
                        ins.then_inc(up_done, 1)
            pe.wait_ge(up_free, FT + 4)
            token_out(C_DOWN, 4, lambda k, i: uT[:, k, i * P:(i + 1) * P], lambda i, half: (x_ready, 4 + i + 1))
            turn(T_N1)
            pe.wait_ge(turn_evac, 32)
            pe.wait_ge(onehot_load, 32)
            take(0)
            pe.matmul(ps[0:8, 0, :], btab[:, :], onehot, start=True, stop=True).then_inc(btab_done, 1)
            free_when[0] = (bline_ready, 1)
            count = dict(conv=0, vm=0, qn=0, om=0)
            pending = []

            def norm_sums():
                q, = pending
                pending.clear()
                pe.wait_ge(sq_done, q)
                b = q % 4
                group(b, hstd_done, q)
                pe.matmul(ps[:, b, :], ones[:, :], stage[:, 0, (q % 2) * 512:(q % 2) * 512 + 512],
                          start=True, stop=True).then_inc(ssb_done, 1)

            for g, (kind, c, j) in enumerate(G2):
                g += len(G1)
                bank = 4 + g % 4
                use_chunk(c)
                if kind == "gates":
                    group(bank, gates_raw, 1)
                    for i in range(NT):
                        for k in range(KT):
                            ins = pe.matmul(ps[:, bank, 16 * i:16 * i + 16], hT[:, k, i * P:(i + 1) * P],
                                            ring_view(c, KT, 16)[:, k, :], start=(k == 0), stop=(k == KT - 1))
                elif kind in ("conv", "qnorm", "knorm", "om"):
                    if kind == "conv":
                        count["conv"] += 1
                        group(bank, conv_in, count["conv"])
                    elif kind == "om":
                        count["om"] += 1
                        group(bank, sig_done, count["om"])
                    else:
                        count["qn"] += 1
                        group(bank, qkn_done, count["qn"])
                    wv = ring_view(c, KT, 256 if kind == "knorm" else 512)
                    for k in range(KT):
                        ins = pe.matmul(ps[:, bank, :], wv[:, k, j * P:(j + 1) * P], hT[:, k, :],
                                        start=(k == 0), stop=(k == KT - 1))
                elif kind == "vm":
                    count["vm"] += 1
                    group(bank, vext_done, count["vm"])
                    for k in range(KT):
                        ins = pe.matmul(ps[:, bank, :], hT[:, k, j * P:(j + 1) * P], ring_view(c, KT, 512)[:, k, :],
                                        start=(k == 0), stop=(k == KT - 1))
                else:
                    group(bank, va2_done, 1)
                    for i in range(NT):
                        for k in range(KT):
                            ins = pe.matmul(ps[:, bank, P * i:P * i + P], hT[:, k, i * P:(i + 1) * P],
                                            ring_view(c, KT, 256)[:, k, P:256], start=(k == 0), stop=(k == KT - 1))
                ins.then_inc(proj_done, 1)
                if pending:
                    norm_sums()
                if kind in ("qnorm", "knorm"):
                    pending.append(count["qn"])
            pe.wait_ge(gate_rows, 1)
            for kind in range(2):
                take(kind)
                for i in range(NT):
                    ins = pe.transpose(ps[0:MROWS, kind, i * P:(i + 1) * P], GL[:, kind, i, :], ident[:, :])
                ins.then_inc(grow_done, 1)
                free_when[kind] = (grow_evac, kind + 1)
            pe.wait_ge(kdup_done, 2)
            pe.wait_ge(va2_done, 1)
            pe.wait_ge(scan_done, 1)
            take(2)
            for kind in range(2):
                for i in range(NT):
                    n = kind * NT + i
                    ins = pe.transpose(ps[:, 2, n * MROWS:(n + 1) * MROWS], rows[0:MROWS, kind, i * P:(i + 1) * P],
                                       ident[0:MROWS, 0:MROWS])
            ins.then_inc(gcol_done, 1)
            pe.wait_ge(qk_ready, 8)
            pe.wait_ge(acol_ready, 1)
            pe.wait_ge(em_ready, 1)
            pe.wait_ge(bias_load, 16)

            def bcast_m(r):
                h, dr = r // 2, r % 2
                group(4 + r % 2, wexp_done, 7 * (r + 1))
                pe.matmul(ps[:, 4 + r % 2, :], selr[:, dr * 4 + h, :], rows[0:MROWS, 3, :],
                          start=True, stop=True).then_inc(mb_done, 1)

            def qk(h):
                for j in range(NT):
                    group(j, sw_done, 4 * (2 * h + 2))
                    ins = pe.matmul(ps[:, j, :], qkT[:, 4 + h, j * P:(j + 1) * P], qkT[:, h, :],
                                    start=True, stop=True)
                ins.then_inc(qk_done, 1)

            def num(r):
                h, dr = r // 2, r % 2
                pe.wait_ge(sw_done, 4 * (r + 1))
                group(6, hsum_done, r + 1)
                group(7, hsum_done, r + 1)
                for i in range(NT):
                    js = range(0, i + 1) if dr == 0 else range(i, NT)
                    for j in js:
                        ins = pe.matmul(ps[:, 6 + i // 2, (i % 2) * 129:(i % 2) * 129 + 129],
                                        E[:, r % 2, j, i * P:(i + 1) * P], vext[:, j, h, :],
                                        start=(j == js[0]), stop=(j == js[-1]))
                ins.then_inc(num_done, 1)

            pe.wait_ge(vext_done, 4)
            pe.wait_ge(vone_done, 1)
            attention(ALL2)
            bcast_m(0)
            qk(0)
            bcast_m(1)
            for r in range(8):
                if r % 2 and r < 7:
                    qk(r // 2 + 1)
                num(r)
                if r + 2 < 8:
                    bcast_m(r + 2)
            turn(T_BR)
            gs = bo = 0
            for half in range(2):
                for br_ in range(2):
                    c = C_MERGE + 3 * half + br_
                    use_chunk(c)
                    for j in range(4):
                        bank = 4 + gs % 4
                        gs += 1
                        group(bank, gate_sig, gs)
                        for k in range(KT):
                            ins = pe.matmul(ps[:, bank, :], ring_view(c, KT, 512)[:, k, j * P:(j + 1) * P], hT[:, k, :],
                                            start=(k == 0), stop=(k == KT - 1))
                        ins.then_inc(proj_done, 1)
                c = C_MERGE + 3 * half + 2
                pe.wait_ge(turn_evac, 40)
                use_chunk(c)
                pe.wait_ge(branch_load, 16 * (half + 1))
                for j in range(4):
                    for br_ in range(2):
                        bank = (2 * bo + br_) % 4
                        group(bank, u_done, bo + 1)
                        for k in range(4):
                            ins = pe.matmul(ps[:, bank, :],
                                            ring[c % 2][:, br_ * 2048 + k * 512 + j * P:br_ * 2048 + k * 512 + (j + 1) * P],
                                            yT[:, 4 * br_ + k, :], start=(k == 0), stop=(k == 3))
                    bo += 1
                    ins.then_inc(y_done, 1)
                ydone[0] += 4
            pe.wait_ge(u_done, 8)
            token_out(C_WO2, 1, lambda k, i: merged[:, k, i * P:(i + 1) * P],
                      lambda i, half: (x_ready, 8 + 4 * half + i + 1))
            turn(T_N2)
            pe.wait_ge(turn_evac, 48)
            pe.wait_ge(wr_load, 32)
            take(4, 5, 6, 7)
            for i in range(NT):
                for k in range(KT):
                    ins = pe.matmul(ps[:, 4, i * (NG + NE):(i + 1) * (NG + NE)], hT[:, k, i * P:(i + 1) * P],
                                    wr[:, k, :], start=(k == 0), stop=(k == KT - 1))
            ins.then_inc(logits_done, 1)
            pe.wait_ge(sel_ready, 1)
            for i in range(NT):
                for j in range(i + 1):
                    pe.matmul(ps[:, 5, i * NE:(i + 1) * NE], ltri if j == i else allone, msel[:, 2, j, :],
                              start=(j == 0), stop=(j == i))
            for j in range(NT):
                ins = pe.matmul(ps[:, 5, NT * NE:(NT + 1) * NE], allone, msel[:, 2, j, :],
                                start=(j == 0), stop=(j == NT - 1))
            ins.then_inc(rank_done, 1)
            pe.wait_ge(id_load, 16)
            pe.transpose(ps[0:BLK, 6, 0:BLOCKS], smb[0:BLOCKS, 0, 0:BLK], ident[0:BLOCKS, 0:BLOCKS]).then_inc(idT_done, 1)
            pe.wait_ge(ids_ready, 1)
            take(0, 1, 2, 3)

            def turn_tokens(src, ready_sem):
                for k in range(KT):
                    ins = pe.transpose(ps[:, k // 4, (k % 4) * BLK:(k % 4 + 1) * BLK],
                                       src[:, k * P:(k + 1) * P], ident[0:BLK, 0:BLK])
                ins.then_inc(ready_sem, 1)

            wviews = [[expert_w[s][j].rearrange("p (k n) -> p k n", k=k) for j, k in enumerate((8, 8, 4))] for s in range(2)]

            def products(s, part, bank):
                for j in range(4):
                    for k in range(KT):
                        ins = pe.matmul(ps[:, bank, j * BLK:(j + 1) * BLK], wviews[s][part][:, k, j * P:(j + 1) * P],
                                        xsT[:, s, k, :], start=(k == 0), stop=(k == KT - 1))
                return ins

            def down(s, bank):
                for half in range(2):
                    for k in range(4):
                        ins = pe.matmul(ps[0:BLK, bank + half, :], hTe[:, s, k, :],
                                        wviews[s][2][:, k, half * 512:(half + 1) * 512], start=(k == 0), stop=(k == 3))
                return ins

            def expert(e, s, turns_of, first=False, last=False):
                pe.wait_ge(xT_ready, e + 1)
                if not first:
                    pe.wait_ge(hte_ready, e)
                pe.wait_ge(wg_load[s], turns_of * 16 + 16)
                products(s, 0, 2)
                pe.wait_ge(wu_load[s], turns_of * 16 + 16)
                products(s, 1, 3).then_inc(gu_done, 1)
                if not last:
                    t = 1 - s
                    pe.wait_ge(gather[t], (turns_of + s) * 16 + 16)
                    turn_tokens(xs[0:BLK, t, :], xt_done)
                pe.wait_ge(hte_ready, e + 1)
                pe.wait_ge(wd_load[s], turns_of * 16 + 16)
                down(s, 4 + 2 * s).then_inc(down_done, 1)

            pe.wait_ge(gather[0], 16)
            turn_tokens(xs[0:BLK, 0, :], xt_done)
            for e in range(2):
                expert(e, e, 0, first=(e == 0))
            with pe.Fori(1, NE // 2 - 1) as it:
                for s in range(2):
                    pe.wait_ge(ys_ready, it * 2 + (s - 1))
                    expert(it * 2 + s, s, it)
            for s in range(2):
                pe.wait_ge(ys_ready, NE - 2 + s - 1)
                expert(NE - 2 + s, s, NE // 2 - 1, last=(s == 1))
            pe.wait_ge(job_ready, 1)
            pe.wait_ge(ys_ready, NE)
            n = pe.value_load(njobs[0:1, 0:1], min_val=0, max_val=MAXJOBS)
            pe.sem_inc(ov["free"], 1)
            with pe.If(n > 0):
                with pe.Fori(0, n) as j:
                    pe.wait_ge(ov["gather"], j * 16 + 16)
                    turn_tokens(xs[0:BLK, 0, :], ov["xt"])
                    pe.wait_ge(ov["xT"], j + 1)
                    pe.wait_ge(ov["wg"], j * 16 + 16)
                    products(0, 0, 2)
                    pe.wait_ge(ov["wu"], j * 16 + 16)
                    products(0, 1, 3).then_inc(ov["gu"], 1)
                    pe.wait_ge(ov["hte"], j + 1)
                    pe.wait_ge(ov["wd"], j * 16 + 16)
                    down(0, 4).then_inc(ov["down"], 1)
                    pe.wait_ge(ov["ys"], j + 1)
                    pe.sem_inc(ov["free"], 1)

        @block.scalar
        def _(act):
            steps = [0]

            def then(ins):
                steps[0] += 1
                ins.then_inc(ac, 1)
                act.wait_ge(ac, steps[0])

            def bcast(src):
                return src.partition_broadcast(P)

            smalls = []

            def small_in(dst, src):
                smalls.append(dst)
                act.dma_start(dst, src, allow_slow_non_contiguous=True).then_inc(small_load, 16)

            for n, name in ((0, "g_pre_mix"), (2, "g_pre_mlp"), (3, "norm1_g_2")):
                small_in(gcol[:, n, :], io[name][0].rearrange("(k p) -> p k", p=P))
            small_in(gcol[:, 4, 4:8], io["mlstm_out_gain_2"][0].rearrange("h p -> p h"))
            small_in(gcol[:, 5, 0:1], io["g_diff_sub"][0].rearrange("(k p) -> p k", p=P))
            for n, name in enumerate(("lambda_q1", "lambda_k1", "lambda_q2", "lambda_k2")):
                small_in(lam_in[:, n, :], bcast(io[name][0]))
            small_in(rope[:, 0, :], io["rope_cos"])
            small_in(rope[:, 1, :], io["rope_sin"])
            for w in range(CONV):
                small_in(convw[:, :, w], io["mlstm_conv_w_2"][0, w].rearrange("(k p) -> p k", p=P))
            small_in(convb[:, :], io["mlstm_conv_b_2"][0].rearrange("(k p) -> p k", p=P))
            small_in(gateb[:, :], bcast(io["mlstm_gate_b_2"][0].rearrange("a b c -> (a b c)")))
            small_in(sink[:, :], bcast(io["attn_sink_2"][0]))
            for h in range(2):
                small_in(gqk[64 * h:64 * h + 64, 0:1], io["attn_q_gain_2"][0].rearrange("(p o) -> p o", o=1))
                small_in(gqk[64 * h:64 * h + 64, 1:2], io["attn_k_gain_2"][0].rearrange("(p o) -> p o", o=1))
            small_in(mergeb[:, :], io["merge_b_2"][0].rearrange("(k p) -> p k", p=P))
            small_in(btab[:, :], io["rel_bias_table_2"])
            small_in(br[:, 0:NG], bcast(io["b_router_group_2"][0]))
            small_in(br[:, NG:NG + NE], bcast(io["b_router_expert_2"][0]))

            assert len(smalls) == N_SMALL, len(smalls)

            def sumsq(i, src, out_col, done, n_done):
                act.activation(ptb[:, :, :], src, ACT.Square, accum_out=out_col).then_inc(done, 1)
                act.wait_ge(done, n_done)

            def norm(n, i):
                q = 4 * NORM[n] + i
                if n == T_PRE:
                    act.wait_ge(x_load[i], 16)
                else:
                    act.wait_ge(x_ready, {T_MLP: 0, T_N1: 4, T_N2: 12}[n] + i + 1)
                sumsq(i, x[:, i, :].rearrange("p (a b) -> p a b", a=2), ss[:, q:q + 1], sumsq_done, q + 1)
                act.activation(std[:, q:q + 1], ss[:, q:q + 1], ACT.Sqrt, bias=epsc[:, 0:1], scale=1.0 / D
                               ).then_inc(std_done, 1)

            def y_norm(e, i):
                q = 4 * e + i
                act.wait_ge(y_done, 8 * e + 4 + i + 1)
                sumsq(i, ps[:, 2 * i:2 * i + 2, :], ssy[:, q:q + 1], ysumsq, q + 1)
                act.activation(stdy[:, q:q + 1], ssy[:, q:q + 1], ACT.Sqrt, bias=epsc[:, 0:1], scale=1.0 / D
                               ).then_inc(ystd, 1)

            def y_norm_then(e, n):
                for a in range(NT + 1):
                    if a < NT:
                        y_norm(e, a)
                    if a >= 1:
                        norm(n, a - 1)

            act.wait_ge(const_ready, 1)
            act.wait_ge(dv, 1)
            for i in range(NT):
                norm(T_PRE, i)
            act.wait_ge(lam_dot, 1)
            act.activation(lamv[:, 2:4], lamv[:, 0:2], ACT.Exp).then_inc(lam_exp, 1)
            swaps = 0
            for g, (kind, _, _, dst) in enumerate(G1):
                bank = 4 + g % 4
                if kind in ("rope", "ki"):
                    act.wait_ge(proj_done, g + 1)
                    if swaps >= 2:
                        act.wait_ge(rope_done, swaps - 1)
                    for r in range(4 if kind == "rope" else 2):
                        ins = act.activation(ptb[32 * r:32 * r + 32, swaps % 2, :],
                                             ps[32 * (r ^ 1):32 * (r ^ 1) + 32, bank, :], ACT.Copy)
                    ins.then_inc(swap_done, 1)
                    swaps += 1
                    if kind == "ki":
                        act.wait_ge(rope_done, swaps)
                        act.activation(kiT[64:128, :], kiT[0:64, :], ACT.Copy).then_inc(ki_dup, 1)
                elif kind == "val":
                    act.wait_ge(proj_done, g + 1)
                    act.activation(dst, ps[:, bank, :], ACT.Copy).then_inc(val_done, 1)
                if g + 1 == N_IDX_FROM:
                    for q, (i, h) in enumerate(IDX):
                        act.wait_ge(idx_done, q + 1)
                        if q >= 2:
                            act.wait_ge(comb_done, q - 1)
                        act.activation(rbuf[:, q % 2, 0:(i + 1) * P], ps[:, q % 4, 0:(i + 1) * P], ACT.Relu
                                       ).then_inc(relu_done, 1)
            def attention(us):
                us = list(us)

                def exps(un):
                    for c in range(len(un["maps"])):
                        m = un["m"] + c
                        act.wait_ge(negmax, m + 1)
                        if un["kind"] == "window":
                            act.activation(es[:, m - M1 + 0:m - M1 + 1], sink[:, un["h"]:un["h"] + 1], ACT.Exp,
                                           bias=nm[:, m:m + 1])
                        row = smb[:, m % 4, 0:un["w"]]
                        act.activation(row, row, ACT.Exp, bias=nm[:, m:m + 1], scale=un["scale"],
                                       accum_out=den[:, m:m + 1]).then_inc(exp_done, 1)

                def take_turned(un):
                    u = un["u"]
                    act.wait_ge(probT_done, u + 1)
                    if u >= 2:
                        act.wait_ge(pv_done, u - 1)
                    act.activation(ptb[:, u % 2, 0:un["w"]], ps[:, 4 + u % 2, 0:un["w"]], ACT.Copy).then_inc(pt_ready, 1)

                for a in range(len(us) + 5):
                    if a < len(us):
                        exps(units[us[a]])
                    if 0 <= a - 1 < len(us):
                        take_turned(units[us[a - 1]])
                    for lag, part in ((3, 0), (4, 1)):
                        if 0 <= a - lag < len(us):
                            un = units[us[a - lag]]
                            if not (un["kind"] == "diff" and un["last"]):
                                continue
                            i = un["tile"]
                            if part == 0:
                                act.wait_ge(pv_done, un["u"] + 1)
                                if i:
                                    act.wait_ge(o_ss, i)
                                act.activation(stage[:, 0, 0:512], ps[:, 6 + un["g"] % 2, :], ACT.Square
                                               ).then_inc(o_sq, 1)
                            else:
                                act.wait_ge(o_ss, i + 1)
                                act.activation(hstd[:, 4 * i:4 * i + 4], hss[:, 4 * i:4 * i + 4], ACT.Sqrt,
                                               bias=epsc[:, 0:1], scale=1.0 / P).then_inc(o_std, 1)

            attention(ALL1)
            y_norm_then(0, T_MLP)
            with act.Fori(0, 4) as it:
                for f in range(8):
                    act.wait_ge(up_done, it * 8 + (f + 1))
                    act.activation(smb[:, f % 4, :], ps[:, 4 + f % 4, :], ACT.Relu).then_inc(up_relu, 1)
            act.wait_ge(up_free, FT + 4)
            act.dma_start(onehot, io["bucket_onehot"]).then_inc(onehot_load, 16)
            act.dma_start(wmask, io["window_mask"]).then_inc(onehot_load, 16)
            y_norm_then(1, T_N1)
            convs = vms = qn = oms = 0

            def silu(c):
                act.wait_ge(conv_done, c + 1)
                act.activation(qkT[:, c, :], qkT[:, c, :], ACT.Silu, bias=convb[:, c:c + 1]).then_inc(qk_ready, 1)

            def head_std(q):
                act.wait_ge(ssb_done, q)
                if q >= 3:
                    act.wait_ge(qkn_done, q - 2)
                act.activation(stage[:, 1, (q % 2) * 512:(q % 2) * 512 + 512], ps[:, q % 4, :], ACT.Sqrt,
                               bias=epsc[:, 0:1], scale=1.0 / HD).then_inc(hstd_done, 1)

            for g, (kind, _, c) in enumerate(G2):
                g += len(G1)
                bank = 4 + g % 4
                src = ps[:, bank, :]
                if kind == "gates":
                    act.wait_ge(gates_raw, 1)
                    fv = G[:, :, :].rearrange("p i (d k h) -> p k i d h", d=2, k=2)[:, 1]
                    lv = [lfw[:, q, :, :].rearrange("p i (d h) -> p i d h", d=2) for q in range(3)]
                    then(act.activation(lv[0], fv, ACT.Abs))
                    then(act.activation(lv[1], lv[0], ACT.Exp, scale=-1.0))
                    act.activation(lv[2], lv[1], ACT.Ln, bias=1.0).then_inc(gate_abs, 1)
                    continue
                act.wait_ge(proj_done, g + 1)
                if kind == "conv":
                    act.activation(convin[:, convs, 2:514], src, ACT.Copy).then_inc(conv_in, 1)
                    convs += 1
                    if convs >= 2:
                        silu(convs - 2)
                elif kind == "vm":
                    act.activation(vext[:, c, :, 0:DM], src.rearrange("p (h e) -> p h e", h=4), ACT.Copy
                                   ).then_inc(vext_done, 1)
                    if vms == 0:
                        silu(7)
                    vms += 1
                elif kind in ("qnorm", "knorm"):
                    qn += 1
                    if qn >= 3:
                        act.wait_ge(ssb_done, qn - 2)
                    act.activation(stage[:, 0, (qn % 2) * 512:(qn % 2) * 512 + 512], src, ACT.Square).then_inc(sq_done, 1)
                    if qn >= 2:
                        head_std(qn - 1)
                elif kind == "va2":
                    act.activation(va2[:, :, :].rearrange("p i c -> p (i c)"), src, ACT.Copy).then_inc(va2_done, 1)
                    head_std(5)
                    act.wait_ge(qkn_done, 5)
                    act.activation(kdup[64:128, 0, :], kdup[0:64, 0, :], ACT.Copy).then_inc(kdup_done, 1)
                    act.activation(kdup[0:64, 1, :], kdup[64:128, 1, :], ACT.Copy).then_inc(kdup_done, 1)
                else:
                    act.activation(sigT[:, c, :], src, ACT.Sigmoid).then_inc(sig_done, 1)
            act.wait_ge(acol_ready, 1)
            act.activation(colsb[:, 1, :, :], ps[:, 2, NT * MROWS:2 * NT * MROWS].rearrange("p (i r) -> p i r", i=NT),
                           ACT.Exp, scale=-1.0).then_inc(em_ready, 1)
            attention(ALL2)
            act.wait_ge(pv_done, len(units))
            act.wait_ge(acol_ready, 1)
            for r in range(8):
                h, dr = r // 2, r % 2
                act.wait_ge(nmd_done, r + 1)
                if r >= 2:
                    act.wait_ge(num_done, r - 1)
                for j in range(NT):
                    a_col = colsb[:, 0, j, 32 * dr + h:32 * dr + h + 1]
                    act.activation(E[:, r % 2, j, j * P:(j + 1) * P], nmd[:, r % 2, j, :], ACT.Exp, bias=a_col
                                   ).then_inc(wexp_done, 1)
                    lo, hi = ((j + 1) * P, 512) if dr == 0 else (0, j * P)
                    if lo < hi:
                        act.activation(E[:, r % 2, j, lo:hi], ps[:, 4 + r % 2, lo:hi], ACT.Exp, bias=a_col
                                       ).then_inc(wexp_done, 1)
            act.wait_ge(hsum_done, 8)
            for a in range(NT + 1):
                if a < NT:
                    if a >= 2:
                        act.wait_ge(mss_done, a - 1)
                    act.activation(stage[:, a % 2, 0:512], mix[:, a, 512:1024], ACT.Square).then_inc(msq_done, 1)
                if a >= 1:
                    act.wait_ge(mss_done, a)
                    at = 16 + 4 * (a - 1)
                    act.activation(hstd[:, at:at + 4], hss[:, at:at + 4], ACT.Sqrt, bias=epsc[:, 0:1], scale=1.0 / DM
                                   ).then_inc(mstd_done, 1)
            gs = 0
            for half in range(2):
                for br_ in range(2):
                    for j in range(4):
                        bank = 4 + gs % 4
                        gs += 1
                        act.wait_ge(proj_done, len(G1) + len(G2) + gs)
                        if half:
                            act.wait_ge(u_done, j + 1)
                        b_ = 8 * br_ + 4 * half + j
                        act.activation(gates[:, br_, j, :], ps[:, bank, :], ACT.Sigmoid, bias=mergeb[:, b_:b_ + 1]
                                       ).then_inc(gate_sig, 1)
            for i in range(NT):
                norm(T_N2, i)
            for n in range(2):
                act.wait_ge(r_exp, n + 1)
                if n == 0:
                    act.activation(r_ge, r_gd, ACT.Exp).then_inc(r_exp_done, 1)
                else:
                    act.activation(r_x2, r_dv, ACT.Exp).then_inc(r_exp_done, 1)
            def expert(e, s, turns_of, first=False):
                act.wait_ge(gu_done, e + 1)
                act.activation(sg[:, s, :, :].rearrange("p k t -> p (k t)"), ps[:, 2, 0:4 * BLK], ACT.Silu
                               ).then_inc(silu_done, 1)
                act.wait_ge(down_done, e + 1)
                if not first:
                    act.wait_ge(y_store[s], turns_of * 16)
                act.activation(ys[0:BLK, s, :].rearrange("p (a b) -> p a b", a=2), ps[0:BLK, 4 + 2 * s:6 + 2 * s, :],
                               ACT.Copy).then_inc(ys_ready, 1)
                act.wait_ge(ys_ready, e + 1)
                act.dma_start(y_dram[bass.ds(e * BLK, BLK), :], ys[0:BLK, s, :]).then_inc(y_store[s], 16)

            for e in range(2):
                expert(e, e, 0, first=True)
            with act.Fori(1, NE // 2) as it:
                for s in range(2):
                    expert(it * 2 + s, s, it)
            act.wait_ge(job_ready, 1)
            for s in range(2):
                act.wait_ge(y_store[s], 16 * (NE // 2))
            n = act.value_load(njobs[0:1, 0:1], min_val=0, max_val=MAXJOBS)
            with act.If(n > 0):
                with act.Fori(0, n) as j:
                    act.wait_ge(ov["gu"], j + 1)
                    act.activation(sg[:, 0, :, :].rearrange("p k t -> p (k t)"), ps[:, 2, 0:4 * BLK], ACT.Silu
                                   ).then_inc(ov["silu"], 1)
                    act.wait_ge(ov["down"], j + 1)
                    act.activation(ys[0:BLK, 0, :].rearrange("p (a b) -> p a b", a=2), ps[0:BLK, 4:6, :],
                                   ACT.Copy).then_inc(ov["ys"], 1)
                    act.wait_ge(ov["ys"], j + 1)
                    act.dma_start(y_dram[bass.ds(j * BLK + NE * BLK, BLK), :], ys[0:BLK, 0, :]).then_inc(ov["store"], 16)
                    act.wait_ge(ov["store"], j * 16 + 16)

        @block.vector
        def _(dve):
            steps = [0]

            def then(ins):
                steps[0] += 1
                ins.then_inc(dv, 1)
                dve.wait_ge(dv, steps[0])

            def bc(col_, n):
                return col_.unsqueeze(len(col_.shape)).broadcast_to(list(col_.shape) + [n])

            turned = [0]

            def take_turned(n, i):
                for half in range(2):
                    g = turned[0]
                    turned[0] += 1
                    dve.wait_ge(turn_done, g + 1)
                    src = ps[:, (2 * i + half) % 4, :].rearrange("p (k t) -> p k t", k=4)
                    dst = (yT if n == T_BR else hT)[:, 4 * half:4 * half + 4, i * P:(i + 1) * P]
                    if n == T_N2 or (n == T_BR and half == 0):
                        dve.tensor_copy(dst, src).then_inc(turn_evac, 1)
                    elif n == T_BR:
                        then(dve.tensor_tensor(dst, src, bc(gcol[:, 4, 4:8], P), ALU.mult))
                        dve.tensor_tensor(dst, dst, sigT[:, :, i * P:(i + 1) * P], ALU.mult).then_inc(turn_evac, 1)
                    else:
                        gi = {T_PRE: 0, T_MIX: 1, T_MLP: 2, T_N1: 3}[n]
                        dve.tensor_tensor(dst, src, bc(gcol[:, gi, 4 * half:4 * half + 4], P), ALU.mult
                                          ).then_inc(turn_evac, 1)

            def norm_stage(n, i):
                q = 4 * NORM[n] + i
                dve.wait_ge(std_done, q + 1)
                then(dve.reciprocal(rstd[:, q:q + 1], std[:, q:q + 1]))
                if i >= 2:
                    dve.wait_ge(turn_done, 8 * n + 2 * (i - 2) + 2)
                    if n == T_N2:
                        dve.wait_ge(h_store[i % 2], 16 * (i // 2))
                if n == T_N2:
                    dve.scalar_tensor_tensor(out=stage[:, i % 2, :], in0=x[:, i, :], scalar=rstd[:, q:q + 1],
                                             in1=gb[:, :], op0=ALU.mult, op1=ALU.mult).then_inc(turn_src, 1)
                else:
                    dve.tensor_scalar(stage[:, i % 2, :], x[:, i, :], rstd[:, q:q + 1], None, ALU.mult
                                      ).then_inc(turn_src, 1)

            def norm(n):
                for a in range(NT + 1):
                    if a < NT:
                        norm_stage(n, a)
                    if a >= 1:
                        take_turned(n, a - 1)

            def add_normed(e, n, i):
                q = 4 * e + i
                dve.wait_ge(ystd, q + 1)
                then(dve.reciprocal(rsty[:, q:q + 1], stdy[:, q:q + 1]))
                if i >= 2:
                    dve.wait_ge(turn_done, 8 * n + 2 * (i - 2) + 2)
                st = stage[:, i % 2, :]
                then(dve.scalar_tensor_tensor(out=st.rearrange("p (a b) -> p a b", a=2), in0=ps[:, 2 * i:2 * i + 2, :],
                                              scalar=rsty[:, q:q + 1], in1=gb[:, :].rearrange("p (a b) -> p a b", a=2),
                                              op0=ALU.mult, op1=ALU.mult))
                dve.tensor_tensor(x[:, i, :], x[:, i, :], st, ALU.add).then_inc(x_ready, 1)

            dve.wait_ge(const_ready, 1)
            then(dve.memset(epsc[:, :], EPS))
            dve.wait_ge(small_load, 16 * N_SMALL)
            then(dve.tensor_scalar(gcol[:, 1, 4:8], gcol[:, 5, 0:1].broadcast_to([P, 4]), 1.0 - LAM_INIT, None, ALU.mult))
            norm(T_PRE)
            for n in range(2):
                then(dve.tensor_tensor_reduce(lam_in[:, 2 * n, :], lam_in[:, 2 * n, :], lam_in[:, 2 * n + 1, :],
                                              1.0, 0.0, ALU.mult, ALU.add, lamv[:, n:n + 1]))
            dve.sem_inc(lam_dot, 1)
            dve.wait_ge(lam_exp, 1)
            then(dve.tensor_tensor(lamv[:, 4:5], lamv[:, 3:4], lamv[:, 2:3], ALU.subtract))
            then(dve.tensor_scalar(lamv[:, 5:6], lamv[:, 4:5], -LAM_INIT, None, ALU.add))

            def take_steps():
                for i in range(1, NT):
                    row = idx_s[:, i - 1, 0:(i + 1) * P]
                    for q in range(TOPK // 8):
                        then(dve.max(m8, row))
                        then(dve.match_replace(row, m8, row, TAKEN))
                        if q == TOPK // 8 - 1:
                            then(dve.tensor_scalar(dmask[:, i - 1, 0:(i + 1) * P], row, TAKEN, NEG,
                                                   ALU.not_equal, ALU.mult))
                        yield

            steps_left = take_steps()
            ropes = 0
            for g, (kind, _, _, dst) in enumerate(G1):
                bank = 4 + g % 4
                if kind in ("rope", "ki"):
                    n = P if kind == "rope" else HD
                    d_ = dst if kind == "rope" else kiT[0:HD, :]
                    dve.wait_ge(proj_done, g + 1)
                    sw = ptb[0:n, ropes % 2, :]
                    ropes += 1
                    dve.wait_ge(swap_done, ropes)
                    dve.tensor_tensor(d_, ps[0:n, bank, :], rope[0:n, 0, :], ALU.mult)
                    then(dve.tensor_tensor(sw, sw, rope[0:n, 1, :], ALU.mult))
                    dve.tensor_tensor(d_, d_, sw, ALU.add).then_inc(rope_done, 1)
                elif kind == "wi":
                    dve.wait_ge(proj_done, g + 1)
                    dve.tensor_copy(wi[:, :, :], ps[:, bank, 0:32].rearrange("p (i h) -> p i h", i=NT)).then_inc(wi_done, 1)
                if g + 1 == N_IDX_FROM:
                    dve.wait_ge(wi_done, 1)
                    for q, (i, h) in enumerate(IDX):
                        w = (i + 1) * P
                        dve.wait_ge(relu_done, q + 1)
                        row = idx_s[:, i - 1, 0:w]
                        if h == 0:
                            dve.tensor_scalar(row, rbuf[:, q % 2, 0:w], wi[:, i, h:h + 1], None, ALU.mult
                                              ).then_inc(comb_done, 1)
                        else:
                            dve.wait_ge(comb_done, q)
                            dve.scalar_tensor_tensor(out=row, in0=rbuf[:, q % 2, 0:w], scalar=wi[:, i, h:h + 1],
                                                     in1=row, op0=ALU.mult, op1=ALU.add).then_inc(comb_done, 1)
                        if h == 7:
                            dve.wait_ge(comb_done, q + 1)
                            then(dve.tensor_scalar(row, row, IDX_SCALE, None, ALU.mult))
                            diag = idx_s[:, i - 1, w - P:w]
                            then(dve.scalar_tensor_tensor(out=diag, in0=cmask[:, 384:512], scalar=LOWEST / NEG,
                                                          in1=diag, op0=ALU.mult, op1=ALU.add))
                if g >= N_IDX_FROM and kind == "rope":
                    for _ in range(3):
                        next(steps_left, None)
            for _ in steps_left:
                pass
            def attention(us):
                us = list(us)

                def scores(un):
                    w = un["w"]
                    for c, (_, _, mask) in enumerate(un["maps"]):
                        m = un["m"] + c
                        dve.wait_ge(score_done, m + 1)
                        if m >= 4:
                            dve.wait_ge(probT_done, map_unit[m - 4] + 1)
                        dve.tensor_tensor_reduce(smb[:, m % 4, 0:w], ps[:, m % 4, 0:w], mask, 1.0, LOWEST,
                                                 ALU.add, ALU.max, mx[:, m:m + 1]).then_inc(masked, 1)
                        dve.wait_ge(masked, m + 1)
                        if un["kind"] == "window":
                            dve.tensor_scalar(nm[:, m:m + 1], mx[:, m:m + 1], sink[:, un["h"]:un["h"] + 1], -1.0,
                                              ALU.max, ALU.mult).then_inc(negmax, 1)
                        else:
                            dve.tensor_scalar(nm[:, m:m + 1], mx[:, m:m + 1], -un["scale"], None, ALU.mult
                                              ).then_inc(negmax, 1)

                def difference(un):
                    m = un["m"]
                    dve.wait_ge(exp_done, m + 2)
                    then(dve.reciprocal(den[:, m:m + 2], den[:, m:m + 2]))
                    then(dve.tensor_scalar(den[:, m + 1:m + 2], den[:, m + 1:m + 2], lamv[:, 5:6], None, ALU.mult))
                    a_, b_ = smb[:, m % 4, 0:un["w"]], smb[:, (m + 1) % 4, 0:un["w"]]
                    then(dve.tensor_scalar(a_, a_, den[:, m:m + 1], None, ALU.mult))
                    dve.scalar_tensor_tensor(out=a_, in0=b_, scalar=den[:, m + 1:m + 2], in1=a_,
                                             op0=ALU.mult, op1=ALU.add).then_inc(diff_done, 1)

                def outputs(un):
                    i, bank = un["tile"], 6 + un["g"] % 2
                    dve.wait_ge(pv_done, un["u"] + 1)
                    m0 = un["m"] - 7
                    r8 = den[:, m0:m0 + 8]
                    if un["kind"] == "window":
                        then(dve.tensor_tensor(r8, r8, es[:, m0 - M1:m0 - M1 + 8], ALU.add))
                    then(dve.reciprocal(r8, r8))
                    dve.tensor_tensor(mix[:, i, 0:512].rearrange("p (h e) -> p h e", h=8),
                                      ps[:, bank, :].rearrange("p (h e) -> p h e", h=8), bc(r8, HD), ALU.mult
                                      ).then_inc(o_evac, 1)

                def diff_squares(un):
                    i = un["tile"]
                    dve.wait_ge(o_sq, i + 1)
                    dve.tensor_reduce(hss[:, 4 * i:4 * i + 4], stage[:, 0, 0:512].rearrange("p (h e) -> p h e", h=4),
                                      AX.X, ALU.add).then_inc(o_ss, 1)

                def diff_outputs(un):
                    i, bank = un["tile"], 6 + un["g"] % 2
                    dve.wait_ge(o_std, i + 1)
                    then(dve.reciprocal(hrs[:, 4 * i:4 * i + 4], hstd[:, 4 * i:4 * i + 4]))
                    dve.tensor_tensor(mix[:, i, 512:1024].rearrange("p (h e) -> p h e", h=4),
                                      ps[:, bank, :].rearrange("p (h e) -> p h e", h=4),
                                      bc(hrs[:, 4 * i:4 * i + 4], P), ALU.mult).then_inc(o_evac, 1)

                for a in range(len(us) + 6):
                    if a < len(us):
                        scores(units[us[a]])
                    if 0 <= a - 1 < len(us) and units[us[a - 1]]["kind"] == "diff":
                        difference(units[us[a - 1]])
                    for lag, kinds, part in ((3, ("topk", "window"), outputs), (4, ("diff",), diff_squares),
                                             (5, ("diff",), diff_outputs)):
                        if 0 <= a - lag < len(us) and units[us[a - lag]]["last"] and units[us[a - lag]]["kind"] in kinds:
                            part(units[us[a - lag]])

            attention(ALL1)
            for i in range(NT):
                take_turned(T_MIX, i)
            def epilog(e, n):
                dve.wait_ge(gb_load, 16 * (e + 1))
                for a in range(NT + 2):
                    if a < NT:
                        add_normed(e, n, a)
                    if 0 <= a - 1 < NT:
                        norm_stage(n, a - 1)
                    if 0 <= a - 2:
                        take_turned(n, a - 2)

            epilog(0, T_MLP)
            dve.sem_inc(up_free, 4)
            with dve.Fori(0, 4) as it:
                for f in range(8):
                    dve.wait_ge(up_relu, it * 8 + (f + 1))
                    dve.tensor_tensor(uT[:, bass.ds(it * 8 + f, 1), :], smb[:, f % 4:f % 4 + 1, :],
                                      smb[:, f % 4:f % 4 + 1, :], ALU.mult).then_inc(up_free, 1)
            epilog(1, T_N1)
            dve.memset(vext[:, :, :, DM:DM + 1], 1.0).then_inc(vone_done, 1)
            for a in (0, 514):
                dve.memset(convin[:, :, a:a + 2], 0.0)
            then(dve.tensor_scalar(gqk[:, 0:1], gqk[:, 0:1], HD ** -0.5, None, ALU.mult))
            dve.wait_ge(onehot_load, 32)
            dve.wait_ge(btab_done, 1)
            dve.tensor_tensor(bline, ps[0:8, 0, :], wmask, ALU.add).then_inc(bline_ready, 1)
            convs = qn = 0

            def head_norm(q):
                g = [a for a, x_ in enumerate(G2) if x_[0] in ("qnorm", "knorm")][q - 1] + len(G1)
                bank = 4 + g % 4
                dve.wait_ge(hstd_done, q)
                rs = stage[:, 1, (q % 2) * 512:(q % 2) * 512 + 512]
                then(dve.reciprocal(rs, rs))
                if q <= 4:
                    dve.scalar_tensor_tensor(out=qT[:, q - 1, :], in0=ps[:, bank, :], scalar=gqk[:, 0:1], in1=rs,
                                             op0=ALU.mult, op1=ALU.mult).then_inc(qkn_done, 1)
                else:
                    for h in range(2):
                        r = slice(64 * h, 64 * h + 64)
                        ins = dve.scalar_tensor_tensor(out=kdup[r, h, :], in0=ps[r, bank, :], scalar=gqk[r, 1:2],
                                                       in1=rs[r, :], op0=ALU.mult, op1=ALU.mult)
                    ins.then_inc(qkn_done, 1)

            for g, (kind, _, c) in enumerate(G2):
                g += len(G1)
                bank = 4 + g % 4
                if kind == "gates":
                    dve.wait_ge(proj_done, g + 1)
                    gbb = gateb[:, :].unsqueeze(1).broadcast_to([P, NT, 16])
                    dve.tensor_tensor(G[:, :, :], ps[:, bank, 0:64].rearrange("p (i c) -> p i c", i=NT), gbb, ALU.add
                                      ).then_inc(gates_raw, 1)
                    dve.wait_ge(gates_raw, 1)
                    dve.wait_ge(const_ready, 2)
                    gv = G[:, :, :].rearrange("p i (d k h) -> p k i d h", d=2, k=2)
                    lv = [lfw[:, q, :, :].rearrange("p i (d h) -> p i d h", d=2) for q in range(3)]
                    dve.wait_ge(gate_abs, 1)
                    then(dve.tensor_scalar(lv[0], gv[:, 1], 0.0, None, ALU.min))
                    then(dve.tensor_tensor(lfw[:, 0], lfw[:, 0], lfw[:, 2], ALU.subtract))
                    for dr in range(2):
                        dve.tensor_copy(GL[:, 0, :, 32 * dr:32 * dr + 4], gv[:, 0, :, dr, :])
                        ins = dve.tensor_copy(GL[:, 1, :, 32 * dr:32 * dr + 4], lv[0][:, :, dr, :])
                    ins.then_inc(gate_rows, 1)
                elif kind == "conv":
                    dve.wait_ge(conv_in, convs + 1)
                    acc = qkT[:, convs, :]
                    for w in range(CONV):
                        tap = convin[:, convs, w:w + 512]
                        if w == 0:
                            then(dve.tensor_scalar(acc, tap, convw[:, convs, 0:1], None, ALU.mult))
                        else:
                            ins = dve.scalar_tensor_tensor(out=acc, in0=tap, scalar=convw[:, convs, w:w + 1], in1=acc,
                                                           op0=ALU.mult, op1=ALU.add)
                            if w < CONV - 1:
                                then(ins)
                            else:
                                ins.then_inc(conv_done, 1)
                    convs += 1
                elif kind in ("qnorm", "knorm"):
                    qn += 1
                    if qn >= 2:
                        head_norm(qn - 1)
                elif kind == "va2":
                    head_norm(5)
            for kind in range(2):
                dve.wait_ge(grow_done, kind + 1)
                dve.tensor_copy(rows[:, kind, :], ps[0:MROWS, kind, :]).then_inc(grow_evac, 1)
            dve.wait_ge(grow_evac, 2)
            order = ((slice(0, 4), slice(None)), (slice(32, 36), slice(None, None, -1)))
            for pr, fr in order:
                ins = dve.tensor_tensor_scan(rows[pr, 2, fr], one_row[pr, fr], rows[pr, 1, fr], 0.0, ALU.mult, ALU.add)
            then(ins)
            then(dve.tensor_tensor(rows[:, 0, :], rows[:, 0, :], rows[:, 2, :], ALU.subtract))
            for pr, fr in order:
                ins = dve.tensor_tensor_scan(rows[pr, 3, fr], zero_row[pr, fr], rows[pr, 0, fr], 0.0, ALU.add, ALU.max)
            then(ins)
            then(dve.tensor_tensor(rows[:, 1, :], rows[:, 2, :], rows[:, 3, :], ALU.add))
            dve.tensor_scalar(rows[:, 3, :], rows[:, 3, :], -1.0, None, ALU.mult).then_inc(scan_done, 1)
            dve.wait_ge(gcol_done, 1)
            dve.tensor_copy(colsb[:, 0, :, :], ps[:, 2, 0:NT * MROWS].rearrange("p (i r) -> p i r", i=NT)
                            ).then_inc(acol_ready, 1)
            dve.wait_ge(bias_load, 16)
            attention(ALL2)
            dve.wait_ge(em_ready, 1)

            def masked_m(r):
                tri = (fmask[:, :] if r % 2 == 0 else cmask[:, 384:512])
                dve.wait_ge(mb_done, r + 1)
                if r >= 2:
                    dve.wait_ge(wexp_done, 7 * (r - 1))
                dve.tensor_tensor(nmd[:, r % 2, :, :], ps[:, 4 + r % 2, :].rearrange("p (j t) -> p j t", j=NT),
                                  tri.unsqueeze(1).broadcast_to([P, NT, P]), ALU.add).then_inc(nmd_done, 1)

            def weigh(r):
                dve.wait_ge(qk_done, r // 2 + 1)
                for j in range(NT):
                    lo, hi = (j * P, 512) if r % 2 == 0 else (0, (j + 1) * P)
                    if j == 0:
                        dve.wait_ge(wexp_done, 7 * (r + 1))
                    dve.scalar_tensor_tensor(out=E[:, r % 2, j, lo:hi], in0=ps[:, j, lo:hi], scalar=DM ** -0.5,
                                             in1=E[:, r % 2, j, lo:hi], op0=ALU.mult, op1=ALU.mult).then_inc(sw_done, 1)

            def head_sum(r):
                h, dr = r // 2, r % 2
                dve.wait_ge(num_done, r + 1)
                nd = ps[:, 6:8, 0:258].rearrange("p b (c e) -> p b c e", e=DM + 1)
                d0, d1 = mden[:, 0, :], mden[:, 1, :]
                then(dve.tensor_copy(d0.rearrange("p (b c) -> p b c", b=2), nd[:, :, :, DM]))
                then(dve.scalar_tensor_tensor(out=d1, in0=d0, scalar=-1.0, in1=d0, op0=ALU.mult, op1=ALU.max))
                then(dve.tensor_tensor(d1, d1, colsb[:, 1, :, 32 * dr + h], ALU.max))
                then(dve.reciprocal(d0, d1))
                at = slice(512 + h * DM, 512 + (h + 1) * DM)
                for b_ in range(2):
                    dst = mix[:, 2 * b_:2 * b_ + 2, at]
                    tmp = stage[:, 0, b_ * 256:(b_ + 1) * 256].rearrange("p (c e) -> p c e", c=2)
                    ins = dve.tensor_tensor(dst if dr == 0 else tmp, nd[:, b_, :, 0:DM],
                                            bc(d0[:, 2 * b_:2 * b_ + 2], DM), ALU.mult)
                    if dr == 0:
                        if b_ == 1:
                            ins.then_inc(hsum_done, 1)
                    else:
                        then(ins)
                        ins = dve.tensor_tensor(dst, dst, tmp, ALU.add)
                        if b_ == 1:
                            ins.then_inc(hsum_done, 1)

            masked_m(0)
            for r in range(8):
                if r < 7:
                    masked_m(r + 1)
                weigh(r)
                if r >= 1:
                    head_sum(r - 1)
            head_sum(7)
            for a in range(NT + 1):
                if a < NT:
                    dve.wait_ge(msq_done, a + 1)
                    at = 16 + 4 * a
                    dve.tensor_reduce(hss[:, at:at + 4], stage[:, a % 2, 0:512].rearrange("p (h e) -> p h e", h=4),
                                      AX.X, ALU.add).then_inc(mss_done, 1)
                if a >= 1:
                    i = a - 1
                    at = 16 + 4 * i
                    dve.wait_ge(mstd_done, i + 1)
                    then(dve.reciprocal(hrs[:, at:at + 4], hstd[:, at:at + 4]))
                    mv = mix[:, i, 512:1024].rearrange("p (h e) -> p h e", h=4)
                    dve.tensor_tensor(mv, mv, bc(hrs[:, at:at + 4], DM), ALU.mult).then_inc(mnorm_done, 1)
            dve.wait_ge(sig_done, 4)
            for i in range(NT):
                take_turned(T_BR, i)
            for half in range(2):
                for j in range(4):
                    bo = 4 * half + j
                    dve.wait_ge(y_done, 16 + bo + 1)
                    dve.wait_ge(gate_sig, 8 * half + 4 + j + 1)
                    a_, b_ = merged[:, bo, :], stage[:, 0, (j % 2) * 512:(j % 2) * 512 + 512]
                    dve.tensor_tensor(a_, gates[:, 0, j, :], ps[:, (2 * bo) % 4, :], ALU.mult)
                    then(dve.tensor_tensor(b_, gates[:, 1, j, :], ps[:, (2 * bo + 1) % 4, :], ALU.mult))
                    dve.tensor_tensor(a_, a_, b_, ALU.add).then_inc(u_done, 1)
            for half in range(2):
                for i in range(NT):
                    dve.wait_ge(y_done, 24 + 4 * half + i + 1)
                    at = x[:, i, half * 512:(half + 1) * 512]
                    dve.tensor_tensor(at, at, ps[:, 2 * i + half, :], ALU.add).then_inc(x_ready, 1)
            dve.wait_ge(gb_load, 48)
            norm(T_N2)
            dve.wait_ge(logits_done, 1)
            nall = NG + NE
            then(dve.tensor_tensor(lg[:, :, :], ps[:, 4, 0:NT * nall].rearrange("p (i c) -> p i c", i=NT),
                                   br[:, :].unsqueeze(1).broadcast_to([P, NT, nall]), ALU.add))
            gl = lg[:, :, 0:NG]
            el = lg[:, :, NG:nall].rearrange("p i (g e) -> p i e g", g=NG)

            def first_best(vals, n, out_max, eq, low, out_hot):
                then(dve.tensor_reduce(out_max, vals, AX.X, ALU.max))
                then(dve.tensor_tensor(eq, vals, bc(out_max, n), ALU.is_equal))
                place = r_place[:, 0:n].unsqueeze(1).broadcast_to([P, NT, n])
                then(dve.tensor_tensor(eq, eq, place, ALU.mult))
                then(dve.tensor_reduce(low, eq, AX.X, ALU.min))
                then(dve.tensor_tensor(out_hot, bc(low, n), place, ALU.is_equal))

            then(dve.tensor_scalar(r_place, iot[:, 0:8], -64.0, None, ALU.add))
            first_best(gl, NG, r_gm, r_eq4, r_low, r_hg)
            dve.tensor_tensor(r_gd, gl, bc(r_gm, NG), ALU.subtract).then_inc(r_exp, 1)
            then(dve.tensor_tensor(r_sel, el, r_hg.unsqueeze(2).broadcast_to([P, NT, EPG, NG]), ALU.mult))
            then(dve.tensor_reduce(r_e, r_sel, AX.X, ALU.add))
            first_best(r_e, EPG, r_v1, r_eq8, r_low, r_h1)
            then(dve.scalar_tensor_tensor(out=r_e2, in0=r_h1, scalar=LOWEST, in1=r_e, op0=ALU.mult, op1=ALU.add))
            first_best(r_e2, EPG, r_v2, r_eq8, r_low, r_h2)
            dve.wait_ge(r_exp_done, 1)
            dve.tensor_tensor(r_dv, r_v2, r_v1, ALU.subtract).then_inc(r_exp, 1)
            for c, hot in enumerate((r_h1, r_h2)):
                ins = dve.tensor_tensor(msel[:, c, :, :].rearrange("p i (g e) -> p i g e", g=NG),
                                        r_hg.unsqueeze(3).broadcast_to([P, NT, NG, EPG]),
                                        hot.unsqueeze(2).broadcast_to([P, NT, NG, EPG]), ALU.mult)
            then(ins)
            dve.tensor_tensor(msel[:, 2, :, :], msel[:, 0, :, :], msel[:, 1, :, :], ALU.add).then_inc(sel_ready, 1)
            dve.wait_ge(r_exp_done, 2)
            then(dve.tensor_reduce(r_gm, r_ge, AX.X, ALU.add))
            then(dve.reciprocal(r_gm, r_gm))
            then(dve.tensor_scalar(r_low, r_x2, 1.0, None, ALU.add))
            then(dve.reciprocal(r_low, r_low))
            then(dve.tensor_tensor(wpos[:, 0, :], r_low, r_gm, ALU.mult))
            then(dve.tensor_tensor(wpos[:, 1, :], wpos[:, 0, :], r_x2, ALU.mult))
            dve.wait_ge(rank_done, 1)
            cnt = ps[:, 5, NT * NE:(NT + 1) * NE]
            then(dve.tensor_scalar(r_ov, cnt, float(BLK), None, ALU.is_gt))
            for k in range(2, NBLK):
                then(dve.tensor_scalar(r_t, cnt, float(k * BLK), None, ALU.is_gt))
                then(dve.tensor_tensor(r_ov, r_ov, r_t, ALU.add))
            then(dve.tensor_tensor_scan(r_cum, allone[:, 0:NE], r_ov, 0.0, ALU.mult, ALU.add))
            then(dve.tensor_tensor(r_ov, r_cum, r_ov, ALU.subtract))
            then(dve.tensor_tensor(r_ov, r_ov, iot[:, 0:NE], ALU.subtract))
            then(dve.tensor_scalar(r_ov, r_ov, float(NE - 1), float(BLK), ALU.add, ALU.mult))
            then(dve.tensor_scalar(r_off, iot[:, 0:NE], float(BLK), None, ALU.mult))
            ranks = ps[:, 5, 0:NT * NE].rearrange("p (i e) -> p i e", i=NT)
            over = msel[:, 2, :, :]
            then(dve.tensor_scalar(over, ranks, float(BLK), None, ALU.is_ge))
            then(dve.tensor_tensor(over, over, r_ov.unsqueeze(1).broadcast_to([P, NT, NE]), ALU.mult))
            then(dve.tensor_tensor(r_rank, ranks, r_off.unsqueeze(1).broadcast_to([P, NT, NE]), ALU.add))
            then(dve.tensor_tensor(r_rank, r_rank, over, ALU.add))
            for c in range(2):
                then(dve.tensor_tensor(r_row, msel[:, c, :, :], r_rank, ALU.mult))
                then(dve.tensor_reduce(r_low, r_row, AX.X, ALU.add))
                ins = dve.tensor_copy(ipos[:, c, :], r_low)
                if c == 0:
                    then(ins)
            ins.then_inc(pos_ready, 1)
            then(dve.tensor_copy(njobs[:, :], r_cum[0:1, NE - 1:NE]))
            then(dve.tensor_tensor(j_le, r_cum[0:1, :].unsqueeze(1).broadcast_to([1, MAXJOBS, NE]),
                                   bc(iot[0:1, 0:MAXJOBS], NE), ALU.is_le))
            then(dve.tensor_reduce(j_ex, j_le, AX.X, ALU.add))
            then(dve.tensor_scalar(j_ex, j_ex, float(NE - 1), None, ALU.min))
            then(dve.tensor_copy(jobs[:, :], j_ex))
            dve.sem_inc(job_ready, 1)
            dve.wait_ge(idT_done, 1)
            dve.tensor_copy(idsT[:, :], ps[0:BLK, 6, 0:BLOCKS]).then_inc(ids_ready, 1)
            def turned_tokens(s, wait, value, ready):
                dve.wait_ge(wait, value)
                for half in range(2):
                    ins = dve.tensor_copy(xsT[:, s, 4 * half:4 * half + 4, :],
                                          ps[:, half, 0:4 * BLK].rearrange("p (k t) -> p k t", k=4))
                ins.then_inc(ready, 1)

            def hidden(s, wait, value, ready):
                dve.wait_ge(wait, value)
                dve.tensor_tensor(hTe[:, s, :, :].rearrange("p k t -> p (k t)"), sg[:, s, :, :].rearrange("p k t -> p (k t)"),
                                  ps[:, 3, 0:4 * BLK], ALU.mult).then_inc(ready, 1)

            turned_tokens(0, xt_done, 1, xT_ready)
            with dve.Fori(0, NE // 2 - 1) as it:
                for s in range(2):
                    e = it * 2 + s
                    hidden(s, silu_done, e + 1, hte_ready)
                    turned_tokens(1 - s, xt_done, e + 2, xT_ready)
            hidden(0, silu_done, NE - 1, hte_ready)
            turned_tokens(1, xt_done, NE, xT_ready)
            hidden(1, silu_done, NE, hte_ready)
            n = dve.value_load(njobs[0:1, 0:1], min_val=0, max_val=MAXJOBS)
            with dve.If(n > 0):
                with dve.Fori(0, n) as j:
                    turned_tokens(0, ov["xt"], j + 1, ov["xT"])
                    hidden(0, ov["silu"], j + 1, ov["hte"])
            for c in range(2):
                for i in range(NT):
                    dve.wait_ge(y_gather[i], 16 * (c + 1))
                    dve.scalar_tensor_tensor(out=x[:, i, :], in0=yg[:, i, :], scalar=wpos[:, c, i:i + 1],
                                             in1=x[:, i, :], op0=ALU.mult, op1=ALU.add).then_inc(add_done, 1)


_INS = ["x", "w_in", "w_out", "w_up", "w_down", "g_pre_mix", "g_post_mix", "g_pre_mlp", "g_post_mlp",
        "g_diff_sub", "lambda_q1", "lambda_k1", "lambda_q2", "lambda_k2", "norm1_g_2", "w_in_2",
        "attn_q_gain_2", "attn_k_gain_2", "attn_sink_2", "rel_bias_table_2", "mlstm_conv_w_2",
        "mlstm_conv_b_2", "mlstm_gate_b_2", "mlstm_out_gain_2", "w_branch_attn_2", "w_branch_mlstm_2",
        "merge_b_2", "w_out_2", "norm2_g_2", "w_router_group_2", "b_router_group_2",
        "w_router_expert_2", "b_router_expert_2", "w_expert_gate_2", "w_expert_up_2", "w_expert_down_2"]


def shape_constants():
    inv = (1.0 / (np.float32(10000.0) ** (np.arange(0, HD, 2, dtype=np.float32) / np.float32(HD)))).astype(np.float32)
    ang = (np.arange(SEQ, dtype=np.float32)[None, :] * inv[:, None]).astype(np.float32)
    cos, sin = np.cos(ang), np.sin(ang)
    rel = np.arange(512) - 255
    n = np.abs(rel)
    nf = np.maximum(n, 1).astype(np.float32)
    large = 8 + (np.log(nf / 8) / np.float32(math.log(128 / 8)) * np.float32(8)).astype(np.int32)
    bucket = np.where(rel > 0, 16, 0) + np.where(n < 8, n, np.minimum(large, 15))
    onehot = (np.arange(32)[:, None] == bucket[None, :]).astype(np.float32)
    window = np.where(np.abs(rel) <= 128, 0.0, NEG).astype(np.float32)
    return {"rope_cos": np.concatenate([cos] * 4).astype(np.float32),
            "rope_sin": np.concatenate([-sin, sin] * 2).astype(np.float32),
            "bucket_onehot": onehot, "window_mask": np.repeat(window[None, :], 8, axis=0)}


def kernel(**inputs):
    import concourse.bacc as _bacc
    from concourse.bass_utils import run_bass_kernel_spmd as _run

    nc = _bacc.Bacc("TRN2", target_bir_lowering=False, num_devices=1)
    arrays, io = {}, {}
    given = {name: np.ascontiguousarray(inputs[name]) for name in _INS}
    for name, a in {**given, **shape_constants()}.items():
        arrays[f"in_{name}"] = a
        io[name] = nc.dram_tensor(f"in_{name}", a.shape, mybir.dt.from_np(a.dtype), kind="ExternalInput").ap()
    out = nc.dram_tensor("out_x", (1, SEQ, D), F32, kind="ExternalOutput").ap()
    build(nc, io, out)
    r = _run(nc, [arrays], core_ids=[0])
    return r.results[0]["out_x"]
```

```python
import math
from contextlib import ExitStack

import numpy as np

import concourse.bass as bass
from concourse import mybir

F32 = mybir.dt.float32
I32 = mybir.dt.int32
ALU = mybir.AluOpType
ACT = mybir.ActivationFunctionType
AX = mybir.AxisListType

P = 128
D = 1024
SEQ = 512
NT = SEQ // P
KT = D // P
HD = 64
D_FF = 4 * D
FT = D_FF // P
EPS = 1e-6
NEG = -1e30
LOWEST = -3.0e38
TAKEN = -3.4e38
TOPK = 128
IDX_SCALE = (8 ** -0.5) * (64 ** -0.5)
LAM_INIT = 0.8 - 0.6 * math.exp(-0.3 * 0)
CONV = 5
DM = 128
MROWS = 36
NE, NG, EPG = 32, 4, 8
BLK = 96
NBLK = -(-SEQ // BLK)
N_SMALL = 15
MAXJOBS = 2 * SEQ // BLK
BLOCKS = NE + MAXJOBS
ROWS = BLOCKS * BLK

QA, KA, VA, QI, KI, WI, QD, KD, VD = 0, 512, 1024, 1536, 2048, 2112, 2120, 2632, 3144
QA2, KVA2, QM, KM, VM, OM, GM, MG = 0, 512, 768, 1280, 1792, 2304, 2816, 2832


def build(nc, io, out):
    ctx = ExitStack()
    with ctx:
        def sb(name, shape, dt=F32):
            return ctx.enter_context(nc.sbuf_tensor(name, shape, dt))

        def sem(name):
            return ctx.enter_context(nc.semaphore(name))

        ps = ctx.enter_context(nc.psum_tensor("ps", [P, 8, 512], F32))
        W = sb("W", [P, 6 * 4096])
        ring = [W[:, s * 4096:(s + 1) * 4096] for s in range(2)]
        R = W[:, 2 * 4096:]
        expert_w = [[W[:, (3 * s + j) * 4096:(3 * s + j + 1) * 4096] for j in range(3)] for s in (1, 0)]
        x = sb("x", [P, NT, D])
        hT = sb("hT", [P, KT, SEQ])
        mix = sb("mix", [P, NT, D])
        yT = sb("yT", [P, KT, SEQ])
        cbuf = sb("cbuf", [P, 8 * 516])
        stage = sb("stage", [P, 2, D])
        smb = sb("smb", [P, 4, 512])
        ptb = sb("ptb", [P, 2, 512])
        gb = sb("gb", [P, D])
        ident = sb("ident", [P, P])
        cmask = sb("cmask", [P, 512])
        fmask = sb("fmask", [P, P])
        rope = yT[:, 0:2, :]
        ones = sb("ones", [P, P])
        gcol = sb("gcol", [P, 6, 8])
        small = sb("small", [P, 640])
        cur = [0]

        def col(n):
            a = cur[0]
            cur[0] += n
            assert cur[0] <= 640
            return small[:, a:a + n]

        ss, std, rstd = col(16), col(16), col(16)
        ssy, stdy, rsty = col(8), col(8), col(8)
        mx, nm, den, es = col(96), col(96), col(96), col(32)
        hss, hstd, hrs = col(32), col(32), col(32)
        lamv = col(8)
        epsc = col(1)
        m8 = col(8)
        wi = sb("wi", [P, NT, 8])
        lam_in = cbuf[:, 0:4 * HD].rearrange("p (n d) -> p n d", n=4)

        qiT = R[:, 0:2048].rearrange("p (c t) -> p c t", c=4)
        kiT = R[:, 2048:2560]
        qdT = R[:, 2560:4608].rearrange("p (c t) -> p c t", c=4)
        kdT = R[:, 4608:6656].rearrange("p (c t) -> p c t", c=4)
        qaT = R[:, 6656:8704].rearrange("p (c t) -> p c t", c=4)
        kaT = R[:, 8704:10752].rearrange("p (c t) -> p c t", c=4)
        vd = R[:, 10752:12800].rearrange("p (i c) -> p i c", i=NT)
        va = R[:, 12800:14848].rearrange("p (i c) -> p i c", i=NT)
        uT = R[:, 0:FT * 512].rearrange("p (f t) -> p f t", f=FT)
        idx_s = cbuf[:, 0:1536].rearrange("p (i t) -> p i t", i=3)
        dmask = cbuf[:, 1536:3072].rearrange("p (i t) -> p i t", i=3)
        rbuf = cbuf[:, 3072:4096].rearrange("p (s t) -> p s t", s=2)
        qkT = R[:, 0:4096].rearrange("p (c t) -> p c t", c=8)
        vext = R[:, 4096:6160].rearrange("p (i h e) -> p i h e", i=NT, h=4)
        sigT = R[:, 6160:8208].rearrange("p (c t) -> p c t", c=4)
        bias = R[:, 8208:11280].rearrange("p (h t) -> p h t", h=8)
        qT = R[:, 11280:13328].rearrange("p (c t) -> p c t", c=4)
        kdup = R[:, 13328:14352].rearrange("p (g t) -> p g t", g=2)
        va2 = R[:, 14352:14864].rearrange("p (i c) -> p i c", i=NT)
        E = R[:, 8208:12304].rearrange("p (s j t) -> p s j t", s=2, j=NT)
        nmd = R[:, 12304:13328].rearrange("p (s j t) -> p s j t", s=2, j=NT)
        convin = cbuf[:, :].rearrange("p (c t) -> p c t", c=8)
        merged = cbuf[:, 0:4096].rearrange("p (c t) -> p c t", c=8)
        gates = R[:, 0:4096].rearrange("p (b c t) -> p b c t", b=2, c=4)
        gw = [gb[:, a:b] for a, b in ((0, 64), (64, 352), (352, 448), (448, 736))]
        G = gw[0].rearrange("p (i c) -> p i c", i=NT)
        GL = gw[1].rearrange("p (q i r) -> p q i r", q=2, i=NT)
        lfw = gw[2].rearrange("p (q i c) -> p q i c", q=3, i=NT)
        rows = yT[0:MROWS, 0:4, :]
        one_row = yT[0:MROWS, 4, :]
        zero_row = yT[0:MROWS, 5, :]
        selr = yT[0:MROWS, 6:8, :].rearrange("p a (r m) -> p (a r) m", m=P)
        onehot = smb[0:NE, 0, :]
        wmask = smb[0:8, 1, :]
        bline = smb[0:8, 2, :]
        colsb = gw[3].rearrange("p (q i r) -> p q i r", q=2, i=NT)
        VECS = (("g_pre_mix", "(k p) -> k p"), ("g_pre_mlp", "(k p) -> k p"), ("norm1_g_2", "(k p) -> k p"),
                ("mlstm_out_gain_2", "h p -> h p"), ("g_diff_sub", "(k p) -> k p"), ("mlstm_conv_b_2", "(k p) -> k p"),
                ("merge_b_2", "(k p) -> k p"), ("mlstm_conv_w_2", "w (k p) -> (w k) p"))
        N_VECS = 3 * KT + 4 + 1 + 8 + 16 + 8 * CONV
        vec_rows = mix[0:N_VECS, 1, 0:P]
        mden = sb("mden", [P, 4, 4])
        convw = sb("convw", [P, 8, CONV])
        convb = sb("convb", [P, 8])
        gateb = sb("gateb", [P, 16])
        sink = sb("sink", [P, 8])
        gqk = sb("gqk", [P, 2])
        mergeb = sb("mergeb", [P, 16])
        btab = sb("btab", [NE, 8])
        yTw = yT[:, :, :].rearrange("p a b -> p (a b)")
        late = 32 * BLK
        wr = smb[:, 0, 0:KT * (NG + NE)].rearrange("p (k e) -> p k e", k=KT)
        ltri = yTw[:, late:late + P]
        allone = yTw[:, late + P:late + 2 * P]
        br = sb("br", [P, NG + NE])
        lg = cbuf[:, 0:NT * (NG + NE)].rearrange("p (i c) -> p i c", i=NT)
        msel = cbuf[:, 256:256 + 3 * NT * NE].rearrange("p (q i e) -> p q i e", q=3, i=NT)
        both_rows = cbuf[:, 256 + 2 * NT * NE:256 + 3 * NT * NE]
        wpos = sb("wpos", [P, 2, NT])
        ipos = sb("ipos", [P, 2, NT], I32)
        tokid = sb("tokid", [P, NT])
        iot = sb("iot", [P, P])
        idsT = cbuf[0:BLK, 1024:1024 + BLOCKS].bitcast(I32)
        idcol = sb("idcol", [BLK, 3], I32)
        jobs = sb("jobs", [1, MAXJOBS], I32)
        njobs = sb("njobs", [1, 1], I32)
        iti = mix[:, 0, 0:P].bitcast(I32)
        rtw = ptb[:, :, :].rearrange("p a b -> p (a b)")
        rcur = [0]

        def work(*shape):
            n = int(np.prod(shape))
            a = rcur[0]
            rcur[0] += n
            assert rcur[0] <= 1024
            v = rtw[:, a:a + n]
            names = "abc"[:len(shape)]
            if len(shape) == 1:
                return v
            return v.rearrange(f"p ({' '.join(names)}) -> p {' '.join(names)}", **dict(zip(names, shape)))

        r_place = work(8)
        r_gm, r_low, r_v1, r_v2, r_dv, r_x2 = (work(NT) for _ in range(6))
        r_gd, r_ge, r_eq4, r_hg = (work(NT, NG) for _ in range(4))
        r_e, r_e2, r_eq8, r_h1, r_h2 = (work(NT, EPG) for _ in range(5))
        r_sel = work(NT, EPG, NG)
        r_rank, r_row = work(NT, NE), work(NT, NE)
        r_ov, r_cum, block_start = work(NE), work(NE), work(BLOCKS)
        more = cbuf[:, 1088:1088 + NE * (NBLK - 1)].rearrange("p (e k) -> p e k", e=NE)
        j_ex = smb[0:1, 3, 0:MAXJOBS]
        r_rows = work(2, NT)
        r_blk = work(2 * NT)
        place_hot = cbuf[:, 1280:1280 + 2 * NT * BLK].rearrange("p (n r) -> p n r", n=2 * NT)
        block_tok, from_block = (cbuf[:, a:a + 2 * NT * BLOCKS].rearrange("p (n b) -> p n b", n=2 * NT)
                                 for a in (1280 + 2 * NT * P, 1280 + 2 * NT * (P + BLOCKS)))
        j_le = smb[0:1, 2, 0:MAXJOBS * NE].rearrange("p (j e) -> p j e", e=NE)
        xs = mix[:, 0:2, :]
        ys = mix[:, 2:4, :]
        xsT = yTw[:, 0:16 * BLK].rearrange("p (s k t) -> p s k t", s=2, k=KT)
        hTe = yTw[:, 16 * BLK:24 * BLK].rearrange("p (s k t) -> p s k t", s=2, k=4)
        sg = yTw[:, 24 * BLK:32 * BLK].rearrange("p (s k t) -> p s k t", s=2, k=4)
        yg = [hT[:, :, :].rearrange("p (a c) t -> p a (c t)", a=4), expert_w[0][0].rearrange("p (a c) -> p a c", a=4)]

        h_dram = nc.dram_tensor("h_scratch", (SEQ, D), F32, kind="Internal").ap()
        y_dram = nc.dram_tensor("y_scratch", (ROWS, D), F32, kind="Internal").ap()
        l_dram = nc.dram_tensor("bias_scratch", (8, P, 512), F32, kind="Internal").ap()

        w1, w2 = io["w_in"][0], io["w_in_2"][0]

        def cols_of(w, a, n):
            return w[:, a:a + n].rearrange("(k p) c -> p k c", p=P)

        chunks = [cols_of(w1, a, n) for a, n in
                  ((QI, 512), (KI, 72), (QD, 512), (KD, 512), (VD, 512), (QA, 512), (KA, 512), (VA, 512))]
        C_WO = len(chunks)
        chunks += [cols_of(io["w_out"][0], 512 * h, 512) for h in range(2)]
        C_UP = len(chunks)
        C_DOWN = C_UP + 8
        C_P2 = C_DOWN + 8
        chunks2 = [cols_of(w2, a, n) for a, n in
                   ((QM, 512), (KM, 512), (VM, 512), (QA2, 512), (KVA2, 256), (OM, 512))]
        C_MERGE = C_P2 + len(chunks2)
        C_WO2 = C_MERGE + 6

        def ring_view(c, k, n):
            return ring[c % 2][:, 0:k * n].rearrange("p (k n) -> p k n", k=k)

        def gates_view(c):
            return ring[c % 2][:, KT * 256:KT * 272].rearrange("p (k n) -> p k n", k=KT)

        const_ready = sem("const_ready")
        zero_ready = sem("zero_ready")
        x_load = [sem(f"x_load{i}") for i in range(NT)]
        small_load = sem("small_load")
        gb_load = sem("gb_load")
        gain_load, vecs_done, vecs_taken = sem("gain_load"), sem("vecs_done"), sem("vecs_taken")
        ring_load = [sem(f"ring_load{s}") for s in range(2)]
        branch_load, gates_load = sem("branch_load"), sem("gates_load")
        down_used = sem("down_used")
        dv = sem("dv")
        ac = sem("ac")
        sumsq_done, std_done = sem("sumsq_done"), sem("std_done")
        turn_src, turn_done, turn_evac = sem("turn_src"), sem("turn_done"), sem("turn_evac")
        proj_done = sem("proj_done")
        swap_done, rope_done = sem("swap_done"), sem("rope_done")
        val_done, wi_done, ki_dup = sem("val_done"), sem("wi_done"), sem("ki_dup")
        idx_done, relu_done, comb_done = sem("idx_done"), sem("relu_done"), sem("comb_done")
        lam_dot, lam_exp = sem("lam_dot"), sem("lam_exp")
        score_done, masked, negmax = sem("score_done"), sem("masked"), sem("negmax")
        exp_done, diff_done = sem("exp_done"), sem("diff_done")
        probT_done, pt_ready, pv_done = sem("probT_done"), sem("pt_ready"), sem("pv_done")
        o_sq, o_ss, o_std, o_evac = sem("o_sq"), sem("o_ss"), sem("o_std"), sem("o_evac")
        y_done, x_ready = sem("y_done"), sem("x_ready")
        ysumsq, ystd = sem("ysumsq"), sem("ystd")
        up_done, up_relu, up_free = sem("up_done"), sem("up_relu"), sem("up_free")
        gates_raw, gate_abs, gate_rows = sem("gates_raw"), sem("gate_abs"), sem("gate_rows")
        conv_in, conv_done, qk_ready = sem("conv_in"), sem("conv_done"), sem("qk_ready")
        vone_done = sem("vone_done")
        vext_done, va2_done, sig_done = sem("vext_done"), sem("va2_done"), sem("sig_done")
        sq_done, ssb_done, hstd_done, qkn_done, kdup_done = (
            sem("sq_done"), sem("ssb_done"), sem("hstd_done"), sem("qkn_done"), sem("kdup_done"))
        btab_done, bline_ready, bline_store, bias_load = (
            sem("btab_done"), sem("bline_ready"), sem("bline_store"), sem("bias_load"))
        onehot_load = sem("onehot_load")
        grow_done, grow_evac, scan_done, gcol_done, acol_ready, em_ready = (
            sem("grow_done"), sem("grow_evac"), sem("scan_done"), sem("gcol_done"), sem("acol_ready"),
            sem("em_ready"))
        mb_done, nmd_done, wexp_done, qk_done, sw_done, num_done, hsum_done = (
            sem("mb_done"), sem("nmd_done"), sem("wexp_done"), sem("qk_done"), sem("sw_done"),
            sem("num_done"), sem("hsum_done"))
        msq_done, mss_done, mstd_done, mnorm_done = sem("msq_done"), sem("mss_done"), sem("mstd_done"), sem("mnorm_done")
        gate_done, gate_sig, u_done = sem("gate_done"), sem("gate_sig"), sem("u_done")
        logits_done, r_exp, r_exp_done = sem("logits_done"), sem("r_exp"), sem("r_exp_done")
        h_store = [sem(f"h_store{s}") for s in range(2)]
        sel_ready, rank_done, slots_ready, y_zero = (
            sem("sel_ready"), sem("rank_done"), sem("slots_ready"), sem("y_zero"))
        wr_load, masks_ready = sem("wr_load"), sem("masks_ready")
        fetches = sem("fetches")
        idT_done, ids_ready, job_ready = sem("idT_done"), sem("ids_ready"), sem("job_ready")
        wg_load = [sem(f"wg_load{s}") for s in range(2)]
        wu_load = [sem(f"wu_load{s}") for s in range(2)]
        wd_load = [sem(f"wd_load{s}") for s in range(2)]
        gather = [sem(f"gather{s}") for s in range(2)]
        y_store = [sem(f"y_store{s}") for s in range(2)]
        idcol_ready, xt_done, xT_ready, gu_done, silu_done, hte_ready, down_done, ys_ready = (
            sem("idcol_ready"), sem("xt_done"), sem("xT_ready"), sem("gu_done"), sem("silu_done"),
            sem("hte_ready"), sem("down_done"), sem("ys_ready"))
        ov = {n: sem(f"over_{n}") for n in
              ("wg", "wu", "wd", "id", "gather", "xt", "xT", "gu", "silu", "hte", "down", "ys", "store", "free")}
        y_gather = [[sem(f"y_gather{c}_{i}") for i in range(NT)] for c in range(2)]
        add_done, out_store = sem("add_done"), sem("out_store")

        G1 = [("rope", 0, c, qiT[:, c, :]) for c in range(4)]
        G1 += [("ki", 1, 0, kiT), ("wi", 1, 0, None)]
        N_IDX_FROM = len(G1)
        for chunk, dst in ((2, qdT), (3, kdT)):
            G1 += [("rope", chunk, c, dst[:, c, :]) for c in range(4)]
        G1 += [("val", 4, i, vd[:, i, :]) for i in range(NT)]
        for chunk, dst in ((5, qaT), (6, kaT)):
            G1 += [("rope", chunk, c, dst[:, c, :]) for c in range(4)]
        G1 += [("val", 7, i, va[:, i, :]) for i in range(NT)]
        b = C_P2
        G2 = [("conv", b, c) for c in range(4)] + [("conv", b + 1, c) for c in range(4)]
        G2 += [("vm", b + 2, i) for i in range(NT)]
        G2 += [("qnorm", b + 3, c) for c in range(4)]
        C_GATES = b + 4
        G2 += [("gates", b + 4, 0), ("knorm", b + 4, 0), ("va2", b + 4, 0)]
        G2 += [("om", b + 5, c) for c in range(4)]
        IDX = [(i, h) for i in range(1, NT) for h in range(8)]

        def idx_part(g):
            n = 3 * (g - N_IDX_FROM)
            return list(enumerate(IDX))[n:n + 3] if n >= 0 else []

        IDX_END = N_IDX_FROM + len(IDX) // 3

        units = []
        for i in range(NT):
            w = (i + 1) * P
            cm = cmask[:, 512 - w:512]
            diffs, topks = [], []
            for h in range(4):
                maps = [(qdT[64 * c:64 * c + 64, h, i * P:(i + 1) * P], kdT[64 * c:64 * c + 64, h, 0:w], cm)
                        for c in range(2)]
                diffs.append(dict(maps=maps, w=w, k0=0, v=vd, vc=(h * P, (h + 1) * P), oc=(h * P, (h + 1) * P),
                                  kind="diff", tile=i, h=h, g=2 * i, dc=16 * i + 2 * h, last=h == 3, scale=HD ** -0.5))
            for h in range(8):
                r = 64 * (h % 2)
                m = cm if i == 0 else dmask[:, i - 1, 0:w]
                topks.append(dict(maps=[(qaT[r:r + 64, h // 2, i * P:(i + 1) * P], kaT[r:r + 64, h // 2, 0:w], m)],
                                  w=w, k0=0, v=va, vc=(h * HD, (h + 1) * HD), oc=(h * HD, (h + 1) * HD), g=2 * i + 1,
                                  kind="topk", tile=i, h=h, dc=16 * i + 8 + h, last=h == 7, scale=HD ** -0.5))
            for h in range(4):
                units += [diffs[h], topks[h]]
            units += topks[4:]
        N_UNITS1 = len(units)
        for n in range(NT):
            lo, hi = max(0, n - 1), min(NT, n + 2)
            for h in range(8):
                r, off = 64 * (h % 2), (lo - n + 1) * P
                w = (hi - lo) * P
                kv = h // 4
                units.append(dict(maps=[(qT[r:r + 64, h // 2, n * P:(n + 1) * P], kdup[r:r + 64, kv, lo * P:hi * P],
                                         bias[:, h, off:off + w])],
                                  w=w, k0=lo, v=va2, vc=(kv * HD, (kv + 1) * HD), oc=(h * HD, (h + 1) * HD),
                                  kind="window", tile=n, h=h, g=2 * NT + n, dc=16 * NT + 8 * n + h, last=h == 7,
                                  scale=1.0))
        m = d = 0
        map_unit = []
        for u, un in enumerate(units):
            un["u"], un["m"] = u, m
            m += len(un["maps"])
            map_unit += [u] * len(un["maps"])
            d += un["kind"] == "diff"
            un["d"] = d
        ALL1 = range(0, N_UNITS1)
        ALL2 = range(N_UNITS1, len(units))
        M1 = units[N_UNITS1]["m"]
        MAPS = m

        chunk_done = {}
        for g, it_ in enumerate(G1 + G2):
            chunk_done[it_[1]] = (proj_done, g + 1)
        for half in range(2):
            chunk_done[C_WO + half] = (y_done, 4 * (half + 1))
            for q in range(4):
                chunk_done[C_DOWN + 4 * half + q] = ((down_used, 3 * half + q + 1) if q < 3 else
                                                     (y_done, 8 + 4 * (half + 1)))
            for br_ in range(2):
                chunk_done[C_MERGE + 3 * half + br_] = (proj_done, len(G1) + len(G2) + 8 * half + 4 * (br_ + 1))
            chunk_done[C_MERGE + 3 * half + 2] = (y_done, 16 + 4 * (half + 1))
            chunk_done[C_WO2 + half] = (y_done, 24 + 4 * (half + 1))
        for q in range(8):
            chunk_done[C_UP + q] = (up_done, 4 * (q + 1))

        T_PRE, T_MIX, T_MLP, T_N1, T_BR, T_N2 = range(6)
        NORM = {T_PRE: 0, T_MLP: 1, T_N1: 2, T_N2: 3}

        block = ctx.enter_context(nc.Block())

        @block.sync
        def _(sp):
            for i in range(NT):
                sp.dma_start(x[:, i, :], io["x"][0, i * P:(i + 1) * P, :]).then_inc(x_load[i], 16)

            def load(c, src):
                if c >= 2:
                    sp.wait_ge(*chunk_done[c - 2])
                k, n = src.shape[1], src.shape[2]
                sp.dma_start(ring_view(c, k, n), src).then_inc(ring_load[c % 2], 16)

            def up_cols(at):
                return io["w_up"][0][:, at].rearrange("(k p) c -> p k c", p=P)

            row = 0
            for name, pattern in VECS:
                src = io[name][0].rearrange(pattern, p=P)
                sp.dma_start(vec_rows[row:row + src.shape[0], :], src).then_inc(gain_load, 16)
                row += src.shape[0]
            assert row == N_VECS
            for c in range(2):
                load(c, chunks[c])
            def bcast(src):
                return src.partition_broadcast(P)

            smalls = []

            def small_in(dst, src):
                smalls.append(dst)
                sp.dma_start(dst, src, allow_slow_non_contiguous=True).then_inc(small_load, 16)

            for n, name in enumerate(("lambda_q1", "lambda_k1", "lambda_q2", "lambda_k2")):
                small_in(lam_in[:, n, :], bcast(io[name][0]))
            small_in(rope[:, 0, :], io["rope_cos"])
            small_in(rope[:, 1, :], io["rope_sin"])
            small_in(gateb[:, :], bcast(io["mlstm_gate_b_2"][0].rearrange("a b c -> (a b c)")))
            small_in(sink[:, :], bcast(io["attn_sink_2"][0]))
            for h in range(2):
                small_in(gqk[64 * h:64 * h + 64, 0:1], io["attn_q_gain_2"][0].rearrange("(p o) -> p o", o=1))
                small_in(gqk[64 * h:64 * h + 64, 1:2], io["attn_k_gain_2"][0].rearrange("(p o) -> p o", o=1))
            small_in(btab[:, :], io["rel_bias_table_2"])
            small_in(br[:, 0:NG], bcast(io["b_router_group_2"][0]))
            small_in(br[:, NG:NG + NE], bcast(io["b_router_expert_2"][0]))

            assert len(smalls) == N_SMALL, len(smalls)

            for c in range(2, C_UP):
                load(c, chunks[c])
            for n in range(2):
                load(C_UP + n, up_cols(slice(n * 512, (n + 1) * 512)))
            with sp.Fori(0, 3) as it:
                for s in range(2):
                    sp.wait_ge(up_done, it * 8 + 4 * (s + 1))
                    sp.dma_start(ring_view(s, KT, 512), up_cols(bass.ds(it * 1024 + (2 + s) * 512, 512))
                                 ).then_inc(ring_load[s], 16)
            for n in range(8):
                half, q = n // 4, n % 4
                load(C_DOWN + n, io["w_down"][0][q * 1024:(q + 1) * 1024, half * 512:(half + 1) * 512]
                     .rearrange("(k p) c -> p k c", p=P))
            for n, src in enumerate(chunks2):
                load(C_P2 + n, src)
                if C_P2 + n == C_GATES:
                    sp.dma_start(gates_view(C_GATES), cols_of(w2, GM, 16)).then_inc(gates_load, 16)
            for half in range(2):
                c = C_MERGE + 3 * half
                load(c, cols_of(w2, MG + 512 * half, 512))
                load(c + 1, cols_of(w2, MG + D + 512 * half, 512))
                c += 2
                sp.wait_ge(*chunk_done[c - 2])
                for j, (name, sm) in enumerate((("w_branch_attn_2", ring_load[c % 2]), ("w_branch_mlstm_2", branch_load))):
                    sp.dma_start(ring[c % 2][:, j * 2048:(j + 1) * 2048].rearrange("p (k n) -> p k n", k=4),
                                 io[name][0][:, half * 512:(half + 1) * 512].rearrange("(k p) c -> p k c", p=P)
                                 ).then_inc(sm, 16)
            for half in range(2):
                load(C_WO2 + half, cols_of(io["w_out_2"][0], 512 * half, 512))
            names = ("w_expert_gate_2", "w_expert_up_2", "w_expert_down_2")
            views = [[expert_w[s][j].rearrange("p (k n) -> p k n", k=k) for j, k in enumerate((8, 8, 4))] for s in range(2)]
            source = [io[nm_].rearrange("l e (k p) n -> (l e) p k n", p=P) for nm_ in names]
            loads = (wg_load, wu_load, wd_load)
            sp.wait_ge(turn_evac, 40)
            for j in range(3):
                sp.dma_start(views[0][j], source[j][0]).then_inc(loads[j][0], 16)
            slot_free = {c % 2: chunk_done[c] for c in (C_WO2, C_WO2 + 1)}
            first = C_WO2 % 2
            for j in (2, first, 1 - first):
                sp.wait_ge(*(slot_free[j] if j < 2 else (u_done, 8)))
                if j == 1 - first:
                    sp.wait_ge(turn_evac, 48)
                sp.dma_start(views[1][j], source[j][1]).then_inc(loads[j][1], 16)
            with sp.Fori(0, NE // 2 - 1) as it:
                for s in range(2):
                    e = it * 2 + (2 + s)
                    for j, used in enumerate((gate_done, gu_done, down_done)):
                        sp.wait_ge(used, it * 2 + (s + 1))
                        sp.dma_start(views[s][j], source[j][e]).then_inc(loads[j][s], 16)
            sp.wait_ge(job_ready, 1)
            sp.wait_ge(down_done, NE)
            n = sp.value_load(njobs[0:1, 0:1], min_val=0, max_val=MAXJOBS)
            with sp.If(n > 0):
                with sp.Fori(0, n) as j:
                    ex = sp.value_load(jobs[0:1, bass.ds(j, 1)], min_val=0, max_val=NE - 1)
                    sp.wait_ge(ov["free"], j + 1)
                    for q, nm_ in enumerate(("wg", "wu", "wd")):
                        sp.dma_start(views[0][q], source[q][ex]).then_inc(ov[nm_], 16)
            for i in range(NT):
                sp.wait_ge(add_done, NT + i + 1)
                sp.dma_start(out[0, i * P:(i + 1) * P, :], x[:, i, :]).then_inc(out_store, 16)
            sp.wait_ge(out_store, 16 * NT)

        @block.gpsimd
        def _(pool):
            step = [0]

            def then(ins):
                step[0] += 1
                ins.then_inc(zero_ready, 1)
                pool.wait_ge(zero_ready, step[0])

            for t, v in ((ident, 0.0), (cmask, 0.0), (fmask, 0.0), (ones, 0.0)):
                then(pool.memset(t[:, :], v))
            then(pool.affine_select(out=ident[:, :], in_=ident[:, :], compare_op=ALU.not_equal, fill=1.0,
                                    base=0, pattern=[[-1, P]], channel_multiplier=1))
            then(pool.affine_select(out=cmask[:, 384:512], in_=cmask[:, 384:512], compare_op=ALU.is_ge, fill=NEG,
                                    base=0, pattern=[[-1, P]], channel_multiplier=1))
            then(pool.affine_select(out=fmask[:, :], in_=fmask[:, :], compare_op=ALU.is_ge, fill=NEG,
                                    base=0, pattern=[[1, P]], channel_multiplier=-1))
            for r in range(2):
                then(pool.memset(ones[64 * r:64 * r + 64, 64 * r:64 * r + 64], 1.0))
            then(pool.iota(iti[:, :], pattern=[[1, P]], base=0, channel_multiplier=0))
            then(pool.tensor_copy(iot[:, :], iti[:, :]))
            then(pool.iota(iti[:, 0:NT], pattern=[[P, NT]], base=0, channel_multiplier=1))
            then(pool.tensor_copy(tokid[:, :], iti[:, 0:NT]))
            pool.memset(gcol[:, 1, 0:4], 1.0).then_inc(const_ready, 1)
            pool.wait_ge(turn_evac, 8)
            pool.dma_start(gb[:, :], io["g_post_mix"].partition_broadcast(P).rearrange("p o d -> p (o d)")).then_inc(gb_load, 16)
            pool.wait_ge(x_ready, 4)
            pool.dma_start(y_dram[NE * BLK:ROWS, :].rearrange("(s j) (q c) -> s (j q) c", s=BLK, c=256),
                           cmask[0:BLK, 0:256].unsqueeze(1).broadcast_to([BLK, 4 * MAXJOBS, 256])).then_inc(y_zero, 16)
            pool.dma_start(gb[:, :], io["g_post_mlp"].partition_broadcast(P).rearrange("p o d -> p (o d)")).then_inc(gb_load, 16)
            pool.wait_ge(x_ready, 8)
            then(pool.memset(yT[0:MROWS, :, :], 0.0))
            then(pool.memset(one_row, 1.0))
            for dr in range(2):
                then(pool.affine_select(out=selr[:, 4 * dr:4 * dr + 4, :], in_=selr[:, 4 * dr:4 * dr + 4, :],
                                        compare_op=ALU.not_equal, fill=1.0, base=-32 * dr,
                                        pattern=[[-1, 4], [0, P]], channel_multiplier=1))
            pool.memset(GL[:, :, :, :], 0.0).then_inc(const_ready, 1)
            pool.wait_ge(bline_ready, 1)
            pool.dma_start(l_dram, bline.unsqueeze(1).broadcast_to([8, P, 512])).then_inc(bline_store, 16)
            pool.wait_ge(bline_store, 16)
            skew = bass.AP(tensor=l_dram.tensor, offset=P - 1, ap=[[511, P], [P * 512, 8], [1, 3 * P]])
            pool.dma_start(bias, skew).then_inc(bias_load, 16)
            pool.wait_ge(hsum_done, 8)
            pool.dma_start(gb[:, :], io["norm2_g_2"].partition_broadcast(P).rearrange("p o d -> p (o d)")).then_inc(gb_load, 16)
            for dst, name in ((wr[:, :, 0:NG], "w_router_group_2"), (wr[:, :, NG:NG + NE], "w_router_expert_2")):
                pool.dma_start(dst, io[name][0].rearrange("(k p) e -> p k e", p=P), allow_slow_non_contiguous=True
                               ).then_inc(wr_load, 16)
            pool.wait_ge(u_done, 8)
            then(pool.memset(allone, 1.0))
            then(pool.memset(ltri, 0.0))
            pool.affine_select(out=ltri, in_=ltri, compare_op=ALU.is_ge, fill=1.0,
                               base=0, pattern=[[-1, P]], channel_multiplier=1).then_inc(masks_ready, 1)
            pool.wait_ge(y_zero, 16)
            pool.wait_ge(ids_ready, 1)
            for s in range(2):
                pool.wait_ge(h_store[s], 16 * (NT // 2))

            def fetch(e, s):
                pool.tensor_copy(idcol[:, s:s + 1], idsT[:, bass.ds(e, 1)]).then_inc(idcol_ready, 1)
                pool.wait_ge(idcol_ready, e + 1)
                pool.sem_inc(fetches, 1)
                pool.indirect_dma_start(out=xs[0:BLK, s, :], out_offset=None, in_=h_dram,
                                        in_offset=bass.IndirectOffsetOnAxis(ap=idcol[:, s:s + 1], axis=0)).then_inc(gather[s], 16)

            for e in range(2):
                fetch(e, e)
            with pool.Fori(0, NE // 2 - 1) as it:
                for s in range(2):
                    pool.wait_ge(xt_done, it * 2 + (s + 1))
                    fetch(it * 2 + (2 + s), s)
            pool.wait_ge(xt_done, NE)
            n = pool.value_load(njobs[0:1, 0:1], min_val=0, max_val=MAXJOBS)
            with pool.If(n > 0):
                with pool.Fori(0, n) as j:
                    pool.tensor_copy(idcol[:, 2:3], idsT[:, bass.ds(j + NE, 1)]).then_inc(ov["id"], 1)
                    pool.wait_ge(ov["id"], j + 1)
                    pool.sem_inc(fetches, 1)
                    pool.indirect_dma_start(out=xs[0:BLK, 0, :], out_offset=None, in_=h_dram,
                                            in_offset=bass.IndirectOffsetOnAxis(ap=idcol[:, 2:3], axis=0)).then_inc(ov["gather"], 16)
                    pool.wait_ge(ov["store"], j * 16 + 16)
            for s in range(2):
                pool.wait_ge(y_store[s], 16 * (NE // 2))
            for c in range(2):
                for i in range(NT):
                    pool.indirect_dma_start(out=yg[c][:, i, :], out_offset=None, in_=y_dram,
                                            in_offset=bass.IndirectOffsetOnAxis(ap=ipos[:, c, i:i + 1], axis=0),
                                            bounds_check=ROWS - 1).then_inc(y_gather[c][i], 16)

        @block.tensor
        def _(pe):
            free_when = {}

            def take(*banks):
                for b in banks:
                    if b in free_when:
                        pe.wait_ge(*free_when.pop(b))

            pe.wait_ge(const_ready, 1)
            turns = [0]

            def turn(n, tiles=range(NT)):
                for i in tiles:
                    src = (mix if n in (T_MIX, T_BR) else None)
                    if n in NORM:
                        pe.wait_ge(turn_src, 4 * NORM[n] + i + 1)
                    elif n == T_MIX:
                        pe.wait_ge(o_evac, 2 * i + 2)
                    else:
                        pe.wait_ge(o_evac, 2 * NT + i + 1)
                        pe.wait_ge(mnorm_done, i + 1)
                    for half in range(2):
                        b = (2 * i + half) % 4
                        take(b)
                        for k in range(4):
                            f = (4 * half + k) * P
                            t = src[:, i, f:f + P] if src is not None else stage[:, i % 2, f:f + P]
                            ins = pe.transpose(ps[:, b, k * P:(k + 1) * P], t, ident[:, :])
                        ins.then_inc(turn_done, 1)
                        turns[0] += 1
                        free_when[b] = (turn_evac, turns[0])

            chunk_seen = [-1]

            def use_chunk(c):
                if c != chunk_seen[0]:
                    pe.wait_ge(ring_load[c % 2], 16 * (c // 2 + 1))
                    chunk_seen[0] = c

            def group(bank, wait, value):
                take(bank)
                free_when[bank] = (wait, value)

            pe.wait_ge(gain_load, 16 * len(VECS))
            pe.transpose(ps[:, 7, 0:N_VECS], vec_rows, ident[0:N_VECS, 0:N_VECS]).then_inc(vecs_done, 1)
            free_when[7] = (vecs_taken, 1)
            turn(T_PRE)
            pe.wait_ge(turn_evac, 8)
            ropes = vals = 0
            for g, (kind, c, j, _) in enumerate(G1):
                bank = 4 + g % 4
                use_chunk(c)
                if kind in ("rope", "ki"):
                    ropes += 1
                    n = P if kind == "rope" else HD
                    group(bank, rope_done, ropes)
                    wv = ring_view(c, KT, 512 if kind == "rope" else 72)
                    for k in range(KT):
                        ins = pe.matmul(ps[0:n, bank, :], wv[:, k, j * P:j * P + n], hT[:, k, :],
                                        start=(k == 0), stop=(k == KT - 1))
                elif kind == "val":
                    vals += 1
                    group(bank, val_done, vals)
                    wv = ring_view(c, KT, 512)
                    for k in range(KT):
                        ins = pe.matmul(ps[:, bank, :], hT[:, k, j * P:(j + 1) * P], wv[:, k, :],
                                        start=(k == 0), stop=(k == KT - 1))
                else:
                    group(bank, wi_done, 1)
                    wv = ring_view(c, KT, 72)
                    for i in range(NT):
                        for k in range(KT):
                            ins = pe.matmul(ps[:, bank, 8 * i:8 * i + 8], hT[:, k, i * P:(i + 1) * P],
                                            wv[:, k, HD:72], start=(k == 0), stop=(k == KT - 1))
                ins.then_inc(proj_done, 1)
                if idx_part(g):
                    pe.wait_ge(rope_done, 5)
                    pe.wait_ge(ki_dup, 1)
                    for q, (i, h) in idx_part(g):
                        group(q % 4, relu_done, q + 1)
                        r = 64 * (h % 2)
                        pe.matmul(ps[:, q % 4, 0:(i + 1) * P], qiT[r:r + 64, h // 2, i * P:(i + 1) * P],
                                  kiT[r:r + 64, 0:(i + 1) * P], start=True, stop=True).then_inc(idx_done, 1)
            def attention(us):
                us = list(us)

                def scores(un):
                    for c, (q, k, _) in enumerate(un["maps"]):
                        m = un["m"] + c
                        group(m % 4, masked, m + 1)
                        pe.matmul(ps[:, m % 4, 0:un["w"]], q, k, start=True, stop=True).then_inc(score_done, 1)

                def turn_probs(un):
                    u = un["u"]
                    m = un["m"]
                    if un["kind"] == "diff":
                        pe.wait_ge(diff_done, un["d"])
                    else:
                        pe.wait_ge(exp_done, m + 1)
                    group(4 + u % 2, pt_ready, u + 1)
                    for k in range(un["w"] // P):
                        ins = pe.transpose(ps[:, 4 + u % 2, k * P:(k + 1) * P], smb[:, m % 4, k * P:(k + 1) * P],
                                           ident[:, :])
                    ins.then_inc(probT_done, 1)

                def values(un):
                    u = un["u"]
                    pe.wait_ge(pt_ready, u + 1)
                    bank = 6 + un["g"] % 2
                    if un["h"] == 0:
                        group(bank, o_evac, un["g"] + 1)
                    n = un["w"] // P
                    for k in range(n):
                        ins = pe.matmul(ps[:, bank, un["oc"][0]:un["oc"][1]], ptb[:, u % 2, k * P:(k + 1) * P],
                                        un["v"][:, un["k0"] + k, un["vc"][0]:un["vc"][1]],
                                        start=(k == 0), stop=(k == n - 1))
                    ins.then_inc(pv_done, 1)

                for a in range(len(us) + 3):
                    if a < len(us):
                        scores(units[us[a]])
                    if 0 <= a - 2 < len(us):
                        turn_probs(units[us[a - 2]])
                    if 0 <= a - 3:
                        values(units[us[a - 3]])

            pe.wait_ge(rope_done, 21)
            pe.wait_ge(val_done, 8)
            attention(ALL1)
            turn(T_MIX)
            ydone = [0]

            def token_out(c0, nchunk, lhs, when, n):
                for half in range(2):
                    for q in range(nchunk):
                        c = c0 + half * nchunk + q
                        use_chunk(c)
                        for i in range(NT):
                            bank = 2 * i + half
                            if q == 0:
                                take(bank)
                            for k in range(8):
                                ins = pe.matmul(ps[:, bank, :], lhs(8 * q + k, i), ring_view(c, KT, 512)[:, k, :],
                                                start=(q == 0 and k == 0), stop=(q == nchunk - 1 and k == 7))
                            if q == nchunk - 1:
                                ydone[0] += 1
                                ins.then_inc(y_done, 1)
                                free_when[bank] = when(i, half)
                                if half == 1 and i >= 2:
                                    turn(n, [i - 2])
                            elif i == NT - 1:
                                ins.then_inc(down_used, 1)
                turn(n, [2])
                if n != T_N2:
                    turn(n, [3])

            pe.wait_ge(turn_evac, 16)
            token_out(C_WO, 1, lambda k, i: hT[:, k, i * P:(i + 1) * P], lambda i, half: (x_ready, i + 1), T_MLP)
            pe.wait_ge(turn_evac, 24)
            take(4, 5, 6, 7)
            with pe.Fori(0, 4) as it:
                for s in range(2):
                    pe.wait_ge(ring_load[s], it * 16 + 16 * ((C_UP + s) // 2 + 1))
                    for j in range(4):
                        f = 4 * s + j
                        pe.wait_ge(up_free, it * 8 + (f + 1))
                        for k in range(KT):
                            ins = pe.matmul(ps[:, 4 + f % 4, :], ring_view(s, KT, 512)[:, k, j * P:(j + 1) * P],
                                            hT[:, k, :], start=(k == 0), stop=(k == KT - 1))
                        ins.then_inc(up_done, 1)
            pe.wait_ge(up_free, FT + 4)
            token_out(C_DOWN, 4, lambda k, i: uT[:, k, i * P:(i + 1) * P], lambda i, half: (x_ready, 4 + i + 1), T_N1)
            pe.wait_ge(turn_evac, 32)
            pe.wait_ge(onehot_load, 32)
            take(0)
            pe.matmul(ps[0:8, 0, :], btab[:, :], onehot, start=True, stop=True).then_inc(btab_done, 1)
            free_when[0] = (bline_ready, 1)
            count = dict(conv=0, vm=0, qn=0, om=0)
            pending = []

            def norm_sums():
                q, = pending
                pending.clear()
                pe.wait_ge(sq_done, q)
                b = q % 4
                group(b, hstd_done, q)
                pe.matmul(ps[:, b, :], ones[:, :], stage[:, 0, (q % 2) * 512:(q % 2) * 512 + 512],
                          start=True, stop=True).then_inc(ssb_done, 1)

            def gate_rows_out():
                pe.wait_ge(gate_rows, 1)
                for q in range(2):
                    take(q)
                    for i in range(NT):
                        ins = pe.transpose(ps[0:MROWS, q, i * P:(i + 1) * P], GL[:, q, i, :], ident[:, :])
                    ins.then_inc(grow_done, 1)
                    free_when[q] = (grow_evac, q + 1)

            def gate_columns():
                pe.wait_ge(scan_done, 1)
                take(2)
                for q in range(2):
                    for i in range(NT):
                        n = q * NT + i
                        ins = pe.transpose(ps[:, 2, n * MROWS:(n + 1) * MROWS], rows[0:MROWS, q, i * P:(i + 1) * P],
                                           ident[0:MROWS, 0:MROWS])
                ins.then_inc(gcol_done, 1)

            for g, (kind, c, j) in enumerate(G2):
                g += len(G1)
                bank = 4 + g % 4
                use_chunk(c)
                if kind == "gates":
                    pe.wait_ge(gates_load, 16)
                    group(bank, gates_raw, 1)
                    for i in range(NT):
                        for k in range(KT):
                            ins = pe.matmul(ps[:, bank, 16 * i:16 * i + 16], hT[:, k, i * P:(i + 1) * P],
                                            gates_view(c)[:, k, :], start=(k == 0), stop=(k == KT - 1))
                elif kind in ("conv", "qnorm", "knorm", "om"):
                    if kind == "conv":
                        count["conv"] += 1
                        group(bank, conv_in, count["conv"])
                    elif kind == "om":
                        count["om"] += 1
                        group(bank, sig_done, count["om"])
                    else:
                        count["qn"] += 1
                        group(bank, qkn_done, count["qn"])
                    wv = ring_view(c, KT, 256 if kind == "knorm" else 512)
                    for k in range(KT):
                        ins = pe.matmul(ps[:, bank, :], wv[:, k, j * P:(j + 1) * P], hT[:, k, :],
                                        start=(k == 0), stop=(k == KT - 1))
                elif kind == "vm":
                    count["vm"] += 1
                    group(bank, vext_done, count["vm"])
                    for k in range(KT):
                        ins = pe.matmul(ps[:, bank, :], hT[:, k, j * P:(j + 1) * P], ring_view(c, KT, 512)[:, k, :],
                                        start=(k == 0), stop=(k == KT - 1))
                else:
                    group(bank, va2_done, 1)
                    for i in range(NT):
                        for k in range(KT):
                            ins = pe.matmul(ps[:, bank, P * i:P * i + P], hT[:, k, i * P:(i + 1) * P],
                                            ring_view(c, KT, 256)[:, k, P:256], start=(k == 0), stop=(k == KT - 1))
                ins.then_inc(proj_done, 1)
                if pending:
                    norm_sums()
                if kind in ("qnorm", "knorm"):
                    pending.append(count["qn"])
                if kind == "om" and j == 0:
                    gate_rows_out()
                if kind == "om" and j == 2:
                    gate_columns()
            pe.wait_ge(kdup_done, 2)
            pe.wait_ge(va2_done, 1)
            pe.wait_ge(qk_ready, 8)
            pe.wait_ge(acol_ready, 1)
            pe.wait_ge(em_ready, 1)
            pe.wait_ge(bias_load, 16)

            def bcast_m(r):
                h, dr = r // 2, r % 2
                group(4 + r % 2, wexp_done, 7 * (r + 1))
                pe.matmul(ps[:, 4 + r % 2, :], selr[:, dr * 4 + h, :], rows[0:MROWS, 3, :],
                          start=True, stop=True).then_inc(mb_done, 1)

            def qk(h):
                for j in range(NT):
                    group(j, sw_done, 4 * (2 * h + 1) + j + 1)
                    pe.matmul(ps[:, j, :], qkT[:, 4 + h, j * P:(j + 1) * P], qkT[:, h, :],
                                    start=True, stop=True).then_inc(qk_done, 1)

            def num(r):
                h, dr = r // 2, r % 2
                pe.wait_ge(sw_done, 4 * (r + 1))
                group(6, hsum_done, r + 1)
                group(7, hsum_done, r + 1)
                for i in range(NT):
                    js = range(0, i + 1) if dr == 0 else range(i, NT)
                    for j in js:
                        ins = pe.matmul(ps[:, 6 + i // 2, (i % 2) * 129:(i % 2) * 129 + 129],
                                        E[:, r % 2, j, i * P:(i + 1) * P], vext[:, j, h, :],
                                        start=(j == js[0]), stop=(j == js[-1]))
                ins.then_inc(num_done, 1)

            pe.wait_ge(vext_done, 4)
            pe.wait_ge(vone_done, 1)
            attention(ALL2)
            bcast_m(0)
            qk(0)
            bcast_m(1)
            for r in range(8):
                if r + 2 < 8:
                    bcast_m(r + 2)
                if r % 2 and r < 7:
                    qk(r // 2 + 1)
                num(r)
            def merge_gates(half):
                for br_ in range(2):
                    c = C_MERGE + 3 * half + br_
                    use_chunk(c)
                    for j in range(4):
                        gs = 8 * half + 4 * br_ + j
                        group(4 + gs % 4, gate_sig, gs + 1)
                        for k in range(KT):
                            ins = pe.matmul(ps[:, 4 + gs % 4, :], ring_view(c, KT, 512)[:, k, j * P:(j + 1) * P],
                                            hT[:, k, :], start=(k == 0), stop=(k == KT - 1))
                        ins.then_inc(proj_done, 1)

            bo = 0
            for half in range(2):
                merge_gates(half)
                if half == 0:
                    turn(T_BR)
                c = C_MERGE + 3 * half + 2
                pe.wait_ge(turn_evac, 40)
                use_chunk(c)
                pe.wait_ge(branch_load, 16 * (half + 1))
                for j in range(4):
                    for br_ in range(2):
                        bank = (2 * bo + br_) % 4
                        group(bank, u_done, bo + 1)
                        for k in range(4):
                            ins = pe.matmul(ps[:, bank, :],
                                            ring[c % 2][:, br_ * 2048 + k * 512 + j * P:br_ * 2048 + k * 512 + (j + 1) * P],
                                            yT[:, 4 * br_ + k, :], start=(k == 0), stop=(k == 3))
                    bo += 1
                    ins.then_inc(y_done, 1)
                ydone[0] += 4
            pe.wait_ge(u_done, 8)
            token_out(C_WO2, 1, lambda k, i: merged[:, k, i * P:(i + 1) * P],
                      lambda i, half: (x_ready, 8 + 4 * half + i + 1), T_N2)
            pe.wait_ge(wr_load, 32)
            take(4, 5, 6, 7)
            for i in range(NT):
                if i == 2:
                    turn(T_N2, [3])
                pe.wait_ge(turn_evac, 40 + 2 * (i + 1))
                for k in range(KT):
                    ins = pe.matmul(ps[:, 4, i * (NG + NE):(i + 1) * (NG + NE)], hT[:, k, i * P:(i + 1) * P],
                                    wr[:, k, :], start=(k == 0), stop=(k == KT - 1))
            ins.then_inc(logits_done, 1)
            pe.wait_ge(masks_ready, 1)
            pe.wait_ge(sel_ready, 1)
            pe.matmul(ps[:, 5, 0:NT * NE], ltri, both_rows[:, 0:NT * NE], start=True, stop=False)
            for d in range(1, NT):
                pe.matmul(ps[:, 5, d * NE:NT * NE], allone, both_rows[:, 0:(NT - d) * NE], start=False, stop=(d == NT - 1))
            for j in range(NT):
                ins = pe.matmul(ps[:, 7, 0:NE], allone, msel[:, 2, j, :], start=(j == 0), stop=(j == NT - 1))
            ins.then_inc(rank_done, 1)
            pe.wait_ge(slots_ready, 1)
            for n in range(2 * NT):
                ins = pe.matmul(ps[0:BLK, 6, 0:BLOCKS], place_hot[:, n, :], block_tok[:, n, :],
                                start=(n == 0), stop=(n == 2 * NT - 1))
            ins.then_inc(idT_done, 1)
            pe.wait_ge(ids_ready, 1)
            take(0, 1, 2, 3)

            def turn_tokens(src, ready_sem):
                for k in range(KT):
                    ins = pe.transpose(ps[:, k // 4, (k % 4) * BLK:(k % 4 + 1) * BLK],
                                       src[:, k * P:(k + 1) * P], ident[0:BLK, 0:BLK])
                ins.then_inc(ready_sem, 1)

            wviews = [[expert_w[s][j].rearrange("p (k n) -> p k n", k=k) for j, k in enumerate((8, 8, 4))] for s in range(2)]

            def products(s, part, bank):
                for j in range(4):
                    for k in range(KT):
                        ins = pe.matmul(ps[:, bank, j * BLK:(j + 1) * BLK], wviews[s][part][:, k, j * P:(j + 1) * P],
                                        xsT[:, s, k, :], start=(k == 0), stop=(k == KT - 1))
                return ins

            def down(s, bank):
                for half in range(2):
                    for k in range(4):
                        ins = pe.matmul(ps[0:BLK, bank + half, :], hTe[:, s, k, :],
                                        wviews[s][2][:, k, half * 512:(half + 1) * 512], start=(k == 0), stop=(k == 3))
                return ins

            def expert(e, s, turns_of, first=False, last=False):
                pe.wait_ge(xT_ready, e + 1)
                if not first:
                    pe.wait_ge(hte_ready, e)
                pe.wait_ge(wg_load[s], turns_of * 16 + 16)
                products(s, 0, 2).then_inc(gate_done, 1)
                pe.wait_ge(wu_load[s], turns_of * 16 + 16)
                products(s, 1, 3).then_inc(gu_done, 1)
                if not last:
                    t = 1 - s
                    pe.wait_ge(gather[t], (turns_of + s) * 16 + 16)
                    turn_tokens(xs[0:BLK, t, :], xt_done)
                pe.wait_ge(hte_ready, e + 1)
                pe.wait_ge(wd_load[s], turns_of * 16 + 16)
                down(s, 4 + 2 * s).then_inc(down_done, 1)

            pe.wait_ge(gather[0], 16)
            turn_tokens(xs[0:BLK, 0, :], xt_done)
            for e in range(2):
                expert(e, e, 0, first=(e == 0))
            with pe.Fori(1, NE // 2 - 1) as it:
                for s in range(2):
                    pe.wait_ge(ys_ready, it * 2 + (s - 1))
                    expert(it * 2 + s, s, it)
            for s in range(2):
                pe.wait_ge(ys_ready, NE - 2 + s - 1)
                expert(NE - 2 + s, s, NE // 2 - 1, last=(s == 1))
            pe.wait_ge(job_ready, 1)
            pe.wait_ge(ys_ready, NE)
            n = pe.value_load(njobs[0:1, 0:1], min_val=0, max_val=MAXJOBS)
            pe.sem_inc(ov["free"], 1)
            with pe.If(n > 0):
                with pe.Fori(0, n) as j:
                    pe.wait_ge(ov["gather"], j * 16 + 16)
                    turn_tokens(xs[0:BLK, 0, :], ov["xt"])
                    pe.wait_ge(ov["xT"], j + 1)
                    pe.wait_ge(ov["wg"], j * 16 + 16)
                    products(0, 0, 2)
                    pe.wait_ge(ov["wu"], j * 16 + 16)
                    products(0, 1, 3).then_inc(ov["gu"], 1)
                    pe.wait_ge(ov["hte"], j + 1)
                    pe.wait_ge(ov["wd"], j * 16 + 16)
                    down(0, 4).then_inc(ov["down"], 1)
                    pe.wait_ge(ov["ys"], j + 1)
                    pe.sem_inc(ov["free"], 1)

        @block.scalar
        def _(act):
            steps = [0]

            def then(ins):
                steps[0] += 1
                ins.then_inc(ac, 1)
                act.wait_ge(ac, steps[0])

            def sumsq(i, src, out_col, done, n_done):
                act.activation(ptb[:, :, :], src, ACT.Square, accum_out=out_col).then_inc(done, 1)
                act.wait_ge(done, n_done)

            def norm(n, i):
                q = 4 * NORM[n] + i
                if n == T_PRE:
                    act.wait_ge(x_load[i], 16)
                else:
                    act.wait_ge(x_ready, {T_MLP: 0, T_N1: 4, T_N2: 12}[n] + i + 1)
                sumsq(i, x[:, i, :].rearrange("p (a b) -> p a b", a=2), ss[:, q:q + 1], sumsq_done, q + 1)
                act.activation(std[:, q:q + 1], ss[:, q:q + 1], ACT.Sqrt, bias=epsc[:, 0:1], scale=1.0 / D
                               ).then_inc(std_done, 1)

            def y_norm(e, i):
                q = 4 * e + i
                act.wait_ge(y_done, 8 * e + 4 + i + 1)
                sumsq(i, ps[:, 2 * i:2 * i + 2, :], ssy[:, q:q + 1], ysumsq, q + 1)
                act.activation(stdy[:, q:q + 1], ssy[:, q:q + 1], ACT.Sqrt, bias=epsc[:, 0:1], scale=1.0 / D
                               ).then_inc(ystd, 1)

            def y_norm_then(e, n):
                for a in range(NT + 1):
                    if a < NT:
                        y_norm(e, a)
                    if a >= 1:
                        norm(n, a - 1)

            act.wait_ge(const_ready, 1)
            act.wait_ge(dv, 1)
            for i in range(NT):
                norm(T_PRE, i)
            act.wait_ge(lam_dot, 1)
            act.activation(lamv[:, 2:4], lamv[:, 0:2], ACT.Exp).then_inc(lam_exp, 1)
            swaps = 0
            for g, (kind, _, _, dst) in enumerate(G1):
                bank = 4 + g % 4
                if kind in ("rope", "ki"):
                    act.wait_ge(proj_done, g + 1)
                    if swaps >= 2:
                        act.wait_ge(rope_done, swaps - 1)
                    for r in range(4 if kind == "rope" else 2):
                        ins = act.activation(ptb[32 * r:32 * r + 32, swaps % 2, :],
                                             ps[32 * (r ^ 1):32 * (r ^ 1) + 32, bank, :], ACT.Copy)
                    ins.then_inc(swap_done, 1)
                    swaps += 1
                    if kind == "ki":
                        act.wait_ge(rope_done, swaps)
                        act.activation(kiT[64:128, :], kiT[0:64, :], ACT.Copy).then_inc(ki_dup, 1)
                elif kind == "val":
                    act.wait_ge(proj_done, g + 1)
                    act.activation(dst, ps[:, bank, :], ACT.Copy).then_inc(val_done, 1)
                if idx_part(g):
                    for q, (i, h) in idx_part(g):
                        act.wait_ge(idx_done, q + 1)
                        if q >= 2:
                            act.wait_ge(comb_done, q - 1)
                        act.activation(rbuf[:, q % 2, 0:(i + 1) * P], ps[:, q % 4, 0:(i + 1) * P], ACT.Relu
                                       ).then_inc(relu_done, 1)
            def attention(us):
                us = list(us)

                def exps(un):
                    for c in range(len(un["maps"])):
                        m = un["m"] + c
                        act.wait_ge(negmax, m + 1)
                        if un["kind"] == "window":
                            act.activation(es[:, m - M1 + 0:m - M1 + 1], sink[:, un["h"]:un["h"] + 1], ACT.Exp,
                                           bias=nm[:, m:m + 1])
                        row = smb[:, m % 4, 0:un["w"]]
                        act.activation(row, row, ACT.Exp, bias=nm[:, m:m + 1], scale=un["scale"],
                                       accum_out=den[:, un["dc"] + c:un["dc"] + c + 1]).then_inc(exp_done, 1)

                def take_turned(un):
                    u = un["u"]
                    act.wait_ge(probT_done, u + 1)
                    if u >= 2:
                        act.wait_ge(pv_done, u - 1)
                    act.activation(ptb[:, u % 2, 0:un["w"]], ps[:, 4 + u % 2, 0:un["w"]], ACT.Copy).then_inc(pt_ready, 1)

                for a in range(len(us) + 6):
                    if a < len(us):
                        exps(units[us[a]])
                    if 0 <= a - 2 < len(us):
                        take_turned(units[us[a - 2]])
                    for lag, part in ((4, 0), (5, 1)):
                        if 0 <= a - lag < len(us):
                            un = units[us[a - lag]]
                            if not (un["kind"] == "diff" and un["last"]):
                                continue
                            i = un["tile"]
                            if part == 0:
                                act.wait_ge(pv_done, un["u"] + 1)
                                if i:
                                    act.wait_ge(o_ss, i)
                                act.activation(stage[:, 0, 0:512], ps[:, 6 + un["g"] % 2, :], ACT.Square
                                               ).then_inc(o_sq, 1)
                            else:
                                act.wait_ge(o_ss, i + 1)
                                act.activation(hstd[:, 4 * i:4 * i + 4], hss[:, 4 * i:4 * i + 4], ACT.Sqrt,
                                               bias=epsc[:, 0:1], scale=1.0 / P).then_inc(o_std, 1)

            attention(ALL1)
            y_norm_then(0, T_MLP)
            with act.Fori(0, 4) as it:
                for f in range(8):
                    act.wait_ge(up_done, it * 8 + (f + 1))
                    act.activation(smb[:, f % 4, :], ps[:, 4 + f % 4, :], ACT.Relu).then_inc(up_relu, 1)
            act.wait_ge(up_free, FT + 4)
            act.dma_start(onehot, io["bucket_onehot"]).then_inc(onehot_load, 16)
            act.dma_start(wmask, io["window_mask"]).then_inc(onehot_load, 16)
            y_norm_then(1, T_N1)
            convs = vms = qn = oms = 0

            def silu(c):
                act.wait_ge(conv_done, c + 1)
                act.activation(qkT[:, c, :], qkT[:, c, :], ACT.Silu, bias=convb[:, c:c + 1]).then_inc(qk_ready, 1)

            def head_std(q):
                act.wait_ge(ssb_done, q)
                if q >= 3:
                    act.wait_ge(qkn_done, q - 2)
                act.activation(stage[:, 1, (q % 2) * 512:(q % 2) * 512 + 512], ps[:, q % 4, :], ACT.Sqrt,
                               bias=epsc[:, 0:1], scale=1.0 / HD).then_inc(hstd_done, 1)

            for g, (kind, _, c) in enumerate(G2):
                g += len(G1)
                bank = 4 + g % 4
                src = ps[:, bank, :]
                if kind == "gates":
                    act.wait_ge(gates_raw, 1)
                    fv = G[:, :, :].rearrange("p i (d k h) -> p k i d h", d=2, k=2)[:, 1]
                    lv = [lfw[:, q, :, :].rearrange("p i (d h) -> p i d h", d=2) for q in range(3)]
                    then(act.activation(lv[0], fv, ACT.Abs))
                    then(act.activation(lv[1], lv[0], ACT.Exp, scale=-1.0))
                    act.activation(lv[2], lv[1], ACT.Ln, bias=1.0).then_inc(gate_abs, 1)
                    continue
                act.wait_ge(proj_done, g + 1)
                if kind == "conv":
                    act.activation(convin[:, convs, 2:514], src, ACT.Copy).then_inc(conv_in, 1)
                    convs += 1
                    if convs >= 2:
                        silu(convs - 2)
                elif kind == "vm":
                    act.activation(vext[:, c, :, 0:DM], src.rearrange("p (h e) -> p h e", h=4), ACT.Copy
                                   ).then_inc(vext_done, 1)
                    if vms == 0:
                        silu(7)
                    vms += 1
                elif kind in ("qnorm", "knorm"):
                    qn += 1
                    if qn >= 3:
                        act.wait_ge(ssb_done, qn - 2)
                    act.activation(stage[:, 0, (qn % 2) * 512:(qn % 2) * 512 + 512], src, ACT.Square).then_inc(sq_done, 1)
                    if qn >= 2:
                        head_std(qn - 1)
                elif kind == "va2":
                    act.activation(va2[:, :, :].rearrange("p i c -> p (i c)"), src, ACT.Copy).then_inc(va2_done, 1)
                    head_std(5)
                    act.wait_ge(qkn_done, 5)
                    act.activation(kdup[64:128, 0, :], kdup[0:64, 0, :], ACT.Copy).then_inc(kdup_done, 1)
                    act.activation(kdup[0:64, 1, :], kdup[64:128, 1, :], ACT.Copy).then_inc(kdup_done, 1)
                else:
                    act.activation(sigT[:, c, :], src, ACT.Sigmoid).then_inc(sig_done, 1)
            act.wait_ge(acol_ready, 1)
            act.activation(colsb[:, 1, :, :], ps[:, 2, NT * MROWS:2 * NT * MROWS].rearrange("p (i r) -> p i r", i=NT),
                           ACT.Exp, scale=-1.0).then_inc(em_ready, 1)
            attention(ALL2)
            act.wait_ge(pv_done, len(units))
            act.wait_ge(acol_ready, 1)
            for r in range(8):
                h, dr = r // 2, r % 2
                act.wait_ge(nmd_done, r + 1)
                if r >= 2:
                    act.wait_ge(num_done, r - 1)
                for j in range(NT):
                    a_col = colsb[:, 0, j, 32 * dr + h:32 * dr + h + 1]
                    act.activation(E[:, r % 2, j, j * P:(j + 1) * P], nmd[:, r % 2, j, :], ACT.Exp, bias=a_col
                                   ).then_inc(wexp_done, 1)
                    lo, hi = ((j + 1) * P, 512) if dr == 0 else (0, j * P)
                    if lo < hi:
                        act.activation(E[:, r % 2, j, lo:hi], ps[:, 4 + r % 2, lo:hi], ACT.Exp, bias=a_col
                                       ).then_inc(wexp_done, 1)
            act.wait_ge(hsum_done, 8)
            for a in range(NT + 1):
                if a < NT:
                    if a >= 2:
                        act.wait_ge(mss_done, a - 1)
                    act.activation(stage[:, a % 2, 0:512], mix[:, a, 512:1024], ACT.Square).then_inc(msq_done, 1)
                if a >= 1:
                    act.wait_ge(mss_done, a)
                    at = 16 + 4 * (a - 1)
                    act.activation(hstd[:, at:at + 4], hss[:, at:at + 4], ACT.Sqrt, bias=epsc[:, 0:1], scale=1.0 / DM
                                   ).then_inc(mstd_done, 1)
            gs = 0
            for half in range(2):
                for br_ in range(2):
                    for j in range(4):
                        bank = 4 + gs % 4
                        gs += 1
                        act.wait_ge(proj_done, len(G1) + len(G2) + gs)
                        if half:
                            act.wait_ge(u_done, j + 1)
                        b_ = 8 * br_ + 4 * half + j
                        act.activation(gates[:, br_, j, :], ps[:, bank, :], ACT.Sigmoid, bias=mergeb[:, b_:b_ + 1]
                                       ).then_inc(gate_sig, 1)
            for a in range(NT + 1):
                if a < NT:
                    norm(T_N2, a)
                if a >= 1:
                    i = a - 1
                    act.wait_ge(turn_src, 4 * NORM[T_N2] + i + 1)
                    act.dma_start(h_dram[i * P:(i + 1) * P, :], stage[:, i % 2, :]).then_inc(h_store[i % 2], 16)
            for n in range(2):
                act.wait_ge(r_exp, n + 1)
                if n == 0:
                    act.activation(r_ge, r_gd, ACT.Exp).then_inc(r_exp_done, 1)
                else:
                    act.activation(r_x2, r_dv, ACT.Exp).then_inc(r_exp_done, 1)
            def expert(e, s, turns_of, first=False):
                act.wait_ge(gate_done, e + 1)
                act.activation(sg[:, s, :, :].rearrange("p k t -> p (k t)"), ps[:, 2, 0:4 * BLK], ACT.Silu
                               ).then_inc(silu_done, 1)
                act.wait_ge(down_done, e + 1)
                if not first:
                    act.wait_ge(y_store[s], turns_of * 16)
                act.activation(ys[0:BLK, s, :].rearrange("p (a b) -> p a b", a=2), ps[0:BLK, 4 + 2 * s:6 + 2 * s, :],
                               ACT.Copy).then_inc(ys_ready, 1)
                act.wait_ge(ys_ready, e + 1)
                act.dma_start(y_dram[bass.ds(e * BLK, BLK), :], ys[0:BLK, s, :]).then_inc(y_store[s], 16)

            for e in range(2):
                expert(e, e, 0, first=True)
            with act.Fori(1, NE // 2) as it:
                for s in range(2):
                    expert(it * 2 + s, s, it)
            act.wait_ge(job_ready, 1)
            for s in range(2):
                act.wait_ge(y_store[s], 16 * (NE // 2))
            n = act.value_load(njobs[0:1, 0:1], min_val=0, max_val=MAXJOBS)
            with act.If(n > 0):
                with act.Fori(0, n) as j:
                    act.wait_ge(ov["gu"], j + 1)
                    act.activation(sg[:, 0, :, :].rearrange("p k t -> p (k t)"), ps[:, 2, 0:4 * BLK], ACT.Silu
                                   ).then_inc(ov["silu"], 1)
                    act.wait_ge(ov["down"], j + 1)
                    act.activation(ys[0:BLK, 0, :].rearrange("p (a b) -> p a b", a=2), ps[0:BLK, 4:6, :],
                                   ACT.Copy).then_inc(ov["ys"], 1)
                    act.wait_ge(ov["ys"], j + 1)
                    act.dma_start(y_dram[bass.ds(j * BLK + NE * BLK, BLK), :], ys[0:BLK, 0, :]).then_inc(ov["store"], 16)
                    act.wait_ge(ov["store"], j * 16 + 16)

        @block.vector
        def _(dve):
            steps = [0]

            def then(ins):
                steps[0] += 1
                ins.then_inc(dv, 1)
                dve.wait_ge(dv, steps[0])

            def bc(col_, n):
                return col_.unsqueeze(len(col_.shape)).broadcast_to(list(col_.shape) + [n])

            turned = [0]

            def take_turned(n, i):
                for half in range(2):
                    g = turned[0]
                    turned[0] += 1
                    dve.wait_ge(turn_done, g + 1)
                    src = ps[:, (2 * i + half) % 4, :].rearrange("p (k t) -> p k t", k=4)
                    dst = (yT if n == T_BR else hT)[:, 4 * half:4 * half + 4, i * P:(i + 1) * P]
                    if n == T_N2 or (n == T_BR and half == 0):
                        dve.tensor_copy(dst, src).then_inc(turn_evac, 1)
                    elif n == T_BR:
                        then(dve.tensor_tensor(dst, src, bc(gcol[:, 4, 4:8], P), ALU.mult))
                        dve.tensor_tensor(dst, dst, sigT[:, :, i * P:(i + 1) * P], ALU.mult).then_inc(turn_evac, 1)
                    else:
                        gi = {T_PRE: 0, T_MIX: 1, T_MLP: 2, T_N1: 3}[n]
                        dve.tensor_tensor(dst, src, bc(gcol[:, gi, 4 * half:4 * half + 4], P), ALU.mult
                                          ).then_inc(turn_evac, 1)

            def norm_stage(n, i):
                q = 4 * NORM[n] + i
                dve.wait_ge(std_done, q + 1)
                then(dve.reciprocal(rstd[:, q:q + 1], std[:, q:q + 1]))
                if i >= 2:
                    dve.wait_ge(turn_done, 8 * n + 2 * (i - 2) + 2)
                    if n == T_N2:
                        dve.wait_ge(h_store[i % 2], 16 * (i // 2))
                if n == T_N2:
                    dve.scalar_tensor_tensor(out=stage[:, i % 2, :], in0=x[:, i, :], scalar=rstd[:, q:q + 1],
                                             in1=gb[:, :], op0=ALU.mult, op1=ALU.mult).then_inc(turn_src, 1)
                else:
                    dve.tensor_scalar(stage[:, i % 2, :], x[:, i, :], rstd[:, q:q + 1], None, ALU.mult
                                      ).then_inc(turn_src, 1)

            def norm(n):
                for a in range(NT + 1):
                    if a < NT:
                        norm_stage(n, a)
                    if a >= 1:
                        take_turned(n, a - 1)

            def add_normed(e, n, i):
                q = 4 * e + i
                dve.wait_ge(ystd, q + 1)
                then(dve.reciprocal(rsty[:, q:q + 1], stdy[:, q:q + 1]))
                if i >= 2:
                    dve.wait_ge(turn_done, 8 * n + 2 * (i - 2) + 2)
                st = stage[:, i % 2, :]
                then(dve.scalar_tensor_tensor(out=st.rearrange("p (a b) -> p a b", a=2), in0=ps[:, 2 * i:2 * i + 2, :],
                                              scalar=rsty[:, q:q + 1], in1=gb[:, :].rearrange("p (a b) -> p a b", a=2),
                                              op0=ALU.mult, op1=ALU.mult))
                dve.tensor_tensor(x[:, i, :], x[:, i, :], st, ALU.add).then_inc(x_ready, 1)

            dve.wait_ge(const_ready, 1)
            then(dve.memset(epsc[:, :], EPS))
            dve.wait_ge(vecs_done, 1)
            for dst, at, n in ((gcol[:, 0, :], 0, 8), (gcol[:, 2, :], 8, 8), (gcol[:, 3, :], 16, 8), (gcol[:, 4, 4:8], 24, 4),
                               (gcol[:, 5, 0:1], 28, 1), (convb[:, :], 29, 8), (mergeb[:, :], 37, 16)):
                dve.tensor_copy(dst, ps[:, 7, at:at + n])
            dve.tensor_copy(convw[:, :, :], ps[:, 7, 53:53 + 8 * CONV].rearrange("p (w k) -> p k w", w=CONV)
                            ).then_inc(vecs_taken, 1)
            dve.wait_ge(vecs_taken, 1)
            norm(T_PRE)
            dve.wait_ge(small_load, 16 * N_SMALL)
            then(dve.tensor_scalar(gcol[:, 1, 4:8], gcol[:, 5, 0:1].broadcast_to([P, 4]), 1.0 - LAM_INIT, None, ALU.mult))
            for n in range(2):
                then(dve.tensor_tensor_reduce(lam_in[:, 2 * n, :], lam_in[:, 2 * n, :], lam_in[:, 2 * n + 1, :],
                                              1.0, 0.0, ALU.mult, ALU.add, lamv[:, n:n + 1]))
            dve.sem_inc(lam_dot, 1)
            dve.wait_ge(lam_exp, 1)
            then(dve.tensor_tensor(lamv[:, 4:5], lamv[:, 3:4], lamv[:, 2:3], ALU.subtract))
            then(dve.tensor_scalar(lamv[:, 5:6], lamv[:, 4:5], -LAM_INIT, None, ALU.add))

            def take_steps():
                for i in range(1, NT):
                    row = idx_s[:, i - 1, 0:(i + 1) * P]
                    for q in range(TOPK // 8):
                        then(dve.max(m8, row))
                        then(dve.match_replace(row, m8, row, TAKEN))
                        if q == TOPK // 8 - 1:
                            then(dve.tensor_scalar(dmask[:, i - 1, 0:(i + 1) * P], row, TAKEN, NEG,
                                                   ALU.not_equal, ALU.mult))
                        yield

            steps_left = take_steps()
            ropes = 0
            for g, (kind, _, _, dst) in enumerate(G1):
                bank = 4 + g % 4
                if kind in ("rope", "ki"):
                    n = P if kind == "rope" else HD
                    d_ = dst if kind == "rope" else kiT[0:HD, :]
                    dve.wait_ge(proj_done, g + 1)
                    sw = ptb[0:n, ropes % 2, :]
                    ropes += 1
                    dve.wait_ge(swap_done, ropes)
                    dve.tensor_tensor(d_, ps[0:n, bank, :], rope[0:n, 0, :], ALU.mult)
                    then(dve.tensor_tensor(sw, sw, rope[0:n, 1, :], ALU.mult))
                    dve.tensor_tensor(d_, d_, sw, ALU.add).then_inc(rope_done, 1)
                elif kind == "wi":
                    dve.wait_ge(proj_done, g + 1)
                    dve.tensor_copy(wi[:, :, :], ps[:, bank, 0:32].rearrange("p (i h) -> p i h", i=NT)).then_inc(wi_done, 1)
                if idx_part(g):
                    dve.wait_ge(wi_done, 1)
                    for q, (i, h) in idx_part(g):
                        w = (i + 1) * P
                        dve.wait_ge(relu_done, q + 1)
                        row = idx_s[:, i - 1, 0:w]
                        if h == 0:
                            dve.tensor_scalar(row, rbuf[:, q % 2, 0:w], wi[:, i, h:h + 1], None, ALU.mult
                                              ).then_inc(comb_done, 1)
                        else:
                            dve.wait_ge(comb_done, q)
                            dve.scalar_tensor_tensor(out=row, in0=rbuf[:, q % 2, 0:w], scalar=wi[:, i, h:h + 1],
                                                     in1=row, op0=ALU.mult, op1=ALU.add).then_inc(comb_done, 1)
                        if h == 7:
                            dve.wait_ge(comb_done, q + 1)
                            then(dve.tensor_scalar(row, row, IDX_SCALE, None, ALU.mult))
                            diag = idx_s[:, i - 1, w - P:w]
                            then(dve.scalar_tensor_tensor(out=diag, in0=cmask[:, 384:512], scalar=LOWEST / NEG,
                                                          in1=diag, op0=ALU.mult, op1=ALU.add))
                if g >= N_IDX_FROM + 3:
                    for _ in range(3 if g >= IDX_END else 2):
                        next(steps_left, None)
            for _ in steps_left:
                pass
            def attention(us):
                us = list(us)

                def scores(un):
                    w = un["w"]
                    for c, (_, _, mask) in enumerate(un["maps"]):
                        m = un["m"] + c
                        dve.wait_ge(score_done, m + 1)
                        if m >= 4:
                            dve.wait_ge(probT_done, map_unit[m - 4] + 1)
                        dve.tensor_tensor_reduce(smb[:, m % 4, 0:w], ps[:, m % 4, 0:w], mask, 1.0, LOWEST,
                                                 ALU.add, ALU.max, mx[:, m:m + 1]).then_inc(masked, 1)
                        dve.wait_ge(masked, m + 1)
                        if un["kind"] == "window":
                            dve.tensor_scalar(nm[:, m:m + 1], mx[:, m:m + 1], sink[:, un["h"]:un["h"] + 1], -1.0,
                                              ALU.max, ALU.mult).then_inc(negmax, 1)
                        else:
                            dve.tensor_scalar(nm[:, m:m + 1], mx[:, m:m + 1], -un["scale"], None, ALU.mult
                                              ).then_inc(negmax, 1)

                def difference(un):
                    m = un["m"]
                    dve.wait_ge(exp_done, m + 2)
                    dc = un["dc"]
                    then(dve.reciprocal(den[:, dc:dc + 2], den[:, dc:dc + 2]))
                    then(dve.tensor_scalar(den[:, dc + 1:dc + 2], den[:, dc + 1:dc + 2], lamv[:, 5:6], None, ALU.mult))
                    a_, b_ = smb[:, m % 4, 0:un["w"]], smb[:, (m + 1) % 4, 0:un["w"]]
                    then(dve.tensor_scalar(a_, a_, den[:, dc:dc + 1], None, ALU.mult))
                    dve.scalar_tensor_tensor(out=a_, in0=b_, scalar=den[:, dc + 1:dc + 2], in1=a_,
                                             op0=ALU.mult, op1=ALU.add).then_inc(diff_done, 1)

                def outputs(un):
                    i, bank = un["tile"], 6 + un["g"] % 2
                    dve.wait_ge(pv_done, un["u"] + 1)
                    m0, d0 = un["m"] - 7, un["dc"] - 7
                    r8 = den[:, d0:d0 + 8]
                    if un["kind"] == "window":
                        then(dve.tensor_tensor(r8, r8, es[:, m0 - M1:m0 - M1 + 8], ALU.add))
                    then(dve.reciprocal(r8, r8))
                    dve.tensor_tensor(mix[:, i, 0:512].rearrange("p (h e) -> p h e", h=8),
                                      ps[:, bank, :].rearrange("p (h e) -> p h e", h=8), bc(r8, HD), ALU.mult
                                      ).then_inc(o_evac, 1)

                def diff_squares(un):
                    i = un["tile"]
                    dve.wait_ge(o_sq, i + 1)
                    dve.tensor_reduce(hss[:, 4 * i:4 * i + 4], stage[:, 0, 0:512].rearrange("p (h e) -> p h e", h=4),
                                      AX.X, ALU.add).then_inc(o_ss, 1)

                def diff_outputs(un):
                    i, bank = un["tile"], 6 + un["g"] % 2
                    dve.wait_ge(o_std, i + 1)
                    then(dve.reciprocal(hrs[:, 4 * i:4 * i + 4], hstd[:, 4 * i:4 * i + 4]))
                    dve.tensor_tensor(mix[:, i, 512:1024].rearrange("p (h e) -> p h e", h=4),
                                      ps[:, bank, :].rearrange("p (h e) -> p h e", h=4),
                                      bc(hrs[:, 4 * i:4 * i + 4], P), ALU.mult).then_inc(o_evac, 1)

                for a in range(len(us) + 7):
                    if a < len(us):
                        scores(units[us[a]])
                    if 0 <= a - 1 < len(us) and units[us[a - 1]]["kind"] == "diff":
                        difference(units[us[a - 1]])
                    for lag, kinds, part in ((4, ("topk", "window"), outputs), (5, ("diff",), diff_squares),
                                             (6, ("diff",), diff_outputs)):
                        if 0 <= a - lag < len(us) and units[us[a - lag]]["last"] and units[us[a - lag]]["kind"] in kinds:
                            part(units[us[a - lag]])

            attention(ALL1)
            for i in range(NT):
                take_turned(T_MIX, i)
            def epilog(e, n):
                dve.wait_ge(gb_load, 16 * (e + 1))
                for a in range(NT + 2):
                    if a < NT:
                        add_normed(e, n, a)
                    if 0 <= a - 1 < NT:
                        norm_stage(n, a - 1)
                    if 0 <= a - 2:
                        take_turned(n, a - 2)

            epilog(0, T_MLP)
            dve.sem_inc(up_free, 4)
            with dve.Fori(0, 4) as it:
                for f in range(8):
                    dve.wait_ge(up_relu, it * 8 + (f + 1))
                    dve.tensor_tensor(uT[:, bass.ds(it * 8 + f, 1), :], smb[:, f % 4:f % 4 + 1, :],
                                      smb[:, f % 4:f % 4 + 1, :], ALU.mult).then_inc(up_free, 1)
            epilog(1, T_N1)
            dve.memset(vext[:, :, :, DM:DM + 1], 1.0).then_inc(vone_done, 1)
            for a in (0, 514):
                dve.memset(convin[:, :, a:a + 2], 0.0)
            then(dve.tensor_scalar(gqk[:, 0:1], gqk[:, 0:1], HD ** -0.5, None, ALU.mult))
            dve.wait_ge(onehot_load, 32)
            dve.wait_ge(btab_done, 1)
            dve.tensor_tensor(bline, ps[0:8, 0, :], wmask, ALU.add).then_inc(bline_ready, 1)
            convs = qn = 0

            def head_norm(q):
                g = [a for a, x_ in enumerate(G2) if x_[0] in ("qnorm", "knorm")][q - 1] + len(G1)
                bank = 4 + g % 4
                dve.wait_ge(hstd_done, q)
                rs = stage[:, 1, (q % 2) * 512:(q % 2) * 512 + 512]
                then(dve.reciprocal(rs, rs))
                if q <= 4:
                    dve.scalar_tensor_tensor(out=qT[:, q - 1, :], in0=ps[:, bank, :], scalar=gqk[:, 0:1], in1=rs,
                                             op0=ALU.mult, op1=ALU.mult).then_inc(qkn_done, 1)
                else:
                    for h in range(2):
                        r = slice(64 * h, 64 * h + 64)
                        ins = dve.scalar_tensor_tensor(out=kdup[r, h, :], in0=ps[r, bank, :], scalar=gqk[r, 1:2],
                                                       in1=rs[r, :], op0=ALU.mult, op1=ALU.mult)
                    ins.then_inc(qkn_done, 1)

            for g, (kind, _, c) in enumerate(G2):
                g += len(G1)
                bank = 4 + g % 4
                if kind == "gates":
                    dve.wait_ge(proj_done, g + 1)
                    gbb = gateb[:, :].unsqueeze(1).broadcast_to([P, NT, 16])
                    dve.tensor_tensor(G[:, :, :], ps[:, bank, 0:64].rearrange("p (i c) -> p i c", i=NT), gbb, ALU.add
                                      ).then_inc(gates_raw, 1)
                    dve.wait_ge(gates_raw, 1)
                    dve.wait_ge(const_ready, 2)
                    gv = G[:, :, :].rearrange("p i (d k h) -> p k i d h", d=2, k=2)
                    lv = [lfw[:, q, :, :].rearrange("p i (d h) -> p i d h", d=2) for q in range(3)]
                    dve.wait_ge(gate_abs, 1)
                    then(dve.tensor_scalar(lv[0], gv[:, 1], 0.0, None, ALU.min))
                    then(dve.tensor_tensor(lfw[:, 0], lfw[:, 0], lfw[:, 2], ALU.subtract))
                    for dr in range(2):
                        dve.tensor_copy(GL[:, 0, :, 32 * dr:32 * dr + 4], gv[:, 0, :, dr, :])
                        ins = dve.tensor_copy(GL[:, 1, :, 32 * dr:32 * dr + 4], lv[0][:, :, dr, :])
                    ins.then_inc(gate_rows, 1)
                elif kind == "conv":
                    dve.wait_ge(conv_in, convs + 1)
                    acc = qkT[:, convs, :]
                    for w in range(CONV):
                        tap = convin[:, convs, w:w + 512]
                        if w == 0:
                            then(dve.tensor_scalar(acc, tap, convw[:, convs, 0:1], None, ALU.mult))
                        else:
                            ins = dve.scalar_tensor_tensor(out=acc, in0=tap, scalar=convw[:, convs, w:w + 1], in1=acc,
                                                           op0=ALU.mult, op1=ALU.add)
                            if w < CONV - 1:
                                then(ins)
                            else:
                                ins.then_inc(conv_done, 1)
                    convs += 1
                elif kind in ("qnorm", "knorm"):
                    qn += 1
                    if qn >= 2:
                        head_norm(qn - 1)
                elif kind == "va2":
                    head_norm(5)
                elif kind == "om" and c == 0:
                    for q in range(2):
                        dve.wait_ge(grow_done, q + 1)
                        dve.tensor_copy(rows[:, q, :], ps[0:MROWS, q, :]).then_inc(grow_evac, 1)
                    dve.wait_ge(grow_evac, 2)
                    order = ((slice(0, 4), slice(None)), (slice(32, 36), slice(None, None, -1)))
                    for pr, fr in order:
                        ins = dve.tensor_tensor_scan(rows[pr, 2, fr], one_row[pr, fr], rows[pr, 1, fr], 0.0, ALU.mult, ALU.add)
                    then(ins)
                    then(dve.tensor_tensor(rows[:, 0, :], rows[:, 0, :], rows[:, 2, :], ALU.subtract))
                    for pr, fr in order:
                        ins = dve.tensor_tensor_scan(rows[pr, 3, fr], zero_row[pr, fr], rows[pr, 0, fr], 0.0, ALU.add, ALU.max)
                    then(ins)
                    then(dve.tensor_tensor(rows[:, 1, :], rows[:, 2, :], rows[:, 3, :], ALU.add))
                    dve.tensor_scalar(rows[:, 3, :], rows[:, 3, :], -1.0, None, ALU.mult).then_inc(scan_done, 1)
            dve.wait_ge(gcol_done, 1)
            dve.tensor_copy(colsb[:, 0, :, :], ps[:, 2, 0:NT * MROWS].rearrange("p (i r) -> p i r", i=NT)
                            ).then_inc(acol_ready, 1)
            dve.wait_ge(bias_load, 16)
            attention(ALL2)
            dve.wait_ge(em_ready, 1)

            def masked_m(r):
                tri = (fmask[:, :] if r % 2 == 0 else cmask[:, 384:512])
                dve.wait_ge(mb_done, r + 1)
                if r >= 2:
                    dve.wait_ge(wexp_done, 7 * (r - 1))
                dve.tensor_tensor(nmd[:, r % 2, :, :], ps[:, 4 + r % 2, :].rearrange("p (j t) -> p j t", j=NT),
                                  tri.unsqueeze(1).broadcast_to([P, NT, P]), ALU.add).then_inc(nmd_done, 1)

            def weigh(r):
                for j in range(NT):
                    dve.wait_ge(qk_done, 4 * (r // 2) + j + 1)
                    lo, hi = (j * P, 512) if r % 2 == 0 else (0, (j + 1) * P)
                    if j == 0:
                        dve.wait_ge(wexp_done, 7 * (r + 1))
                    dve.scalar_tensor_tensor(out=E[:, r % 2, j, lo:hi], in0=ps[:, j, lo:hi], scalar=DM ** -0.5,
                                             in1=E[:, r % 2, j, lo:hi], op0=ALU.mult, op1=ALU.mult).then_inc(sw_done, 1)

            def head_sum(r):
                h, dr = r // 2, r % 2
                dve.wait_ge(num_done, r + 1)
                nd = ps[:, 6:8, 0:258].rearrange("p b (c e) -> p b c e", e=DM + 1)
                d0, d1 = mden[:, 0, :], mden[:, 1, :]
                then(dve.tensor_copy(d0.rearrange("p (b c) -> p b c", b=2), nd[:, :, :, DM]))
                then(dve.scalar_tensor_tensor(out=d1, in0=d0, scalar=-1.0, in1=d0, op0=ALU.mult, op1=ALU.max))
                then(dve.tensor_tensor(d1, d1, colsb[:, 1, :, 32 * dr + h], ALU.max))
                then(dve.reciprocal(d0, d1))
                at = slice(512 + h * DM, 512 + (h + 1) * DM)
                for b_ in range(2):
                    dst = mix[:, 2 * b_:2 * b_ + 2, at]
                    tmp = stage[:, 0, b_ * 256:(b_ + 1) * 256].rearrange("p (c e) -> p c e", c=2)
                    ins = dve.tensor_tensor(dst if dr == 0 else tmp, nd[:, b_, :, 0:DM],
                                            bc(d0[:, 2 * b_:2 * b_ + 2], DM), ALU.mult)
                    if dr == 0:
                        if b_ == 1:
                            ins.then_inc(hsum_done, 1)
                    else:
                        then(ins)
                        ins = dve.tensor_tensor(dst, dst, tmp, ALU.add)
                        if b_ == 1:
                            ins.then_inc(hsum_done, 1)

            masked_m(0)
            for r in range(8):
                if r < 7:
                    masked_m(r + 1)
                weigh(r)
                if r >= 1:
                    head_sum(r - 1)
            head_sum(7)
            for a in range(NT + 1):
                if a < NT:
                    dve.wait_ge(msq_done, a + 1)
                    at = 16 + 4 * a
                    dve.tensor_reduce(hss[:, at:at + 4], stage[:, a % 2, 0:512].rearrange("p (h e) -> p h e", h=4),
                                      AX.X, ALU.add).then_inc(mss_done, 1)
                if a >= 1:
                    i = a - 1
                    at = 16 + 4 * i
                    dve.wait_ge(mstd_done, i + 1)
                    then(dve.reciprocal(hrs[:, at:at + 4], hstd[:, at:at + 4]))
                    mv = mix[:, i, 512:1024].rearrange("p (h e) -> p h e", h=4)
                    dve.tensor_tensor(mv, mv, bc(hrs[:, at:at + 4], DM), ALU.mult).then_inc(mnorm_done, 1)
            dve.wait_ge(sig_done, 4)
            for i in range(NT):
                take_turned(T_BR, i)
            for half in range(2):
                for j in range(4):
                    bo = 4 * half + j
                    dve.wait_ge(y_done, 16 + bo + 1)
                    dve.wait_ge(gate_sig, 8 * half + 4 + j + 1)
                    a_, b_ = merged[:, bo, :], stage[:, 0, (j % 2) * 512:(j % 2) * 512 + 512]
                    dve.tensor_tensor(a_, gates[:, 0, j, :], ps[:, (2 * bo) % 4, :], ALU.mult)
                    then(dve.tensor_tensor(b_, gates[:, 1, j, :], ps[:, (2 * bo + 1) % 4, :], ALU.mult))
                    dve.tensor_tensor(a_, a_, b_, ALU.add).then_inc(u_done, 1)
            def add_half(half, i):
                dve.wait_ge(y_done, 24 + 4 * half + i + 1)
                at = x[:, i, half * 512:(half + 1) * 512]
                dve.tensor_tensor(at, at, ps[:, 2 * i + half, :], ALU.add).then_inc(x_ready, 1)

            for i in range(NT):
                add_half(0, i)
            dve.wait_ge(gb_load, 48)
            for a in range(NT + 2):
                if a < NT:
                    add_half(1, a)
                if 0 <= a - 1 < NT:
                    norm_stage(T_N2, a - 1)
                if 0 <= a - 2:
                    take_turned(T_N2, a - 2)
            dve.tensor_scalar(block_start, iot[:, 0:BLOCKS], float(BLK), None, ALU.mult)
            then(dve.tensor_scalar(r_place, iot[:, 0:8], -64.0, None, ALU.add))
            dve.wait_ge(logits_done, 1)
            nall = NG + NE
            then(dve.tensor_tensor(lg[:, :, :], ps[:, 4, 0:NT * nall].rearrange("p (i c) -> p i c", i=NT),
                                   br[:, :].unsqueeze(1).broadcast_to([P, NT, nall]), ALU.add))
            gl = lg[:, :, 0:NG]
            el = lg[:, :, NG:nall].rearrange("p i (g e) -> p i e g", g=NG)

            def first_best(vals, n, out_max, eq, low, out_hot):
                then(dve.tensor_reduce(out_max, vals, AX.X, ALU.max))
                then(dve.tensor_tensor(eq, vals, bc(out_max, n), ALU.is_equal))
                place = r_place[:, 0:n].unsqueeze(1).broadcast_to([P, NT, n])
                then(dve.tensor_tensor(eq, eq, place, ALU.mult))
                then(dve.tensor_reduce(low, eq, AX.X, ALU.min))
                then(dve.tensor_tensor(out_hot, bc(low, n), place, ALU.is_equal))

            first_best(gl, NG, r_gm, r_eq4, r_low, r_hg)
            dve.tensor_tensor(r_gd, gl, bc(r_gm, NG), ALU.subtract).then_inc(r_exp, 1)
            then(dve.tensor_tensor(r_sel, el, r_hg.unsqueeze(2).broadcast_to([P, NT, EPG, NG]), ALU.mult))
            then(dve.tensor_reduce(r_e, r_sel, AX.X, ALU.add))
            first_best(r_e, EPG, r_v1, r_eq8, r_low, r_h1)
            then(dve.scalar_tensor_tensor(out=r_e2, in0=r_h1, scalar=LOWEST, in1=r_e, op0=ALU.mult, op1=ALU.add))
            first_best(r_e2, EPG, r_v2, r_eq8, r_low, r_h2)
            dve.wait_ge(r_exp_done, 1)
            dve.tensor_tensor(r_dv, r_v2, r_v1, ALU.subtract).then_inc(r_exp, 1)
            for c, hot in enumerate((r_h1, r_h2)):
                ins = dve.tensor_tensor(msel[:, c, :, :].rearrange("p i (g e) -> p i g e", g=NG),
                                        r_hg.unsqueeze(3).broadcast_to([P, NT, NG, EPG]),
                                        hot.unsqueeze(2).broadcast_to([P, NT, NG, EPG]), ALU.mult)
            then(ins)
            dve.tensor_tensor(msel[:, 2, :, :], msel[:, 0, :, :], msel[:, 1, :, :], ALU.add).then_inc(sel_ready, 1)
            dve.wait_ge(r_exp_done, 2)
            then(dve.tensor_reduce(r_gm, r_ge, AX.X, ALU.add))
            then(dve.reciprocal(r_gm, r_gm))
            then(dve.tensor_scalar(r_low, r_x2, 1.0, None, ALU.add))
            then(dve.reciprocal(r_low, r_low))
            then(dve.tensor_tensor(wpos[:, 0, :], r_low, r_gm, ALU.mult))
            then(dve.tensor_tensor(wpos[:, 1, :], wpos[:, 0, :], r_x2, ALU.mult))
            dve.wait_ge(masks_ready, 1)
            dve.wait_ge(rank_done, 1)
            cnt = ps[:, 7, 0:NE]
            then(dve.tensor_tensor(more, bc(cnt, NBLK - 1), block_start[:, 1:NBLK].unsqueeze(1).broadcast_to([P, NE, NBLK - 1]),
                                   ALU.is_gt))
            then(dve.tensor_reduce(r_ov, more, AX.X, ALU.add))
            then(dve.tensor_tensor_scan(r_cum, allone[:, 0:NE], r_ov, 0.0, ALU.mult, ALU.add))
            then(dve.tensor_tensor(r_ov, r_cum, r_ov, ALU.subtract))
            then(dve.tensor_tensor(r_ov, r_ov, iot[:, 0:NE], ALU.subtract))
            then(dve.tensor_scalar(r_ov, r_ov, float(NE - 1), float(BLK), ALU.add, ALU.mult))
            ranks = ps[:, 5, 0:NT * NE].rearrange("p (i e) -> p i e", i=NT)
            over = msel[:, 2, :, :]
            then(dve.tensor_scalar(over, ranks, float(BLK), None, ALU.is_ge))
            then(dve.tensor_tensor(over, over, r_ov.unsqueeze(1).broadcast_to([P, NT, NE]), ALU.mult))
            then(dve.tensor_tensor(r_rank, ranks, block_start[:, 0:NE].unsqueeze(1).broadcast_to([P, NT, NE]), ALU.add))
            then(dve.tensor_tensor(r_rank, r_rank, over, ALU.add))
            for c in range(2):
                then(dve.tensor_tensor(r_row, msel[:, c, :, :], r_rank, ALU.mult))
                then(dve.tensor_reduce(r_rows[:, c, :], r_row, AX.X, ALU.add))
            rows8 = r_rows.rearrange("p c i -> p (c i)")
            all_blocks = [P, 2 * NT, BLOCKS]
            then(dve.tensor_tensor(from_block, bc(rows8, BLOCKS), block_start.unsqueeze(1).broadcast_to(all_blocks), ALU.is_ge))
            then(dve.tensor_reduce(r_blk, from_block, AX.X, ALU.add))
            then(dve.tensor_tensor(block_tok, bc(r_blk, BLOCKS),
                                   iot[:, 1:BLOCKS + 1].unsqueeze(1).broadcast_to(all_blocks), ALU.is_equal))
            for c in range(2):
                at = block_tok[:, NT * c:NT * (c + 1), :]
                dve.tensor_tensor(at, at, bc(tokid[:, :], BLOCKS), ALU.mult)
            then(dve.tensor_scalar(r_blk, r_blk, -1.0, float(-BLK), ALU.add, ALU.mult))
            then(dve.tensor_tensor(r_blk, r_blk, rows8, ALU.add))
            dve.tensor_tensor(place_hot, bc(r_blk, BLK), iot[:, 0:BLK].unsqueeze(1).broadcast_to([P, 2 * NT, BLK]),
                              ALU.is_equal).then_inc(slots_ready, 1)
            dve.wait_ge(idT_done, 1)
            dve.tensor_copy(idsT[:, :], ps[0:BLK, 6, 0:BLOCKS]).then_inc(ids_ready, 1)
            dve.tensor_copy(ipos[:, :, :], r_rows)
            then(dve.tensor_copy(njobs[:, :], r_cum[0:1, NE - 1:NE]))
            then(dve.tensor_tensor(j_le, r_cum[0:1, :].unsqueeze(1).broadcast_to([1, MAXJOBS, NE]),
                                   bc(iot[0:1, 0:MAXJOBS], NE), ALU.is_le))
            then(dve.tensor_reduce(j_ex, j_le, AX.X, ALU.add))
            then(dve.tensor_scalar(j_ex, j_ex, float(NE - 1), None, ALU.min))
            then(dve.tensor_copy(jobs[:, :], j_ex))
            dve.sem_inc(job_ready, 1)
            def turned_tokens(s, wait, value, ready):
                dve.wait_ge(wait, value)
                for half in range(2):
                    ins = dve.tensor_copy(xsT[:, s, 4 * half:4 * half + 4, :],
                                          ps[:, half, 0:4 * BLK].rearrange("p (k t) -> p k t", k=4))
                ins.then_inc(ready, 1)

            def hidden(s, wait, value, ready, products_done):
                dve.wait_ge(wait, value)
                dve.wait_ge(products_done, value)
                dve.tensor_tensor(hTe[:, s, :, :].rearrange("p k t -> p (k t)"), sg[:, s, :, :].rearrange("p k t -> p (k t)"),
                                  ps[:, 3, 0:4 * BLK], ALU.mult).then_inc(ready, 1)

            turned_tokens(0, xt_done, 1, xT_ready)
            with dve.Fori(0, NE // 2 - 1) as it:
                for s in range(2):
                    e = it * 2 + s
                    hidden(s, silu_done, e + 1, hte_ready, gu_done)
                    turned_tokens(1 - s, xt_done, e + 2, xT_ready)
            hidden(0, silu_done, NE - 1, hte_ready, gu_done)
            turned_tokens(1, xt_done, NE, xT_ready)
            hidden(1, silu_done, NE, hte_ready, gu_done)
            n = dve.value_load(njobs[0:1, 0:1], min_val=0, max_val=MAXJOBS)
            with dve.If(n > 0):
                with dve.Fori(0, n) as j:
                    turned_tokens(0, ov["xt"], j + 1, ov["xT"])
                    hidden(0, ov["silu"], j + 1, ov["hte"], ov["gu"])
            for c in range(2):
                for i in range(NT):
                    dve.wait_ge(y_gather[c][i], 16)
                    if c:
                        dve.wait_ge(add_done, i + 1)
                    dve.scalar_tensor_tensor(out=x[:, i, :], in0=yg[c][:, i, :], scalar=wpos[:, c, i:i + 1],
                                             in1=x[:, i, :], op0=ALU.mult, op1=ALU.add).then_inc(add_done, 1)


_INS = ["x", "w_in", "w_out", "w_up", "w_down", "g_pre_mix", "g_post_mix", "g_pre_mlp", "g_post_mlp",
        "g_diff_sub", "lambda_q1", "lambda_k1", "lambda_q2", "lambda_k2", "norm1_g_2", "w_in_2",
        "attn_q_gain_2", "attn_k_gain_2", "attn_sink_2", "rel_bias_table_2", "mlstm_conv_w_2",
        "mlstm_conv_b_2", "mlstm_gate_b_2", "mlstm_out_gain_2", "w_branch_attn_2", "w_branch_mlstm_2",
        "merge_b_2", "w_out_2", "norm2_g_2", "w_router_group_2", "b_router_group_2",
        "w_router_expert_2", "b_router_expert_2", "w_expert_gate_2", "w_expert_up_2", "w_expert_down_2"]


def shape_constants():
    inv = (1.0 / (np.float32(10000.0) ** (np.arange(0, HD, 2, dtype=np.float32) / np.float32(HD)))).astype(np.float32)
    ang = (np.arange(SEQ, dtype=np.float32)[None, :] * inv[:, None]).astype(np.float32)
    cos, sin = np.cos(ang), np.sin(ang)
    rel = np.arange(512) - 255
    n = np.abs(rel)
    nf = np.maximum(n, 1).astype(np.float32)
    large = 8 + (np.log(nf / 8) / np.float32(math.log(128 / 8)) * np.float32(8)).astype(np.int32)
    bucket = np.where(rel > 0, 16, 0) + np.where(n < 8, n, np.minimum(large, 15))
    onehot = (np.arange(32)[:, None] == bucket[None, :]).astype(np.float32)
    window = np.where(np.abs(rel) <= 128, 0.0, NEG).astype(np.float32)
    return {"rope_cos": np.concatenate([cos] * 4).astype(np.float32),
            "rope_sin": np.concatenate([-sin, sin] * 2).astype(np.float32),
            "bucket_onehot": onehot, "window_mask": np.repeat(window[None, :], 8, axis=0)}


def kernel(**inputs):
    import concourse.bacc as _bacc
    from concourse.bass_utils import run_bass_kernel_spmd as _run

    nc = _bacc.Bacc("TRN2", target_bir_lowering=False, num_devices=1)
    arrays, io = {}, {}
    given = {name: np.ascontiguousarray(inputs[name]) for name in _INS}
    for name, a in {**given, **shape_constants()}.items():
        arrays[f"in_{name}"] = a
        io[name] = nc.dram_tensor(f"in_{name}", a.shape, mybir.dt.from_np(a.dtype), kind="ExternalInput").ap()
    out = nc.dram_tensor("out_x", (1, SEQ, D), F32, kind="ExternalOutput").ap()
    build(nc, io, out)
    r = _run(nc, [arrays], core_ids=[0])
    return r.results[0]["out_x"]
```
